# Optimizing a Trainium2 kernel written in Bass

```python
import math
import jax
import jax.numpy as jnp
from jax import lax
import numpy as np

D_MODEL = 1024
BATCH = 1
SEQ = 1024
DEPTH = 1

N_MIXERS = 2
CHUNK = 64
NORM_EPS = 1e-6

ML_HEADS = 4
ML_QK_DIM = D_MODEL // (2 * ML_HEADS)
ML_V_DIM = D_MODEL // ML_HEADS
ML_QK_WIDTH = ML_HEADS * ML_QK_DIM
ML_V_WIDTH = ML_HEADS * ML_V_DIM
ML_PROJ = 2 * ML_QK_WIDTH + 2 * ML_V_WIDTH + 2 * ML_HEADS
ML_GATE_CAP = 15.0

GDN_K_HEADS = 8
GDN_V_HEADS = 16
GDN_HEAD_DIM = 128
GDN_KEY_WIDTH = GDN_K_HEADS * GDN_HEAD_DIM
GDN_VAL_WIDTH = GDN_V_HEADS * GDN_HEAD_DIM
GDN_CONV_DIM = 2 * GDN_KEY_WIDTH + GDN_VAL_WIDTH
GDN_CONV_WIDTH = 4
GDN_PROJ = GDN_CONV_DIM + GDN_VAL_WIDTH + 2 * GDN_V_HEADS

D_FF = ((8 * D_MODEL + 3 * 256 - 1) // (3 * 256)) * 256

N_ML_LAYERS = (DEPTH + N_MIXERS - 1) // N_MIXERS
N_GDN_LAYERS = DEPTH // N_MIXERS

kernel_name = 'hybrid_mlstm_gdn_adaln_block'

def rms_norm(x, eps=NORM_EPS):
    xf = x.astype(jnp.float32)
    y = xf * lax.rsqrt(jnp.mean(xf * xf, axis=-1, keepdims=True) + eps)
    return y.astype(x.dtype)

def l2_normalize(x, eps=NORM_EPS):
    return x * lax.rsqrt(jnp.sum(x * x, axis=-1, keepdims=True) + eps)

def to_chunks(t):
    b, s, h, d = t.shape
    return t.reshape(b, s // CHUNK, CHUNK, h, d).transpose(0, 3, 1, 2, 4)

def from_chunks(t):
    b, h, nc, l, d = t.shape
    return t.transpose(0, 2, 3, 1, 4).reshape(b, nc * l, h, d)

def causal_depthwise_conv(x, w):
    k = w.shape[0]
    return lax.conv_general_dilated(
        x, w[:, None, :], window_strides=(1,), padding=[(k - 1, 0)],
        dimension_numbers=('NWC', 'WIO', 'NWC'), feature_group_count=x.shape[-1])

def mlstm_chunkwise(q, k, v, log_i, log_f):
    L = q.shape[-2]
    idx = jnp.arange(L)
    causal = idx[:, None] >= idx[None, :]
    b = jnp.cumsum(log_f, axis=-1)
    b_last = b[..., -1]
    d_mat = jnp.where(causal, b[..., :, None] - b[..., None, :] + log_i[..., None, :], -jnp.inf)
    m_intra = jnp.max(d_mat, axis=-1)
    g_end = b_last[..., None] - b + log_i
    m_loc = jnp.max(g_end, axis=-1)
    k_w = k * jnp.exp(g_end - m_loc[..., None])[..., None]
    d_c = jnp.einsum('bhclk,bhclv->bhckv', k_w, v)
    d_n = jnp.sum(k_w, axis=-2)

    def step(carry, xs):
        c_st, n_st, m_st = carry
        dc_c, dn_c, mloc_c, bl_c = xs
        m_new = jnp.maximum(bl_c + m_st, mloc_c)
        a_old = jnp.exp(bl_c + m_st - m_new)
        a_new = jnp.exp(mloc_c - m_new)
        c_new = a_old[..., None, None] * c_st + a_new[..., None, None] * dc_c
        n_new = a_old[..., None] * n_st + a_new[..., None] * dn_c
        return (c_new, n_new, m_new), (c_st, n_st, m_st)

    bsz, nh, _, _, dk = q.shape
    dv = v.shape[-1]
    init = (jnp.zeros((bsz, nh, dk, dv), q.dtype), jnp.zeros((bsz, nh, dk), q.dtype),
            jnp.zeros((bsz, nh), q.dtype))
    xs = tuple(jnp.moveaxis(t, 2, 0) for t in (d_c, d_n, m_loc, b_last))
    _, (c_prev, n_prev, m_prev) = lax.scan(step, init, xs)
    c_prev = jnp.moveaxis(c_prev, 0, 2)
    n_prev = jnp.moveaxis(n_prev, 0, 2)
    m_prev = jnp.moveaxis(m_prev, 0, 2)

    m_inter = b + m_prev[..., None]
    m_t = jnp.maximum(m_inter, m_intra)
    s_inter = jnp.exp(m_inter - m_t)
    p = jnp.exp(d_mat - m_t[..., None]) * jnp.einsum('bhcld,bhcsd->bhcls', q, k)
    num = (s_inter[..., None] * jnp.einsum('bhcld,bhcdv->bhclv', q, c_prev)
           + jnp.einsum('bhcls,bhcsv->bhclv', p, v))
    den = s_inter * jnp.einsum('bhcld,bhcd->bhcl', q, n_prev) + jnp.sum(p, axis=-1)
    return num / jnp.maximum(jnp.abs(den), jnp.exp(-m_t))[..., None]

def gated_delta_chunkwise(q, k, v, g, beta):
    L = q.shape[-2]
    dv = v.shape[-1]
    idx = jnp.arange(L)
    causal = idx[:, None] >= idx[None, :]
    strict = idx[:, None] > idx[None, :]
    G = jnp.cumsum(g, axis=-1)
    decay = jnp.exp(jnp.where(causal, G[..., :, None] - G[..., None, :], -jnp.inf))
    k_beta = k * beta[..., None]
    a_mat = jnp.where(strict, jnp.einsum('bhcld,bhcsd->bhcls', k_beta, k) * decay, 0.0)
    t_mat = a_mat + jnp.eye(L, dtype=a_mat.dtype)
    rhs = jnp.concatenate([v * beta[..., None], k_beta * jnp.exp(G)[..., None]], axis=-1)
    sol = lax.linalg.triangular_solve(t_mat, rhs, left_side=True, lower=True, unit_diagonal=True)
    u, w = sol[..., :dv], sol[..., dv:]
    attn = jnp.einsum('bhcld,bhcsd->bhcls', q, k) * decay
    q_dec = q * jnp.exp(G)[..., None]
    g_last = G[..., -1]
    k_dec = k * jnp.exp(g_last[..., None] - G)[..., None]

    def step(state, xs):
        q_c, k_c, u_c, w_c, attn_c, gl_c = xs
        v_new = u_c - jnp.einsum('bhlk,bhkv->bhlv', w_c, state)
        out = (jnp.einsum('bhlk,bhkv->bhlv', q_c, state)
               + jnp.einsum('bhls,bhsv->bhlv', attn_c, v_new))
        state = state * jnp.exp(gl_c)[..., None, None] + jnp.einsum('bhlk,bhlv->bhkv', k_c, v_new)
        return state, out

    bsz, nh, _, _, dk = q.shape
    init = jnp.zeros((bsz, nh, dk, dv), q.dtype)
    xs = tuple(jnp.moveaxis(t, 2, 0) for t in (q_dec, k_dec, u, w, attn, g_last))
    _, out = lax.scan(step, init, xs)
    return jnp.moveaxis(out, 0, 2)

def mlstm_mixer(h, w_in, b_if, norm_w, w_out):
    bsz, seq, _ = h.shape
    f32 = jnp.float32
    proj = h @ w_in
    q, k, v, o, gates = jnp.split(
        proj, [ML_QK_WIDTH, 2 * ML_QK_WIDTH, 2 * ML_QK_WIDTH + ML_V_WIDTH,
               2 * ML_QK_WIDTH + 2 * ML_V_WIDTH], axis=-1)
    q = q.astype(f32).reshape(bsz, seq, ML_HEADS, ML_QK_DIM)
    k = k.astype(f32).reshape(bsz, seq, ML_HEADS, ML_QK_DIM) * (ML_QK_DIM ** -0.5)
    v = v.astype(f32).reshape(bsz, seq, ML_HEADS, ML_V_DIM)
    gates = gates.astype(f32) + b_if.astype(f32)
    gates = ML_GATE_CAP * jnp.tanh(gates / ML_GATE_CAP)
    log_i, f_pre = jnp.split(gates, 2, axis=-1)
    log_f = jax.nn.log_sigmoid(f_pre)
    hc = mlstm_chunkwise(to_chunks(q), to_chunks(k), to_chunks(v),
                         to_chunks(log_i[..., None])[..., 0], to_chunks(log_f[..., None])[..., 0])
    hc = rms_norm(from_chunks(hc)).reshape(bsz, seq, ML_V_WIDTH) * norm_w.astype(f32)
    out = hc * jax.nn.sigmoid(o.astype(f32))
    return out.astype(h.dtype) @ w_out

def gdn_mixer(h, w_in, conv_w, a_log, dt_bias, norm_w, w_out):
    bsz, seq, _ = h.shape
    f32 = jnp.float32
    proj = h @ w_in
    qkv, z, b_raw, a_raw = jnp.split(
        proj, [GDN_CONV_DIM, GDN_CONV_DIM + GDN_VAL_WIDTH,
               GDN_CONV_DIM + GDN_VAL_WIDTH + GDN_V_HEADS], axis=-1)
    qkv = jax.nn.silu(causal_depthwise_conv(qkv, conv_w)).astype(f32)
    q, k, v = jnp.split(qkv, [GDN_KEY_WIDTH, 2 * GDN_KEY_WIDTH], axis=-1)
    rep = GDN_V_HEADS // GDN_K_HEADS
    q = l2_normalize(q.reshape(bsz, seq, GDN_K_HEADS, GDN_HEAD_DIM)) * (GDN_HEAD_DIM ** -0.5)
    k = l2_normalize(k.reshape(bsz, seq, GDN_K_HEADS, GDN_HEAD_DIM))
    q = jnp.repeat(q, rep, axis=2)
    k = jnp.repeat(k, rep, axis=2)
    v = v.reshape(bsz, seq, GDN_V_HEADS, GDN_HEAD_DIM)
    beta = jax.nn.sigmoid(b_raw.astype(f32))
    g = -jnp.exp(a_log.astype(f32)) * jax.nn.softplus(a_raw.astype(f32) + dt_bias.astype(f32))
    o = gated_delta_chunkwise(to_chunks(q), to_chunks(k), to_chunks(v),
                              to_chunks(g[..., None])[..., 0], to_chunks(beta[..., None])[..., 0])
    o = from_chunks(o)
    z = z.astype(f32).reshape(bsz, seq, GDN_V_HEADS, GDN_HEAD_DIM)
    o = rms_norm(o) * norm_w.astype(f32) * jax.nn.silu(z)
    return o.reshape(bsz, seq, GDN_VAL_WIDTH).astype(h.dtype) @ w_out

def swiglu(h, w_gate_up, w_down):
    gate, up = jnp.split(h @ w_gate_up, 2, axis=-1)
    return (jax.nn.silu(gate) * up) @ w_down

def setup_inputs(seed: int = 0) -> dict:
    key = jax.random.key(seed)
    ks = jax.random.split(key, 20)
    f32 = jnp.float32

    def nrm(k, shape, scale):
        return jax.random.normal(k, shape, f32) * scale

    x = nrm(ks[0], (BATCH, SEQ, D_MODEL), 1.0)
    c = nrm(ks[1], (BATCH, D_MODEL), 1.0)
    ada_w = nrm(ks[2], (DEPTH, D_MODEL, 6 * D_MODEL), 0.5 * D_MODEL ** -0.5)
    ada_b = nrm(ks[3], (DEPTH, 6 * D_MODEL), 0.02)
    ml_w_in = nrm(ks[4], (N_ML_LAYERS, D_MODEL, ML_PROJ), D_MODEL ** -0.5)
    i_bias = nrm(ks[5], (N_ML_LAYERS, ML_HEADS), 0.1)
    f_bias = jnp.linspace(3.0, 6.0, ML_HEADS, dtype=f32)[None, :] + nrm(ks[6], (N_ML_LAYERS, ML_HEADS), 0.1)
    ml_b_if = jnp.concatenate([i_bias, f_bias], axis=-1)
    ml_norm_w = 1.0 + nrm(ks[7], (N_ML_LAYERS, ML_V_WIDTH), 0.02)
    ml_w_out = nrm(ks[8], (N_ML_LAYERS, ML_V_WIDTH, D_MODEL), ML_V_WIDTH ** -0.5)
    gdn_w_in = nrm(ks[9], (N_GDN_LAYERS, D_MODEL, GDN_PROJ), D_MODEL ** -0.5)
    gdn_conv_w = nrm(ks[10], (N_GDN_LAYERS, GDN_CONV_WIDTH, GDN_CONV_DIM), GDN_CONV_WIDTH ** -0.5)
    gdn_a_log = jnp.log(jax.random.uniform(ks[11], (N_GDN_LAYERS, GDN_V_HEADS), f32, 1.0, 16.0))
    dt = jnp.exp(jax.random.uniform(ks[12], (N_GDN_LAYERS, GDN_V_HEADS), f32,
                                    math.log(1e-3), math.log(1e-1)))
    gdn_dt_bias = dt + jnp.log(-jnp.expm1(-dt))
    gdn_norm_w = 1.0 + nrm(ks[13], (N_GDN_LAYERS, GDN_HEAD_DIM), 0.02)
    gdn_w_out = nrm(ks[14], (N_GDN_LAYERS, GDN_VAL_WIDTH, D_MODEL), GDN_VAL_WIDTH ** -0.5)
    ffn_w_gate_up = nrm(ks[15], (DEPTH, D_MODEL, 2 * D_FF), D_MODEL ** -0.5)
    ffn_w_down = nrm(ks[16], (DEPTH, D_FF, D_MODEL), D_FF ** -0.5)
    final_norm_w = 1.0 + nrm(ks[17], (D_MODEL,), 0.02)
    return {'x': x, 'c': c, 'ada_w': ada_w, 'ada_b': ada_b,
            'ml_w_in': ml_w_in, 'ml_b_if': ml_b_if, 'ml_norm_w': ml_norm_w, 'ml_w_out': ml_w_out,
            'gdn_w_in': gdn_w_in, 'gdn_conv_w': gdn_conv_w, 'gdn_a_log': gdn_a_log,
            'gdn_dt_bias': gdn_dt_bias, 'gdn_norm_w': gdn_norm_w, 'gdn_w_out': gdn_w_out,
            'ffn_w_gate_up': ffn_w_gate_up, 'ffn_w_down': ffn_w_down, 'final_norm_w': final_norm_w}

def reference(x, c, ada_w, ada_b, ml_w_in, ml_b_if, ml_norm_w, ml_w_out,
              gdn_w_in, gdn_conv_w, gdn_a_log, gdn_dt_bias, gdn_norm_w, gdn_w_out,
              ffn_w_gate_up, ffn_w_down, final_norm_w):
    c_act = jax.nn.silu(c)
    for layer in range(DEPTH):
        mod = c_act @ ada_w[layer] + ada_b[layer]
        sh1, sc1, g1, sh2, sc2, g2 = [m[:, None, :] for m in jnp.split(mod, 6, axis=-1)]
        h = rms_norm(x) * (1.0 + sc1) + sh1
        j = layer // N_MIXERS
        if layer % N_MIXERS == 0:
            y = mlstm_mixer(h, ml_w_in[j], ml_b_if[j], ml_norm_w[j], ml_w_out[j])
        else:
            y = gdn_mixer(h, gdn_w_in[j], gdn_conv_w[j], gdn_a_log[j], gdn_dt_bias[j],
                          gdn_norm_w[j], gdn_w_out[j])
        x = x + g1 * y
        h = rms_norm(x) * (1.0 + sc2) + sh2
        x = x + g2 * swiglu(h, ffn_w_gate_up[layer], ffn_w_down[layer])
    return rms_norm(x) * final_norm_w


_drawn_inputs = setup_inputs


def setup_inputs(seed=0):
    import zlib

    import numpy as np

    out = dict(_drawn_inputs(seed))
    spreads = {}
    factors = {}
    for name, (base, spread) in spreads.items():
        noise = np.random.default_rng([zlib.crc32(name.encode()), seed]).standard_normal(out[name].shape)
        drawn = base * np.exp(spread * noise) if base else spread * noise
        out[name] = jnp.asarray(drawn.astype(out[name].dtype))
    for name, factor in factors.items():
        out[name] = (out[name] * factor).astype(out[name].dtype)
    return out
```

```python
from contextlib import ExitStack

import concourse.bass as bass
from concourse import mybir

F32 = mybir.dt.float32
F32R = mybir.dt.float32r
ALU = mybir.AluOpType
ACT = mybir.ActivationFunctionType

P = 128
D = 1024
S = 1024
NT = S // P
KD = D // P
NH = 4
DK = 128
DV = 256
DFF = 2816
NF = DFF // P
NG = NF // 2
HALF = 512
UW = 2 * D
EPS = 1e-6
CAP = 15.0
MASKED = 1e30
U_HEAD = 3
U_OUT = U_HEAD * NH
U_FF = U_OUT + 4
NU = U_FF + 3 * NG
GATE_ROWS = 36


def build(nc, x, c_col, ada_first, ada_first_b, ada_rest, ada_rest_b, w_units, w_gates, b_if, norm_w, final_w, out,
          scan_rows, mod_rows):
    with ExitStack() as ctx:
        base = (nc.sbuf_base + 63) // 64 * 64
        ctx.enter_context(nc.sbuf_tensor("arena", [P, (212800 - 64) // 4], F32))

        def at(name, shape, offset, dt=F32):
            return nc.alloc_sbuf_tensor_at(name, shape, dt, offset=base + offset)

        hH = at("hH", [P, KD, S], 0, F32R)
        hL = at("hL", [P, KD, S], 32768, F32R)
        wH = at("wH", [P, 3, UW], 65536, F32R)
        wL = at("wL", [P, 3, UW], 90112, F32R)
        raw = at("raw", [P, UW], 114688)
        G0 = 122880
        ada0 = at("ada0", [P, 2, 4, D], G0)
        rows = at("rows", [P, 8, S], G0)
        hg = at("hg", [P, NT, D], G0)
        sc2 = at("sc2", [P, D], G0)
        sh2 = at("sh2", [P, D], G0 + 4096)
        hn2 = at("hn2", [P, 2, D], G0 + 8192)
        stage = at("stage", [P, 2, S], G0)
        sg = at("sg", [P, 2, HALF], G0 + 8192)
        fw = at("fw", [P, D], G0 + 12288)
        actH = at("actH", [P, 2, S], G0 + 16384, F32R)
        actL = at("actL", [P, 2, S], G0 + 24576, F32R)
        X0 = G0 + 32768
        acc0 = at("acc0", [P, D], X0)
        xin = at("xin", [P, 2, D], X0 + 4096)
        hn1 = at("hn1", [P, 2, D], X0 + 12288)
        sc1 = at("sc1", [P, D], X0 + 20480)
        sh1 = at("sh1", [P, D], X0 + 24576)
        wg_raw = at("wg_raw", [P, KD, GATE_ROWS], X0 + 28672)
        qT = at("qT", [P, S], X0)
        kT = at("kT", [P, S], X0 + 4096)
        va = at("va", [P, NT, DV + 1], X0 + 8192)
        Mb = at("Mb", [P, S], X0 + 16416)
        sI = at("sI", [P, S], X0 + 20512)
        ada = at("ada", [P, 2, HALF], X0 + 24608)
        acc = at("acc", [P, HALF], X0 + 28704)
        x2 = at("x2", [P, NT, D], X0)
        gb = at("gb", [P, D], X0 + 32768)
        b_sh = at("b_sh", [P, D], X0 + 32768)
        Z0 = X0 + 36864
        E = at("E", [P, 2, P], Z0)
        PT = at("PT", [P, 2, P], Z0 + 1024)
        kw = at("kw", [P, 2, P], Z0 + 2048)
        qs = at("qs", [P, 2, P], Z0 + 3072)
        junk = at("junk", [P, D], Z0)
        hc = at("hc", [P, 2, DV], Z0 + 4096)
        th = at("th", [P, 2, DV], Z0 + 6144)
        gate = at("gate", [P, 2, DV], Z0 + 8192)
        C = at("C", [P, DV + 1], Z0 + 10240)
        ident = at("ident", [P, P], Z0 + 11296)
        ones = at("ones", [P, P], Z0 + 11808)
        maskb = at("maskb", [P, P], Z0 + 12320)
        nwb = at("nwb", [P, DV], Z0 + 12832)
        brow = at("brow", [P, HALF], Z0 + 13856)
        adarow = at("adarow", [P, HALF], Z0 + 15904)
        b_sc = at("b_sc", [P, D], Z0 + 13856)
        Y0 = Z0 + 17952
        craw = at("craw", [P, KD], Y0)
        cact = at("cact", [P, KD], Y0 + 32)
        ms = at("ms", [P, 3 * NT], Y0 + 64)
        var = at("var", [P, 3 * NT], Y0 + 160)
        sd = at("sd", [P, 3 * NT], Y0 + 256)
        rstd = at("rstd", [P, 3 * NT], Y0 + 352)
        aT = at("aT", [P, NH * NT], Y0 + 448)
        tT = at("tT", [P, NH * NT], Y0 + 576)
        thr = at("thr", [P, NH * NT], Y0 + 704)
        hms = at("hms", [P, NH * NT], Y0 + 832)
        hvar = at("hvar", [P, NH * NT], Y0 + 960)
        hsd = at("hsd", [P, NH * NT], Y0 + 1088)
        hrs = at("hrs", [P, NH * NT], Y0 + 1216)
        den = at("den", [P, 2], Y0 + 1344)
        rden = at("rden", [P, 2], Y0 + 1376)
        bcol = at("bcol", [P, 1], Y0 + 1408)
        bcol15 = at("bcol15", [P, 1], Y0 + 1440)
        mp = at("mp", [P, NT], Y0 + 1472)
        sqj = at("sqj", [P, DV], Y0 + 1504, mybir.dt.bfloat16)
        tmp = at("tmp", [P, 2, DV], Z0 + 8192)

        T_, NL, NB, A_, DD, M_, SI, MR = range(8)

        def row(n, p0=0, p1=NH):
            return rows[p0:p1, n, :]

        ST = [ctx.enter_context(nc.psum_tensor(f"ST{i}", [P, HALF], F32)) for i in range(2)]
        O = [ctx.enter_context(nc.psum_tensor(f"O{i}", [P, HALF], F32)) for i in range(2)]
        OP = [ctx.enter_context(nc.psum_tensor(f"OP{i}", [P, HALF], F32)) for i in range(2)]
        DC = ctx.enter_context(nc.psum_tensor("DC", [P, HALF], F32))
        AD = ctx.enter_context(nc.psum_tensor("AD", [P, HALF], F32))
        QK_BANKS = [O[0], O[1], ST[0], ST[1]]
        Y_BANKS = [OP[0], OP[1], DC, AD]
        GU_BANKS = [O[0], O[1], ST[0], ST[1]]

        def sem(name):
            return ctx.enter_context(nc.semaphore(name))

        c_in, bif_in, wg_in, bsc_in, bsh_in = sem("c_in"), sem("bif_in"), sem("wg_in"), sem("bsc_in"), sem("bsh_in")
        ada0_in = [sem(f"ada0_in{i}") for i in range(2)]
        x_in = [sem(f"x_in{i}") for i in range(2)]
        x2_in = [sem(f"x2_in{i}") for i in range(4)]
        raw_in = sem("raw_in")
        ada_in = [sem(f"ada_in{i}") for i in range(2)]
        brow_in, rows_out, bc_in, nw_in, mod_out = (sem("brow_in"), sem("rows_out"), sem("bc_in"), sem("nw_in"),
                                                     sem("mod_out"))
        sc2_in, sh2_in, g1_in, g2_in, fw_in = sem("sc2_in"), sem("sh2_in"), sem("g1_in"), sem("g2_in"), sem("fw_in")
        out_done = sem("out_done")
        const_0, const_ok, ones_ok, rows_set = sem("const_0"), sem("const_ok"), sem("ones_ok"), sem("rows_set")
        c_act = sem("c_act")
        acc0_ok, mod0_mm, mod0_ev = sem("acc0_ok"), sem("mod0_mm"), sem("mod0_ev")
        n_ms, n_var, n_sd, n_rstd, n_hn, n_sh, n_tr, n_H, n_L = (
            sem(f"norm_{s}") for s in ("ms", "var", "sd", "rstd", "scaled", "shifted", "transposed", "H", "L"))
        w_H, w_L, w_scaled = sem("w_H"), sem("w_L"), sem("w_scaled")
        wg_zero, wg_H, wg_L, gates_mm = sem("wg_zero"), sem("wg_H"), sem("wg_L"), sem("gates_mm")
        b15_ok, g_act, g_dve, rT_mm, rT_cp, thr_ok = (sem("b15_ok"), sem("g_act"), sem("g_dve"), sem("rT_mm"),
                                                      sem("rT_cp"), sem("thr_ok"))
        qk_mm, qk_ev, v_mm, v_ev, v_one = sem("qk_mm"), sem("qk_ev"), sem("v_mm"), sem("v_ev"), sem("v_one")
        masked, e_ok, st_mm, kwpt, qs_ok = sem("masked"), sem("e_ok"), sem("st_mm"), sem("kwpt"), sem("qs_ok")
        op_mm, th_ok, gate_ok = sem("op_mm"), sem("th_ok"), sem("gate_ok")
        o_mm, dc_mm, c_ok = sem("o_mm"), sem("dc_mm"), sem("c_ok")
        den_ok, rden_ok, hc_ok, hms_ok, hg_ok = sem("den_ok"), sem("rden_ok"), sem("hc_ok"), sem("hms_ok"), sem("hg_ok")
        acc_ok, ad_mm, ad_ev = sem("acc_ok"), sem("ad_mm"), sem("ad_ev")
        h_var, h_sd, h_rs = sem("h_var"), sem("h_sd"), sem("h_rs")
        og_n, og_tr, og_H, og_L = sem("og_n"), sem("og_tr"), sem("og_H"), sem("og_L")
        y_mm, y_g, y_ev = sem("y_mm"), sem("y_g"), sem("y_ev")
        gu_mm, sg_ok, st_ok, a_H, a_L = sem("gu_mm"), sem("sg_ok"), sem("st_ok"), sem("a_H"), sem("a_L")
        d_mm, d_ev, f_out = sem("d_mm"), sem("d_ev"), sem("f_out")

        def slot(k):
            return k % 3

        def unit_weights(k, width):
            return tuple(w[:, slot(k), :].rearrange("p (k n) -> p k n", n=width) for w in (wH, wL))

        def piece(t, i):
            return t[:, i * D:(i + 1) * D]

        block = ctx.enter_context(nc.Block())

        @block.sync
        def _(sp):
            def load_unit(u, first=False):
                if not first:
                    sp.wait_ge(w_L, u * 2)
                src = w_units[u] if isinstance(u, int) else w_units[bass.ds(u, 1), :, :].rearrange("a p n -> (a p) n")
                sp.dma_start(raw[:], src).then_inc(raw_in, 16)

            sp.dma_start(craw[:], c_col).then_inc(c_in, 16)
            sp.dma_start(b_sc[0:1, :], ada_first_b[0:1, :]).then_inc(bsc_in, 16)
            sp.dma_start(b_sh[0:1, :], ada_first_b[1:2, :]).then_inc(bsh_in, 16)
            for m in range(2):
                for j in range(2):
                    if m:
                        sp.wait_ge(acc0_ok, 4 * (j + 1))
                    sp.dma_start(ada0[:, j], ada_first[m, j]).then_inc(ada0_in[j], 16)
                if m == 0:
                    for t in range(2):
                        sp.dma_start(xin[:, t, :], x[t]).then_inc(x_in[t], 16)
                    sp.dma_start(wg_raw[:], w_gates).then_inc(wg_in, 16)
            load_unit(0, True)
            for t in range(2, NT):
                sp.wait_ge(n_hn, t - 1)
                sp.wait_ge(n_ms, t - 1)
                sp.dma_start(xin[:, t % 2, :], x[t]).then_inc(x_in[t % 2], 16)
            load_unit(1)
            load_unit(2)

            def ada_item(h, i, first):
                if not (first and i < 2):
                    sp.wait_ge(acc_ok, h * 16 + i - 1)
                sp.dma_start(ada[:, i % 2, :],
                               ada_rest[bass.ds(h * 16 + i, 1), :, :].rearrange("a p n -> (a p) n")
                               if not first else ada_rest[i]).then_inc(ada_in[i % 2], 16)

            def ada_bias(h, half, first):
                if not (first and half == 0):
                    sp.wait_ge(ad_mm, h * 2 + half)
                sp.dma_start(brow[0:1, :], ada_rest_b[bass.ds(h * 2 + half, 1), :] if not first
                               else ada_rest_b[half:half + 1, :]).then_inc(brow_in, 16)

            def mod_store(h, half, first):
                sp.wait_ge(ad_ev, h * 2 + half + 1)
                sp.dma_start(mod_rows[bass.ds(h * 2 + half, 1), :] if not first else mod_rows[half:half + 1, :],
                               adarow[0:1, :]).then_inc(mod_out, 16)

            def head(h, first):
                load_unit(h * 3 + 3)
                if first:
                    sp.wait_ge(rows_out, 32)
                    m_src, s_src, n_src = scan_rows[0, 0:1, :], scan_rows[1, 0:1, :], norm_w[0:1, :]
                else:
                    sp.wait_ge(gate_ok, h * NT)
                    m_src, s_src = (scan_rows[i, bass.ds(h, 1), :] for i in range(2))
                    n_src = norm_w[bass.ds(h, 1), :]
                sp.dma_start(Mb[:], m_src.to_broadcast([P, S])).then_inc(bc_in, 16)
                sp.dma_start(sI[:], s_src.to_broadcast([P, S])).then_inc(bc_in, 16)
                sp.dma_start(nwb[:], n_src.to_broadcast([P, DV])).then_inc(nw_in, 16)
                ada_bias(h, 0, first)
                ada_item(h, 0, first)
                ada_item(h, 1, first)
                load_unit(h * 3 + 4)
                for c in range(NT):
                    if c < NT - 1:
                        ada_item(h, 2 * c + 2, first)
                        ada_item(h, 2 * c + 3, first)
                    if c == 4:
                        mod_store(h, 0, first)
                        ada_bias(h, 1, first)
                        load_unit(h * 3 + 5)
                mod_store(h, 1, first)

            head(0, True)
            with sp.Fori(1, NH) as h:
                head(h, False)
            sp.wait_ge(o_mm, NT * NH)
            sp.wait_ge(dc_mm, (NT - 1) * NH)
            sp.wait_ge(c_ok, (NT - 1) * NH)
            sp.wait_ge(e_ok, NT * NH)
            sp.wait_ge(kwpt, NT * NH)
            sp.wait_ge(qs_ok, (NT - 1) * NH)
            sp.wait_ge(ad_mm, 2 * NH)
            for i in range(4):
                sp.dma_start(x2[:, 2 * i:2 * i + 2, :],
                             x[2 * i:2 * i + 2].rearrange("t p n -> p t n")).then_inc(x2_in[i], 16)
            with sp.Fori(U_OUT + 3, NU) as u:
                load_unit(u)
            for t in range(NT):
                sp.wait_ge(f_out, t + 1)
                sp.dma_start(out[t], x2[:, t, :]).then_inc(out_done, 16)
            sp.wait_ge(out_done, 16 * NT)

        @block.gpsimd
        def _(pool):
            nc.gpsimd.memset(ones[:], 1.0).then_inc(ones_ok, 1)
            nc.gpsimd.memset(ident[:], 0.0).then_inc(const_0, 1)
            nc.gpsimd.memset(maskb[:], 0.0).then_inc(const_0, 1)
            nc.gpsimd.memset(bcol[:], 0.0).then_inc(const_0, 1)
            pool.wait_ge(const_0, 3)
            nc.gpsimd.affine_select(out=ident[:], in_=ident[:], compare_op=ALU.not_equal, fill=1.0, base=0,
                                    pattern=[[-1, P]], channel_multiplier=1).then_inc(const_ok, 1)
            nc.gpsimd.affine_select(out=maskb[:], in_=maskb[:], compare_op=ALU.is_ge, fill=MASKED, base=0,
                                    pattern=[[1, P]], channel_multiplier=-1).then_inc(const_ok, 1)
            pool.dma_start(bcol[0:NH, :], b_if[0:NH, :]).then_inc(bif_in, 16)
            pool.dma_start(bcol[32:32 + NH, :], b_if[NH:2 * NH, :]).then_inc(bif_in, 16)

            def shift(i, hn, sh):
                pool.wait_ge(n_hn, i + 1)
                nc.gpsimd.tensor_tensor(hn[:, i % 2, :], hn[:, i % 2, :], sh[:], ALU.add).then_inc(n_sh, 1)

            for t in range(NT):
                if t == 0:
                    pool.wait_ge(mod0_ev, 4)
                    nc.gpsimd.memset(rows[0:GATE_ROWS, A_, :], 0.0).then_inc(rows_set, 1)
                    nc.gpsimd.memset(row(DD), 0.0).then_inc(rows_set, 1)
                    nc.gpsimd.memset(row(MR), 1.0).then_inc(rows_set, 1)
                    pool.wait_ge(rows_set, 3)
                    nc.gpsimd.memset(rows[0:NH, MR, 0:S:P], 0.0).then_inc(rows_set, 1)
                shift(t, hn1, sh1)

            def head(h, first):
                if first:
                    pool.wait_ge(g_act, 5)
                    pool.dma_start(scan_rows[1], row(SI)).then_inc(rows_out, 16)
                    pool.dma_start(scan_rows[0], row(M_)).then_inc(rows_out, 16)
                pool.wait_ge(bc_in, h * 32 + 32)
                mv = Mb[:].rearrange("p (c l) -> p c l", l=P)
                nc.gpsimd.tensor_tensor(mv, mv, maskb[:].unsqueeze(1).to_broadcast([P, NT, P]),
                                        ALU.add).then_inc(masked, 1)
                pool.wait_ge(qk_ev, h * 4 + 4)
                for c in range(NT + 1):
                    if 1 <= c < NT:
                        if c >= 2:
                            pool.wait_ge(o_mm, h * NT + c - 1)
                        elif not first:
                            pool.wait_ge(o_mm, h * NT)
                        nc.gpsimd.tensor_tensor(qs[:, c % 2, :], qT[:, c * P:(c + 1) * P],
                                                sI[:, c * P:(c + 1) * P], ALU.mult).then_inc(qs_ok, 1)
                    if 1 <= c:
                        pool.wait_ge(hc_ok, h * NT + c)
                        pool.wait_ge(gate_ok, h * NT + c)
                        dst = (hg[:, c - 1, 0:DV] if first else hg[:, c - 1, bass.ds(h * DV, DV)])
                        nc.gpsimd.tensor_tensor(dst, hc[:, (c - 1) % 2, :], gate[:, (c - 1) % 2, :],
                                                ALU.mult).then_inc(hg_ok, 1)

            head(0, True)
            with pool.Fori(1, NH) as h:
                head(h, False)

            pool.wait_ge(mod_out, 16 * 2 * NH)
            pool.dma_start(gb[:], mod_rows[0:2, :].rearrange("(o a) n -> o (a n)", o=1).to_broadcast([P, D])).then_inc(g1_in, 16)
            pool.wait_ge(og_tr, 2 * NT)
            pool.dma_start(sh2[:], mod_rows[2:4, :].rearrange("(o a) n -> o (a n)", o=1).to_broadcast([P, D])).then_inc(sh2_in, 16)
            pool.dma_start(sc2[:], mod_rows[4:6, :].rearrange("(o a) n -> o (a n)", o=1).to_broadcast([P, D])).then_inc(sc2_in, 16)
            pool.wait_ge(sh2_in, 16)
            for t in range(NT):
                shift(NT + t, hn2, sh2)
            pool.wait_ge(n_tr, 4 * NT)
            pool.dma_start(fw[:], final_w.to_broadcast([P, D])).then_inc(fw_in, 16)
            pool.wait_ge(y_g, 4 * NT)
            pool.dma_start(gb[:], mod_rows[6:8, :].rearrange("(o a) n -> o (a n)", o=1).to_broadcast([P, D])).then_inc(g2_in, 16)
            pool.wait_ge(g2_in, 16)

            def scale_down(u, g):
                pool.wait_ge(raw_in, u * 16 + 16)
                rv = raw[:].rearrange("p (f n) -> p f n", n=D)
                nc.gpsimd.tensor_tensor(rv, rv, gb[:].unsqueeze(1).to_broadcast([P, 2, D]),
                                        ALU.mult).then_inc(w_scaled, 1)

            scale_down(U_FF + 3, 0)
            with pool.Fori(1, NG - 1) as g:
                scale_down(g * 3 + U_FF + 3, g)
            scale_down(NU - 1, NG - 1)

        @block.scalar
        def _(act):
            def split_H(u, k, free=None, pieces=(0, 1), down=None):
                for i in pieces:
                    if i == 0:
                        act.wait_ge(raw_in, u * 16 + 16)
                        if down is not None:
                            act.wait_ge(w_scaled, down)
                        if free is not None:
                            act.wait_ge(*free)
                    nc.scalar.copy(piece(wH[:, slot(k), :], i), piece(raw, i)).then_inc(w_H, 1)

            act.wait_ge(c_in, 16)
            nc.scalar.activation(cact[:], craw[:], ACT.Silu).then_inc(c_act, 1)

            def square(i, src):
                nc.scalar.activation(junk[:], src, ACT.Square, accum_out=ms[:, i:i + 1]).then_inc(n_ms, 1)

            def root(i):
                act.wait_ge(n_var, i + 1)
                nc.scalar.activation(sd[:, i:i + 1], var[:, i:i + 1], ACT.Sqrt).then_inc(n_sd, 1)

            def high(i, t):
                for j in range(2):
                    act.wait_ge(n_tr, 2 * i + j + 1)
                    nc.scalar.copy(hH[:, 4 * j:4 * j + 4, t * P:(t + 1) * P],
                                   ST[j][:].rearrange("p (k n) -> p k n", n=P)).then_inc(n_H, 1)

            def square_x(t):
                act.wait_ge(x_in[t % 2], 16 * (t // 2 + 1))
                if t:
                    act.wait_ge(n_ms, t)
                square(t, xin[:, t % 2, :])
                root(t)

            square_x(0)
            square_x(1)
            for t in range(NT):
                high(t, t)
                if t == 0:
                    act.wait_ge(wg_in, 16)
                    act.wait_ge(wg_zero, 2)
                    wgH = wH[:, 2, 0:KD * P].rearrange("p (k n) -> p k n", n=P)
                    nc.scalar.copy(wgH[:, :, 0:GATE_ROWS], wg_raw[:]).then_inc(wg_H, 1)
                if t == 1:
                    split_H(0, 0)
                if t + 2 < NT:
                    square_x(t + 2)
            split_H(1, 1)

            def evac_qk(h, i):
                act.wait_ge(qk_mm, h * 4 + i + 1)
                dst = (qT if i % 2 == 0 else kT)[:, (i // 2) * HALF:(i // 2 + 1) * HALF]
                nc.scalar.activation(dst, QK_BANKS[i][:], ACT.Copy,
                                     scale=1.0 if i % 2 == 0 else float(DK) ** -0.5).then_inc(qk_ev, 1)

            def gates_scalar():
                act.wait_ge(b15_ok, 1)
                act.wait_ge(mod0_ev, 4)
                for j in range(2):
                    act.wait_ge(gates_mm, j + 1)
                    nc.scalar.activation(rows[0:GATE_ROWS, T_, j * HALF:(j + 1) * HALF], OP[j][0:GATE_ROWS, :],
                                         ACT.Tanh, bias=bcol15[0:GATE_ROWS, :], scale=1.0 / CAP).then_inc(g_act, 1)
                act.wait_ge(g_act, 2)
                nc.scalar.activation(row(NL), row(T_, 32, 32 + NH), ACT.Exp, scale=-CAP).then_inc(g_act, 1)
                act.wait_ge(g_act, 3)
                nc.scalar.activation(row(NL), row(NL), ACT.Ln, bias=1.0).then_inc(g_act, 1)

            def head(h, first):
                if first:
                    evac_qk(h, 0)
                    evac_qk(h, 1)
                    gates_scalar()
                    split_H(2, 2, (gates_mm, 2))
                    evac_qk(h, 2)
                    evac_qk(h, 3)
                    act.wait_ge(g_dve, 6)
                    nc.scalar.activation(row(SI), row(SI), ACT.Exp).then_inc(g_act, 1)
                else:
                    for i in range(4):
                        if i == 0:
                            act.wait_ge(o_mm, h * NT)
                            act.wait_ge(st_mm, h * NT)
                            act.wait_ge(qs_ok, h * (NT - 1))
                        evac_qk(h, i)
                        if i == 0:
                            split_H(h * 3 + 2, 2, (op_mm, h * NT))
                for t in range(NT):
                    act.wait_ge(v_mm, h * NT + t + 1)
                    nc.scalar.copy(va[:, t, 0:DV], OP[t % 2][:, 0:DV]).then_inc(v_ev, 1)
                    if t == 1:
                        split_H(h * 3 + 3, 0, (qk_mm, h * 4 + 4))
                    if t == 5 and first:
                        act.wait_ge(rT_cp, 2)
                        nc.scalar.activation(thr[:], tT[:], ACT.Exp).then_inc(thr_ok, 1)
                act.wait_ge(masked, h + 1)

                def decay(c):
                    if c >= 2:
                        act.wait_ge(kwpt, h * NT + c - 1)
                    elif not first:
                        act.wait_ge(kwpt, h * NT)
                    col = aT[:, c:c + 1] if first else aT[:, bass.ds(h * NT + c, 1)]
                    nc.scalar.activation(E[:, c % 2, :], Mb[:, c * P:(c + 1) * P], ACT.Exp, scale=-1.0,
                                         bias=col).then_inc(e_ok, 1)

                def squares(c):
                    act.wait_ge(hc_ok, h * NT + c + 1)
                    if not (first and c == 0):
                        act.wait_ge(hms_ok, h * NT + c)
                    col = hms[:, c:c + 1] if first else hms[:, bass.ds(h * NT + c, 1)]
                    nc.scalar.activation(sqj[:], hc[:, c % 2, :], ACT.Square, accum_out=col).then_inc(hms_ok, 1)

                decay(0)
                for c in range(NT):
                    if c + 1 < NT:
                        decay(c + 1)
                    act.wait_ge(op_mm, h * NT + c + 1)
                    if c >= 2:
                        act.wait_ge(gate_ok, h * NT + c - 1)
                    elif not first:
                        act.wait_ge(gate_ok, h * NT)
                    nc.scalar.activation(th[:, c % 2, :], OP[c % 2][:, 0:DV], ACT.Tanh, scale=0.5).then_inc(th_ok, 1)
                    if c in (1, 3):
                        split_H(h * 3 + 4, 1, (v_mm, h * NT + NT), pieces=(c // 2,))
                    if c:
                        squares(c - 1)
                squares(NT - 1)

            head(0, True)
            with act.Fori(1, NH) as h:
                head(h, False)

            act.wait_ge(h_var, 1)
            nc.scalar.activation(hsd[:], hvar[:], ACT.Sqrt).then_inc(h_sd, 1)
            split_H(U_OUT + 2, 2, (op_mm, NH * NT))
            for t in range(NT):
                for j in range(2):
                    act.wait_ge(og_tr, 2 * t + j + 1)
                    nc.scalar.copy(hH[:, 4 * j:4 * j + 4, t * P:(t + 1) * P],
                                   ST[j][:].rearrange("p (k n) -> p k n", n=P)).then_inc(og_H, 1)
            split_H(U_OUT + 3, 0, (y_mm, NT))
            split_H(U_FF, 1, (y_mm, 2 * NT))
            split_H(U_FF + 1, 2, (y_mm, 3 * NT))

            def square_x2(t):
                act.wait_ge(y_ev, 3 * NT + t + 1)
                act.wait_ge(n_ms, NT + t)
                square(NT + t, x2[:, t, :])
                root(NT + t)

            square_x2(0)
            for t in range(NT):
                if t + 1 < NT:
                    square_x2(t + 1)
                high(NT + t, t)

            def silu(f_count, half):
                n = f_count * 2 + half
                act.wait_ge(gu_mm, n * 2 + 1)
                if not isinstance(n, int) or n >= 2:
                    act.wait_ge(st_ok, n - 1)
                nc.scalar.activation(sg[:, half, :], GU_BANKS[2 * half][:], ACT.Silu).then_inc(sg_ok, 1)

            def act_high(f_count, f, half):
                n = f_count * 2 + half
                act.wait_ge(st_ok, n + 1)
                nc.scalar.copy(actH[:, f, half * HALF:(half + 1) * HALF],
                               stage[:, f, half * HALF:(half + 1) * HALF]).then_inc(a_H, 1)

            act.wait_ge(n_sh, 2 * NT)
            split_H(U_FF + 2, 0, (y_mm, 4 * NT))
            for half in range(2):
                silu(0, half)
                act_high(0, 0, half)
            split_H(U_FF + 3, 1, (gu_mm, 4), down=1)
            for half in range(2):
                silu(1, half)
                act_high(1, 1, half)

            def group(g, last):
                u = g * 3 + (U_FF - 1)
                split_H(u + 2, 2, (gu_mm, g * 8))
                for half in range(2):
                    silu(g * 2, half)
                split_H(u + 3, 0, (gu_mm, g * 8 + 4), down=NG if last else None)
                act.wait_ge(d_mm, g * 16)
                for half in range(2):
                    act_high(g * 2, 0, half)
                if not last:
                    split_H(u + 4, 1, (d_mm, g * 16), down=g + 1)
                for half in range(2):
                    silu(g * 2 + 1, half)
                    act_high(g * 2 + 1, 1, half)

            with act.Fori(1, NG - 1) as g:
                group(g, False)
            group(NG - 1, True)
            for t in range(NT):
                i = 2 * NT + t
                act.wait_ge(d_ev, 16 * (NG - 1) + 2 * t + 2)
                act.wait_ge(n_ms, i)
                square(i, x2[:, t, :])
                root(i)

        @block.vector
        def _(dve):
            def split_L(u, k, pieces=(0, 1)):
                for i in pieces:
                    dve.wait_ge(w_H, u * 2 + i + 1)
                    nc.vector.tensor_tensor(piece(wL[:, slot(k), :], i), piece(raw, i),
                                            piece(wH[:, slot(k), :], i).bitcast(F32), ALU.subtract).then_inc(w_L, 1)

            for w in (wH, wL):
                nc.vector.memset(w[:, 2, 0:KD * P].bitcast(F32), 0.0).then_inc(wg_zero, 1)
            dve.wait_ge(bif_in, 32)
            nc.vector.tensor_scalar(bcol15[:], bcol[:], 1.0 / CAP, None, ALU.mult).then_inc(b15_ok, 1)

            dve.wait_ge(c_act, 1)
            for m in range(2):
                for k in range(KD):
                    if k % 4 == 0:
                        dve.wait_ge(ada0_in[k // 4], 16 * (m + 1))
                    n = m * KD + k
                    if k == 0:
                        if m:
                            dve.wait_ge(mod0_mm, 2)
                        nc.vector.tensor_scalar(acc0[:], ada0[:, 0, 0, :], cact[:, 0:1], None,
                                                ALU.mult).then_inc(acc0_ok, 1)
                    else:
                        dve.wait_ge(acc0_ok, n)
                        nc.vector.scalar_tensor_tensor(acc0[:], ada0[:, k // 4, k % 4, :], cact[:, k:k + 1], acc0[:],
                                                       ALU.mult, ALU.add).then_inc(acc0_ok, 1)
                if m:
                    for j in range(2):
                        dve.wait_ge(mod0_mm, j + 1)
                        nc.vector.tensor_scalar(sc1[:, j * HALF:(j + 1) * HALF], OP[j][:], 1.0, None,
                                                ALU.add).then_inc(mod0_ev, 1)

            def variance(i):
                dve.wait_ge(n_ms, i + 1)
                nc.vector.tensor_scalar(var[:, i:i + 1], ms[:, i:i + 1], 1.0 / D, EPS, ALU.mult,
                                        ALU.add).then_inc(n_var, 1)

            def norm(i, src, hn, scale):
                dve.wait_ge(n_sd, i + 1)
                nc.vector.reciprocal(rstd[:, i:i + 1], sd[:, i:i + 1]).then_inc(n_rstd, 1)
                dve.wait_ge(n_rstd, i + 1)
                if i % NT >= 2:
                    dve.wait_ge(n_tr, 2 * (i - 1))
                nc.vector.scalar_tensor_tensor(hn[:, i % 2, :], src, rstd[:, i:i + 1], scale[:], ALU.mult,
                                               ALU.mult).then_inc(n_hn, 1)

            def low(i, t):
                for j in range(2):
                    dve.wait_ge(n_H, 2 * i + j + 1)
                    cols = slice(t * P, (t + 1) * P)
                    nc.vector.tensor_tensor(hL[:, 4 * j:4 * j + 4, cols], ST[j][:].rearrange("p (k n) -> p k n", n=P),
                                            hH[:, 4 * j:4 * j + 4, cols].bitcast(F32), ALU.subtract).then_inc(n_L, 1)

            variance(0)
            variance(1)
            for j in range(2):
                dve.wait_ge(mod0_mm, 2 + j + 1)
                nc.vector.tensor_copy(sh1[:, j * HALF:(j + 1) * HALF], (DC, AD)[j][:]).then_inc(mod0_ev, 1)
            dve.wait_ge(mod0_ev, 2)
            norm(0, xin[:, 0, :], hn1, sc1)
            for t in range(NT):
                if t + 1 < NT:
                    if t + 1 >= 2:
                        variance(t + 1)
                    norm(t + 1, xin[:, (t + 1) % 2, :], hn1, sc1)
                low(t, t)
                if t == 0:
                    dve.wait_ge(wg_H, 1)
                    wgH, wgL = (w[:, 2, 0:KD * P].rearrange("p (k n) -> p k n", n=P)[:, :, 0:GATE_ROWS]
                                for w in (wH, wL))
                    nc.vector.tensor_tensor(wgL, wg_raw[:], wgH.bitcast(F32), ALU.subtract).then_inc(wg_L, 1)
                if t == 1:
                    split_L(0, 0)
            split_L(1, 1)

            def gates_rows():
                dve.wait_ge(g_act, 4)
                dve.wait_ge(rows_set, 4)
                nc.vector.tensor_tensor_scan(row(NB), row(MR), row(NL), 0.0, ALU.mult, ALU.add).then_inc(g_dve, 1)
                dve.wait_ge(g_dve, 1)
                nc.vector.scalar_tensor_tensor(row(A_), row(T_), CAP, row(NB), ALU.mult, ALU.add).then_inc(g_dve, 1)
                nc.vector.tensor_scalar(rows[0:NH, DD, P:S:P], rows[0:NH, NB, P - 1:S - 1:P], -1.0, None,
                                        ALU.mult).then_inc(g_dve, 1)
                dve.wait_ge(g_dve, 3)
                nc.vector.tensor_tensor_scan(row(M_), row(DD), row(A_), 0.0, ALU.add, ALU.max).then_inc(g_dve, 1)
                nc.vector.memset(mp[0:NH, 0:1], 0.0).then_inc(g_dve, 1)
                dve.wait_ge(g_dve, 5)
                nc.vector.tensor_tensor(mp[0:NH, 1:NT], rows[0:NH, M_, P - 1:S - 1:P], rows[0:NH, DD, P:S:P],
                                        ALU.add).then_inc(rT_cp, 1)
                dve.wait_ge(rT_cp, 1)
                nc.vector.tensor_tensor(row(SI).rearrange("p (c l) -> p c l", l=P),
                                        mp[0:NH, :].unsqueeze(2).to_broadcast([NH, NT, P]),
                                        row(M_).rearrange("p (c l) -> p c l", l=P), ALU.subtract).then_inc(g_dve, 1)
                nc.vector.tensor_tensor(row(A_, 32, 32 + NH), row(NB), row(M_), ALU.subtract).then_inc(g_dve, 1)

            def gates_columns():
                dve.wait_ge(rT_mm, 1)
                for n, t in enumerate((aT, tT)):
                    ins = nc.vector.tensor_copy(t[:].rearrange("p (h c) -> p c h", h=NH),
                                                AD[:, 0:NT * GATE_ROWS].rearrange("p (c r) -> p c r", r=GATE_ROWS)
                                                [:, :, 32 * n:32 * n + NH])
                ins.then_inc(rT_cp, 1)

            def head(h, first):
                if first:
                    nc.vector.memset(va[:, :, DV:DV + 1], 1.0).then_inc(v_one, 1)
                    gates_rows()
                    split_L(2, 2)
                    split_L(h * 3 + 3, 0)
                    gates_columns()
                    dve.wait_ge(thr_ok, 1)
                else:
                    split_L(h * 3 + 2, 2)
                    split_L(h * 3 + 3, 0)

                def weighted(c):
                    n = h * NT + c
                    dve.wait_ge(st_mm, n + 1)
                    dve.wait_ge(e_ok, n + 1)
                    if c >= 2:
                        dve.wait_ge(o_mm, n - 1)
                        dve.wait_ge(dc_mm, h * (NT - 1) + c - 1)
                    elif not first:
                        dve.wait_ge(o_mm, h * NT)
                        dve.wait_ge(dc_mm, h * (NT - 1))
                    nc.vector.tensor_scalar(kw[:, c % 2, :], ST[c % 2][:, P:2 * P], E[:, c % 2, P - 1:P], None, ALU.mult)
                    nc.vector.tensor_tensor(PT[:, c % 2, :], ST[c % 2][:, 0:P], E[:, c % 2, :],
                                            ALU.mult).then_inc(kwpt, 1)

                def state(c):
                    dve.wait_ge(dc_mm, h * (NT - 1) + c + 1)
                    if c == 0:
                        if not first:
                            dve.wait_ge(o_mm, h * NT)
                        nc.vector.tensor_copy(C[:], DC[:, 0:DV + 1]).then_inc(c_ok, 1)
                    else:
                        dve.wait_ge(c_ok, h * (NT - 1) + c)
                        e = (c + 1) * P - 1
                        nc.vector.scalar_tensor_tensor(C[:], C[:], sI[:, e:e + 1], DC[:, 0:DV + 1], ALU.mult,
                                                       ALU.add).then_inc(c_ok, 1)

                def divide(c):
                    n = h * NT + c
                    dve.wait_ge(o_mm, n + 1)
                    col = thr[:, c:c + 1] if first else thr[:, bass.ds(h * NT + c, 1)]
                    d = den[:, c % 2:c % 2 + 1]
                    nc.vector.tensor_scalar(d, O[c % 2][:, DV:DV + 1], -1.0, col, ALU.mult,
                                            ALU.max).then_inc(den_ok, 1)
                    dve.wait_ge(den_ok, n * 2 + 1)
                    nc.vector.tensor_scalar(d, O[c % 2][:, DV:DV + 1], d, None, ALU.max).then_inc(den_ok, 1)
                    dve.wait_ge(den_ok, n * 2 + 2)
                    nc.vector.reciprocal(rden[:, c % 2:c % 2 + 1], den[:, c % 2:c % 2 + 1]).then_inc(rden_ok, 1)
                    dve.wait_ge(rden_ok, n + 1)
                    if c >= 2:
                        dve.wait_ge(hg_ok, n - 1)
                        dve.wait_ge(hms_ok, n - 1)
                    elif not first:
                        dve.wait_ge(hg_ok, h * NT)
                        dve.wait_ge(hms_ok, h * NT)
                    nc.vector.tensor_scalar(hc[:, c % 2, :], O[c % 2][:, 0:DV], rden[:, c % 2:c % 2 + 1], None,
                                            ALU.mult).then_inc(hc_ok, 1)

                def gating(c):
                    n = h * NT + c
                    dve.wait_ge(th_ok, n + 1)
                    if c == 0:
                        dve.wait_ge(nw_in, h * 16 + 16)
                    if c >= 2:
                        dve.wait_ge(hg_ok, n - 1)
                    elif not first:
                        dve.wait_ge(hg_ok, h * NT)
                    nc.vector.scalar_tensor_tensor(gate[:, c % 2, :], th[:, c % 2, :], 1.0, nwb[:], ALU.add,
                                                   ALU.mult).then_inc(gate_ok, 1)

                def ada_item(i):
                    n = h * 16 + i
                    dve.wait_ge(ada_in[i % 2], h * 128 + (i // 2) * 16 + 16)
                    k = i % KD
                    if not (first and i == 0):
                        dve.wait_ge(acc_ok, n)
                    if k == 0:
                        if not (first and i == 0):
                            dve.wait_ge(ad_mm, h * 2 + i // KD)
                        nc.vector.tensor_scalar(acc[:], ada[:, i % 2, :], cact[:, 0:1], None,
                                                ALU.mult).then_inc(acc_ok, 1)
                    else:
                        nc.vector.scalar_tensor_tensor(acc[:], ada[:, i % 2, :], cact[:, k:k + 1], acc[:],
                                                       ALU.mult, ALU.add).then_inc(acc_ok, 1)

                def mod_row(half):
                    dve.wait_ge(ad_mm, h * 2 + half + 1)
                    if not (first and half == 0):
                        dve.wait_ge(mod_out, h * 32 + half * 16)
                    nc.vector.tensor_copy(adarow[0:1, :], AD[0:1, :]).then_inc(ad_ev, 1)

                for c in range(NT + 1):
                    if 1 <= c < NT:
                        state(c - 1)
                    if c < NT:
                        weighted(c)
                    if c:
                        divide(c - 1)
                        gating(c - 1)
                    if c < NT:
                        ada_item(2 * c)
                        ada_item(2 * c + 1)
                    if c in (2, 4):
                        split_L(h * 3 + 4, 1, pieces=(c // 2 - 1,))
                    if c == 4:
                        mod_row(0)
                mod_row(1)

            head(0, True)
            with dve.Fori(1, NH) as h:
                head(h, False)

            dve.wait_ge(hms_ok, NH * NT)
            nc.vector.tensor_scalar(hvar[:], hms[:], 1.0 / DV, EPS, ALU.mult, ALU.add).then_inc(h_var, 1)
            dve.wait_ge(h_sd, 1)
            nc.vector.reciprocal(hsd[:], hsd[:]).then_inc(h_rs, 1)
            dve.wait_ge(h_rs, 1)
            nc.vector.tensor_scalar(hrs[:], hsd[:], 0.5, None, ALU.mult).then_inc(h_rs, 1)
            dve.wait_ge(h_rs, 2)
            dve.wait_ge(hg_ok, NH * NT)
            rs = hrs[:].rearrange("p (h t) -> p t h", t=NT)

            def head_norm(t):
                hv = hg[:, t, :].rearrange("p (h v) -> p h v", h=NH)
                nc.vector.tensor_tensor(hv, hv, rs[:, t, :].unsqueeze(2).to_broadcast([P, NH, DV]),
                                        ALU.mult).then_inc(og_n, 1)

            def y_tile(n):
                j, t = divmod(n, NT)
                if n == 0:
                    dve.wait_ge(g1_in, 16)
                    dve.wait_ge(hg_ok, NH * NT)
                if j == 0 and t % 2 == 0:
                    dve.wait_ge(x2_in[t // 2], 16)
                dve.wait_ge(y_mm, n + 1)
                if n >= 2:
                    dve.wait_ge(y_ev, n - 1)
                nc.vector.tensor_tensor(tmp[:, n % 2, :], Y_BANKS[n % 4][:, 0:DV], gb[:, j * DV:(j + 1) * DV],
                                        ALU.mult).then_inc(y_g, 1)
                dve.wait_ge(y_g, n + 1)
                cols = slice(j * DV, (j + 1) * DV)
                nc.vector.tensor_tensor(x2[:, t, cols], x2[:, t, cols], tmp[:, n % 2, :], ALU.add).then_inc(y_ev, 1)

            head_norm(0)
            head_norm(1)
            for t in range(NT):
                for j in range(2):
                    dve.wait_ge(og_H, 2 * t + j + 1)
                    cols = slice(t * P, (t + 1) * P)
                    nc.vector.tensor_tensor(hL[:, 4 * j:4 * j + 4, cols], ST[j][:].rearrange("p (k n) -> p k n", n=P),
                                            hH[:, 4 * j:4 * j + 4, cols].bitcast(F32), ALU.subtract).then_inc(og_L, 1)
                if t + 2 < NT:
                    head_norm(t + 2)
                if t == 0:
                    split_L(U_OUT + 2, 2)
                if t >= 1:
                    y_tile(t - 1)
            y_tile(NT - 1)
            split_L(U_OUT + 3, 0)
            for n in range(NT, 2 * NT):
                y_tile(n)
            split_L(U_FF, 1)
            dve.wait_ge(sc2_in, 16)
            nc.vector.tensor_scalar(sc2[:], sc2[:], 1.0, None, ALU.add).then_inc(mod0_ev, 1)
            for n in range(2 * NT, 3 * NT):
                y_tile(n)
            split_L(U_FF + 1, 2)
            dve.wait_ge(mod0_ev, 5)
            for t in range(NT + 2):
                if t < NT:
                    y_tile(3 * NT + t)
                if 1 <= t <= NT:
                    variance(NT + t - 1)
                    norm(NT + t - 1, x2[:, t - 1, :], hn2, sc2)
                if t >= 2:
                    low(NT + t - 2, t - 2)

            def product(f_count, f, half):
                n = f_count * 2 + half
                dve.wait_ge(sg_ok, n + 1)
                dve.wait_ge(gu_mm, n * 2 + 2)
                if not isinstance(n, int) or n >= 4:
                    dve.wait_ge(a_L, n - 3)
                nc.vector.tensor_tensor(stage[:, f, half * HALF:(half + 1) * HALF], sg[:, half, :],
                                        GU_BANKS[2 * half + 1][:], ALU.mult).then_inc(st_ok, 1)

            def act_low(f_count, f, half):
                n = f_count * 2 + half
                dve.wait_ge(a_H, n + 1)
                cols = slice(half * HALF, (half + 1) * HALF)
                nc.vector.tensor_tensor(actL[:, f, cols], stage[:, f, cols], actH[:, f, cols].bitcast(F32),
                                        ALU.subtract).then_inc(a_L, 1)

            def add_down(g, first, lo, hi):
                for n in range(lo, hi):
                    dve.wait_ge(d_mm, g * 16 + n + 1)
                    t, j = divmod(n, 2)
                    cols = slice(j * HALF, (j + 1) * HALF)
                    nc.vector.tensor_tensor(x2[:, t, cols], x2[:, t, cols], Y_BANKS[n % 4][:],
                                            ALU.add).then_inc(d_ev, 1)

            split_L(U_FF + 2, 0)
            for half in range(2):
                product(0, 0, half)
                act_low(0, 0, half)
            split_L(U_FF + 3, 1)
            for half in range(2):
                product(1, 1, half)
                act_low(1, 1, half)

            def group(g, last):
                u = g * 3 + (U_FF - 1)
                split_L(u + 2, 2)
                for half in range(2):
                    product(g * 2, 0, half)
                if last:
                    add_down(g - 1, False, 0, 4)
                    split_L(u + 3, 0)
                    add_down(g - 1, False, 4, 16)
                else:
                    add_down(g - 1, False, 0, 4)
                    split_L(u + 3, 0)
                    add_down(g - 1, False, 4, 16)
                for half in range(2):
                    act_low(g * 2, 0, half)
                if not last:
                    split_L(u + 4, 1)
                for half in range(2):
                    product(g * 2 + 1, 1, half)
                    act_low(g * 2 + 1, 1, half)

            with dve.Fori(1, NG - 1) as g:
                group(g, False)
            group(NG - 1, True)
            dve.wait_ge(fw_in, 16)

            def finish(t):
                i = 2 * NT + t
                variance(i)
                dve.wait_ge(n_sd, i + 1)
                nc.vector.reciprocal(rstd[:, i:i + 1], sd[:, i:i + 1]).then_inc(n_rstd, 1)
                dve.wait_ge(n_rstd, i + 1)
                nc.vector.scalar_tensor_tensor(x2[:, t, :], x2[:, t, :], rstd[:, i:i + 1], fw[:], ALU.mult,
                                               ALU.mult).then_inc(f_out, 1)

            for t in range(NT):
                add_down(NG - 1, False, 2 * t, 2 * t + 2)
                dve.wait_ge(d_ev, 16 * (NG - 1) + 2 * t + 2)
                if t:
                    finish(t - 1)
            finish(NT - 1)

        @block.tensor
        def _(pe):
            def three(out_ap, lhs, rhs, k0, n, last):
                for i, (a, b) in enumerate(((0, 0), (0, 1), (1, 0))):
                    ins = nc.tensor.matmul(out_ap, lhs[a], rhs[b], start=(n == 0 and i == 0), stop=(last and i == 2))
                return ins

            def project(out_ap, lhs, rhs):
                for k in range(KD):
                    ins = three(out_ap, lhs(k), rhs(k), k, k, k == KD - 1)
                return ins

            def h_cols(half):
                return lambda k: tuple(h[:, k, half * HALF:(half + 1) * HALF] for h in (hH, hL))

            def h_tile(t):
                return lambda k: tuple(h[:, k, t * P:(t + 1) * P] for h in (hH, hL))

            pe.wait_ge(ones_ok, 1)
            for m, banks in ((0, OP), (1, (DC, AD))):
                pe.wait_ge(acc0_ok, KD * (m + 1))
                pe.wait_ge((bsc_in, bsh_in)[m], 16)
                b = (b_sc, b_sh)[m]
                for j in range(2):
                    nc.tensor.matmul(banks[j][:], ones[:], acc0[:, j * HALF:(j + 1) * HALF], start=True, stop=False)
                    nc.tensor.matmul(banks[j][:], ones[0:1, :], b[0:1, j * HALF:(j + 1) * HALF], start=False,
                                     stop=True).then_inc(mod0_mm, 1)

            def transposes(i, hn):
                pe.wait_ge(n_sh, i + 1)
                for j in range(2):
                    if i:
                        pe.wait_ge(n_L, 2 * (i - 1) + j + 1)
                    for k in range(4):
                        ins = nc.tensor.transpose(ST[j][:, k * P:(k + 1) * P],
                                                  hn[:, i % 2, (4 * j + k) * P:(4 * j + k + 1) * P], ident[:])
                    ins.then_inc(n_tr, 1)

            pe.wait_ge(const_ok, 2)
            for t in range(4):
                transposes(t, hn1)

            def gates(half):
                pe.wait_ge(wg_L, 1)
                pe.wait_ge(mod0_ev, 4)
                pe.wait_ge(n_L, 8 * (half + 1))
                wg = [w[:, 2, 0:KD * P].rearrange("p (k n) -> p k n", n=P) for w in (wH, wL)]
                project(OP[half][:], lambda k: tuple(w[:, k, :] for w in wg), h_cols(half)).then_inc(gates_mm, 1)

            def qk(h, i):
                ws = unit_weights(0, 2 * DK)
                m = i % 2
                project(QK_BANKS[i][:], lambda k: tuple(w[:, k, m * DK:(m + 1) * DK] for w in ws),
                        h_cols(i // 2)).then_inc(qk_mm, 1)

            def row_transposes():
                pe.wait_ge(g_dve, 7)
                for c in range(NT):
                    ins = nc.tensor.transpose(AD[:, c * GATE_ROWS:(c + 1) * GATE_ROWS],
                                              rows[0:GATE_ROWS, A_, c * P:(c + 1) * P],
                                              ident[0:GATE_ROWS, 0:GATE_ROWS])
                ins.then_inc(rT_mm, 1)

            def head(h, first):
                if first:
                    gates(0)
                    pe.wait_ge(w_L, 2)
                    qk(h, 0)
                    transposes(4, hn1)
                    transposes(5, hn1)
                    qk(h, 1)
                    transposes(6, hn1)
                    transposes(7, hn1)
                    gates(1)
                    qk(h, 2)
                else:
                    pe.wait_ge(w_L, h * 6 + 2)
                    pe.wait_ge(hc_ok, h * NT)
                    pe.wait_ge(kwpt, h * NT)
                    qk(h, 0)
                    qk(h, 1)
                    qk(h, 2)
                qk(h, 3)
                pe.wait_ge(w_L, h * 6 + 4)
                wv = unit_weights(1, DV)
                for t in range(NT):
                    if t >= 2:
                        pe.wait_ge(v_ev, h * NT + t - 1)
                    elif first:
                        pe.wait_ge(g_act, t + 1)
                    else:
                        pe.wait_ge(th_ok, h * NT - 1 + t)
                    project(OP[t % 2][:, 0:DV], h_tile(t),
                            lambda k: tuple(w[:, k, :] for w in wv)).then_inc(v_mm, 1)
                    if first and t == 3:
                        row_transposes()
                pe.wait_ge(qk_ev, h * 4 + 4)
                pe.wait_ge(v_ev, h * NT + NT)
                if first:
                    pe.wait_ge(v_one, 1)
                pe.wait_ge(w_L, h * 6 + 6)
                wo = unit_weights(2, DV)
                for c in range(NT):
                    n = h * NT + c
                    toks = slice(c * P, (c + 1) * P)
                    if c >= 2:
                        pe.wait_ge(kwpt, n - 1)
                    nc.tensor.matmul(ST[c % 2][:, 0:P], kT[:, toks], qT[:, toks], start=True, stop=True)
                    nc.tensor.transpose(ST[c % 2][:, P:2 * P], kT[:, toks], ident[:]).then_inc(st_mm, 1)
                    if c >= 2:
                        pe.wait_ge(th_ok, n - 1)
                    project(OP[c % 2][:, 0:DV], h_tile(c),
                            lambda k: tuple(w[:, k, :] for w in wo)).then_inc(op_mm, 1)
                    pe.wait_ge(kwpt, n + 1)
                    if c >= 2:
                        pe.wait_ge(hc_ok, n - 1)
                    if c:
                        pe.wait_ge(qs_ok, h * (NT - 1) + c)
                        pe.wait_ge(c_ok, h * (NT - 1) + c)
                        nc.tensor.matmul(O[c % 2][:, 0:DV + 1], qs[:, c % 2, :], C[:], start=True, stop=False)
                    nc.tensor.matmul(O[c % 2][:, 0:DV + 1], PT[:, c % 2, :], va[:, c, :], start=(c == 0),
                                     stop=True).then_inc(o_mm, 1)
                    if c < NT - 1:
                        nc.tensor.matmul(DC[:, 0:DV + 1], kw[:, c % 2, :], va[:, c, :], start=True,
                                         stop=True).then_inc(dc_mm, 1)
                    if c % 4 == 3:
                        half = c // 4
                        pe.wait_ge(acc_ok, h * 16 + 8 * half + 8)
                        pe.wait_ge(brow_in, h * 32 + 16 * half + 16)
                        if first and half == 0:
                            pe.wait_ge(rT_cp, 2)
                        else:
                            pe.wait_ge(ad_ev, h * 2 + half)
                        nc.tensor.matmul(AD[0:1, :], ones[:, 0:1], acc[:], start=True, stop=False)
                        nc.tensor.matmul(AD[0:1, :], ones[0:1, 0:1], brow[0:1, :], start=False,
                                         stop=True).then_inc(ad_mm, 1)

            head(0, True)
            with pe.Fori(1, NH) as h:
                head(h, False)

            def out_transposes(t):
                pe.wait_ge(og_n, t + 1)
                for j in range(2):
                    if t:
                        pe.wait_ge(og_L, 2 * t + j - 1)
                    elif j == 0:
                        pe.wait_ge(kwpt, NH * NT)
                    for k in range(4):
                        ins = nc.tensor.transpose(ST[j][:, k * P:(k + 1) * P],
                                                  hg[:, t, (4 * j + k) * P:(4 * j + k + 1) * P], ident[:])
                    ins.then_inc(og_tr, 1)

            def y_tile(n):
                j, t = divmod(n, NT)
                if t == 0:
                    pe.wait_ge(w_L, 2 * (U_OUT + j) + 2)
                if j == 0:
                    pe.wait_ge(og_L, 2 * t + 2)
                if n >= 4:
                    pe.wait_ge(y_g, n - 3)
                else:
                    pe.wait_ge((th_ok, th_ok, c_ok, ad_ev)[n], (NH * NT, NH * NT, NH * (NT - 1), 2 * NH)[n])
                ws = unit_weights(j % 3, DV)
                project(Y_BANKS[n % 4][:, 0:DV], h_tile(t), lambda k: tuple(w[:, k, :] for w in ws)).then_inc(y_mm, 1)

            out_transposes(0)
            out_transposes(1)
            for t in range(NT):
                y_tile(t)
                if t + 2 < NT:
                    out_transposes(t + 2)
            for n in range(NT, 3 * NT):
                y_tile(n)
            for t in range(NT):
                y_tile(3 * NT + t)
                if t >= 2:
                    transposes(NT + t - 2, hn2)

            def gate_up(f_count, k, between=(None, None)):
                ws = unit_weights(k, 2 * P)
                for half in range(2):
                    n = f_count * 2 + half
                    for m in range(2):
                        if half == 0 and between[m]:
                            between[m]()
                        if not isinstance(n, int) or n >= 2:
                            pe.wait_ge((sg_ok, st_ok)[m], n - 1)
                        if isinstance(n, int) and n < 2:
                            pe.wait_ge(n_L, 2 * NT + NT * (half + 1))
                        project(GU_BANKS[2 * half + m][:], lambda k: tuple(w[:, k, m * P:(m + 1) * P] for w in ws),
                                h_cols(half)).then_inc(gu_mm, 1)

            def down(g, k):
                pe.wait_ge(a_L, g * 4 + 4)
                ws = unit_weights(k, D)
                acts = (actH, actL)
                for n in range(16):
                    t, j = divmod(n, 2)
                    if isinstance(g, int) and g == 0 and n < 4:
                        pe.wait_ge(y_g, 4 * NT)
                    else:
                        pe.wait_ge(d_ev, g * 16 + n - 3)
                    for f in range(2):
                        ins = three(Y_BANKS[n % 4][:], tuple(a[:, f, t * P:(t + 1) * P] for a in acts),
                                    tuple(w[:, f, j * HALF:(j + 1) * HALF] for w in ws), f, f, f == 1)
                    ins.then_inc(d_mm, 1)

            pe.wait_ge(w_L, 2 * U_FF + 2)
            gate_up(0, 1, (lambda: transposes(2 * NT - 2, hn2), lambda: transposes(2 * NT - 1, hn2)))
            pe.wait_ge(w_L, 2 * U_FF + 4)
            gate_up(1, 2)

            def group(g):
                u = g * 3 + (U_FF - 1)
                pe.wait_ge(w_L, u * 2 + 2)
                gate_up(g * 2, 0)
                pe.wait_ge(w_L, u * 2 + 4)
                down(g - 1, 1)
                pe.wait_ge(w_L, u * 2 + 6)
                gate_up(g * 2 + 1, 2)

            group(1)
            with pe.Fori(2, NG) as g:
                group(g)
            pe.wait_ge(w_L, 2 * NU)
            down(NG - 1, 0)


def kernel(x, c, ada_w, ada_b, ml_w_in, ml_b_if, ml_norm_w, ml_w_out, gdn_w_in, gdn_conv_w, gdn_a_log, gdn_dt_bias,
           gdn_norm_w, gdn_w_out, ffn_w_gate_up, ffn_w_down, final_norm_w):
    import numpy as np
    import concourse.bacc as bacc
    from concourse.bass_utils import run_bass_kernel_spmd

    def tiled(w):
        return np.asarray(w).reshape(-1, P, w.shape[1]).transpose(1, 0, 2)

    w_in, w_out, gate_up, down = (np.asarray(a)[0] for a in (ml_w_in, ml_w_out, ffn_w_gate_up, ffn_w_down))
    units = []
    for h in range(NH):
        q, k = (w_in[:, n * NH * DK + h * DK:n * NH * DK + (h + 1) * DK] for n in range(2))
        v, o = (w_in[:, D * (n + 1) + h * DV:D * (n + 1) + (h + 1) * DV] for n in range(2))
        units += [np.concatenate([tiled(q), tiled(k)], 2), tiled(v), tiled(o)]
    units += [tiled(w_out[:, j * DV:(j + 1) * DV]) for j in range(4)]

    def gu(f):
        return np.concatenate([tiled(gate_up[:, n * DFF + f * P:n * DFF + (f + 1) * P]) for n in range(2)], 2)

    for g in range(NG):
        units.append(gu(2 * g))
        if g:
            units.append(tiled(down[(g - 1) * 2 * P:g * 2 * P]))
        units.append(gu(2 * g + 1))
    units.append(tiled(down[(NG - 1) * 2 * P:]))
    w_units = np.stack([u.reshape(P, UW) for u in units])

    gates = w_in[:, 3 * D:]
    pad = np.zeros((D, 32 - NH), gates.dtype)
    w_gates = np.ascontiguousarray(tiled(np.concatenate([gates[:, :NH], pad, gates[:, NH:]], 1)))
    mods = np.asarray(ada_w)[0].reshape(D, 6, D).transpose(1, 0, 2)
    first = np.stack([tiled(mods[m]) for m in (1, 0)])
    first = first.reshape(2, P, 2, 4, D).transpose(0, 2, 1, 3, 4)
    rest = np.stack([mods[m].reshape(KD, P, 2, HALF).transpose(2, 0, 1, 3) for m in range(2, 6)])
    b = np.asarray(ada_b)[0].reshape(6, D)
    arrays = {
        "x": np.asarray(x)[0].reshape(NT, P, D),
        "c_col": np.asarray(c)[0].reshape(KD, P).T,
        "ada_first": first,
        "ada_first_b": b[[1, 0]],
        "ada_rest": rest.reshape(8 * KD, P, HALF),
        "ada_rest_b": b[2:].reshape(8, HALF),
        "w_units": w_units,
        "w_gates": w_gates,
        "b_if": np.asarray(ml_b_if)[0].reshape(2 * NH, 1),
        "norm_w": np.asarray(ml_norm_w)[0].reshape(NH, DV),
        "final_w": np.asarray(final_norm_w).reshape(1, D),
    }
    arrays = {n: np.ascontiguousarray(a) for n, a in arrays.items()}
    nc = bacc.Bacc("TRN2", target_bir_lowering=False, num_devices=1)
    args = [nc.dram_tensor(n, a.shape, mybir.dt.from_np(a.dtype), kind="ExternalInput").ap()
            for n, a in arrays.items()]
    args.append(nc.dram_tensor("out", (NT, P, D), F32, kind="ExternalOutput").ap())
    args.append(nc.dram_tensor("scan_rows", (2, NH, S), F32, kind="Internal").ap())
    args.append(nc.dram_tensor("mod_rows", (8, HALF), F32, kind="Internal").ap())
    build(nc, *args)
    got = run_bass_kernel_spmd(nc, [arrays], core_ids=[0])
    return got.results[0]["out"].reshape(1, S, D)
```

```python
from contextlib import ExitStack

import concourse.bass as bass
from concourse import mybir

F32 = mybir.dt.float32
F32R = mybir.dt.float32r
ALU = mybir.AluOpType
ACT = mybir.ActivationFunctionType

P = 128
D = 1024
S = 1024
NT = S // P
KD = D // P
NH = 4
DK = 128
DV = 256
DFF = 2816
NF = DFF // P
NG = NF // 2
HALF = 512
UW = 2 * D
EPS = 1e-6
CAP = 15.0
MASKED = 1e30
U_HEAD = 3
U_OUT = U_HEAD * NH
U_FF = U_OUT + 4
NU = U_FF + 3 * NG
POOL_X = ()
GATE_ROWS = 36


def build(nc, x, c_col, ada_first, ada_first_b, ada_rest, ada_rest_b, w_units, w_gates, b_if, norm_w, final_w, out,
          scan_rows, mod_rows):
    with ExitStack() as ctx:
        base = (nc.sbuf_base + 63) // 64 * 64
        ctx.enter_context(nc.sbuf_tensor("arena", [P, (212800 - 64) // 4], F32))

        def at(name, shape, offset, dt=F32):
            return nc.alloc_sbuf_tensor_at(name, shape, dt, offset=base + offset)

        hH = at("hH", [P, KD, S], 0, F32R)
        hL = at("hL", [P, KD, S], 32768, F32R)
        xnT = at("xnT", [P, KD, S], 32768)
        wH = at("wH", [P, 3, UW], 65536, F32R)
        wL = at("wL", [P, 3, UW], 90112, F32R)
        raw = at("raw", [P, UW], 114688)
        G0 = 122880
        ada0 = at("ada0", [P, 4, KD, 2 * P], G0)
        rows = at("rows", [P, 8, S], G0)
        hg = at("hg", [P, NT, D], G0)
        sc2 = at("sc2", [P, D], G0)
        sh2 = at("sh2", [P, D], G0 + 4096)
        hn2 = at("hn2", [P, 2, D], G0 + 8192)
        stage = at("stage", [P, 2, S], G0)
        sg = at("sg", [P, 2, HALF], G0 + 8192)
        fw = at("fw", [P, D], G0 + 12288)
        actH = at("actH", [P, 2, S], G0 + 16384, F32R)
        actL = at("actL", [P, 2, S], G0 + 24576, F32R)
        X0 = G0 + 32768
        xin = at("xin", [P, NT, D], X0)
        qT = at("qT", [P, S], X0)
        kT = at("kT", [P, S], X0 + 4096)
        va = at("va", [P, NT, DV + 1], X0 + 8192)
        Mb = at("Mb", [P, S], X0 + 16416)
        sI = at("sI", [P, S], X0 + 20512)
        ada = at("ada", [P, 2, HALF], X0 + 24608)
        acc = at("acc", [P, HALF], X0 + 28704)
        x2 = at("x2", [P, NT, D], X0)
        gb = at("gb", [P, D], X0 + 32768)
        acc0 = at("acc0", [P, 2, 2 * P], X0 + 32768)
        b1 = at("b1", [P, 2 * KD], X0 + 34816)
        mod1 = at("mod1", [P, 2 * KD], X0 + 34880)
        wg_raw = at("wg_raw", [P, KD, GATE_ROWS], X0 + 35072)
        Z0 = X0 + 36864
        E = at("E", [P, 2, P], Z0)
        PT = at("PT", [P, 2, P], Z0 + 1024)
        kw = at("kw", [P, 2, P], Z0 + 2048)
        qs = at("qs", [P, 2, P], Z0 + 3072)
        junk = at("junk", [P, D], Z0)
        hc = at("hc", [P, 2, DV], Z0 + 4096)
        th = at("th", [P, 2, DV], Z0 + 6144)
        gate = at("gate", [P, 2, DV], Z0 + 8192)
        C = at("C", [P, DV + 1], Z0 + 10240)
        ident = at("ident", [P, P], Z0 + 11296)
        ones = at("ones", [P, P], Z0 + 11808)
        maskb = at("maskb", [P, P], Z0 + 12320)
        nwb = at("nwb", [P, DV], Z0 + 12832)
        brow = at("brow", [P, HALF], Z0 + 13856)
        adarow = at("adarow", [P, HALF], Z0 + 15904)
        Y0 = Z0 + 17952
        craw = at("craw", [P, KD], Y0)
        cact = at("cact", [P, KD], Y0 + 32)
        ms = at("ms", [P, 3 * NT], Y0 + 64)
        var = at("var", [P, 3 * NT], Y0 + 160)
        sd = at("sd", [P, 3 * NT], Y0 + 256)
        rstd = at("rstd", [P, 3 * NT], Y0 + 352)
        aT = at("aT", [P, NH * NT], Y0 + 448)
        tT = at("tT", [P, NH * NT], Y0 + 576)
        thr = at("thr", [P, NH * NT], Y0 + 704)
        hms = at("hms", [P, NH * NT], Y0 + 832)
        hvar = at("hvar", [P, NH * NT], Y0 + 960)
        hsd = at("hsd", [P, NH * NT], Y0 + 1088)
        hrs = at("hrs", [P, NH * NT], Y0 + 1216)
        den = at("den", [P, 2], Y0 + 1344)
        rden = at("rden", [P, 2], Y0 + 1376)
        bcol = at("bcol", [P, 1], Y0 + 1408)
        bcol15 = at("bcol15", [P, 1], Y0 + 1440)
        mp = at("mp", [P, NT], Y0 + 1472)
        sqj = at("sqj", [P, DV], Y0 + 1504, mybir.dt.bfloat16)
        tmp = at("tmp", [P, 2, DV], Z0 + 8192)

        T_, NL, NB, A_, DD, M_, SI, MR = range(8)

        def row(n, p0=0, p1=NH):
            return rows[p0:p1, n, :]

        ST = [ctx.enter_context(nc.psum_tensor(f"ST{i}", [P, HALF], F32)) for i in range(2)]
        O = [ctx.enter_context(nc.psum_tensor(f"O{i}", [P, HALF], F32)) for i in range(2)]
        OP = [ctx.enter_context(nc.psum_tensor(f"OP{i}", [P, HALF], F32)) for i in range(2)]
        DC = ctx.enter_context(nc.psum_tensor("DC", [P, HALF], F32))
        AD = ctx.enter_context(nc.psum_tensor("AD", [P, HALF], F32))
        QK_BANKS = [O[0], ST[0], ST[1], O[1]]
        Y_BANKS = [OP[0], OP[1], DC, AD]
        XT_BANKS = [ST[0], ST[1], O[0], O[1]]
        MOD_BANKS = [DC, AD]
        GU_BANKS = [O[0], O[1], ST[0], ST[1]]

        def sem(name):
            return ctx.enter_context(nc.semaphore(name))

        c_in, bif_in, wg_in, b1_in = sem("c_in"), sem("bif_in"), sem("wg_in"), sem("b1_in")
        ada0_in = [sem(f"ada0_in{i}") for i in range(4)]
        x_in = [sem(f"x_in{i}") for i in range(NT)]
        x2_in = [sem(f"x2_in{i}") for i in range(4)]
        raw_in = [sem(f"raw_in{i}") for i in range(2)]
        ada_in = [sem(f"ada_in{i}") for i in range(2)]
        brow_in, rows_out, bc_in, nw_in, mod_out = (sem("brow_in"), sem("rows_out"), sem("bc_in"), sem("nw_in"),
                                                     sem("mod_out"))
        sc2_in, sh2_in, g1_in, g2_in, fw_in = sem("sc2_in"), sem("sh2_in"), sem("g1_in"), sem("g2_in"), sem("fw_in")
        out_done = sem("out_done")
        const_0, const_ok, ones_ok, rows_set = sem("const_0"), sem("const_ok"), sem("ones_ok"), sem("rows_set")
        c_act = sem("c_act")
        b1_ok, acc0_ok, mod1_mm, mod1_ok = sem("b1_ok"), sem("acc0_ok"), sem("mod1_mm"), sem("mod1_ok")
        xT_ok = [sem(f"xT_ok{j}") for j in range(2)]
        n_hnp = sem("norm_scaled_pool")
        m_x, m_H, m_L, sc2_ok = sem("modulated"), sem("modulated_H"), sem("modulated_L"), sem("sc2_ok")
        n_ms, n_var, n_sd, n_rstd, n_hn, n_sh, n_tr, n_H, n_L = (
            sem(f"norm_{s}") for s in ("ms", "var", "sd", "rstd", "scaled", "shifted", "transposed", "H", "L"))
        w_H, w_L, w_scaled = sem("w_H"), sem("w_L"), sem("w_scaled")
        wg_zero, wg_H, wg_L, gates_mm = sem("wg_zero"), sem("wg_H"), sem("wg_L"), sem("gates_mm")
        b15_ok, g_act, g_dve, rT_mm, rT_cp, thr_ok = (sem("b15_ok"), sem("g_act"), sem("g_dve"), sem("rT_mm"),
                                                      sem("rT_cp"), sem("thr_ok"))
        qk_mm, qk_ev, v_mm, v_ev, v_one = sem("qk_mm"), sem("qk_ev"), sem("v_mm"), sem("v_ev"), sem("v_one")
        masked, e_ok, st_mm, kwpt, qs_ok = sem("masked"), sem("e_ok"), sem("st_mm"), sem("kwpt"), sem("qs_ok")
        op_mm, th_ok, gate_ok = sem("op_mm"), sem("th_ok"), sem("gate_ok")
        o_mm, dc_mm, c_ok = sem("o_mm"), sem("dc_mm"), sem("c_ok")
        den_ok, rden_ok, hc_ok, hms_ok, hg_ok = sem("den_ok"), sem("rden_ok"), sem("hc_ok"), sem("hms_ok"), sem("hg_ok")
        acc_ok, ad_mm, ad_ev = sem("acc_ok"), sem("ad_mm"), sem("ad_ev")
        h_var, h_sd, h_rs = sem("h_var"), sem("h_sd"), sem("h_rs")
        og_n = [sem(f"og_n{i}") for i in range(2)]
        og_tr, og_H, og_L = sem("og_tr"), sem("og_H"), sem("og_L")
        y_mm, y_g, y_ev = sem("y_mm"), sem("y_g"), sem("y_ev")
        gu_mm, sg_ok, st_ok, a_H, a_L = sem("gu_mm"), sem("sg_ok"), sem("st_ok"), sem("a_H"), sem("a_L")
        d_mm, d_ev, f_out = sem("d_mm"), sem("d_ev"), sem("f_out")

        def slot(k):
            return k % 3

        def unit_weights(k, width):
            return tuple(w[:, slot(k), :].rearrange("p (k n) -> p k n", n=width) for w in (wH, wL))

        def piece(t, i):
            return t[:, i * D:(i + 1) * D]

        def og_banks(t):
            return (O[0], DC) if t == 0 else (ST, O)[1 - t % 2]

        def four(v, t0):
            return v[:].rearrange("p (h t) -> p h t", t=NT)[:, :, t0:t0 + 4]

        block = ctx.enter_context(nc.Block())

        @block.sync
        def _(sp):
            def load_unit(u, pieces=(0, 1)):
                for i in pieces:
                    if not (isinstance(u, int) and u == 0):
                        sp.wait_ge(w_L, u * 2 - 1 + i)
                    src = w_units[u, i] if isinstance(u, int) else \
                        w_units[bass.ds(u, 1), i].rearrange("a p n -> (a p) n")
                    sp.dma_start(piece(raw, i), src).then_inc(raw_in[i], 16)

            sp.dma_start(craw[:], c_col).then_inc(c_in, 16)
            def ada_first_tile(k):
                if k >= 4:
                    sp.wait_ge(acc0_ok, KD * (k - 3))
                sp.dma_start(ada0[:, k % 4], ada_first[k]).then_inc(ada0_in[k % 4], 16)

            for t in range(NT):
                sp.dma_start(xin[:, t, :], x[t]).then_inc(x_in[t], 16)
                if t == 0:
                    sp.dma_start(b1[:], ada_first_b).then_inc(b1_in, 16)
                if t == 5:
                    ada_first_tile(0)
            load_unit(0)
            sp.dma_start(wg_raw[:], w_gates).then_inc(wg_in, 16)
            for k in range(1, KD):
                ada_first_tile(k)
            load_unit(1)
            load_unit(2)

            def ada_item(h, i, first):
                if not (first and i < 2):
                    sp.wait_ge(acc_ok, h * 16 + i - 1)
                sp.dma_start(ada[:, i % 2, :],
                               ada_rest[bass.ds(h * 16 + i, 1), :, :].rearrange("a p n -> (a p) n")
                               if not first else ada_rest[i]).then_inc(ada_in[i % 2], 16)

            def mod_store(n):
                sp.wait_ge(ad_ev, n + 1)
                sp.dma_start(mod_rows[bass.ds(n, 1), :] if not isinstance(n, int) else mod_rows[n:n + 1, :],
                             adarow[0:1, :]).then_inc(mod_out, 16)

            def ada_bias(h, half, first):
                if not (first and half == 0):
                    mod_store(h * 2 + half - 1)
                sp.dma_start(brow[0:1, :], ada_rest_b[bass.ds(h * 2 + half, 1), :] if not first
                               else ada_rest_b[half:half + 1, :]).then_inc(brow_in, 16)

            def head(h, first):
                load_unit(h * 3 + 3)
                if first:
                    sp.wait_ge(rows_out, 32)
                    m_src, s_src, n_src = scan_rows[0, 0:1, :], scan_rows[1, 0:1, :], norm_w[0:1, :]
                else:
                    sp.wait_ge(gate_ok, h * NT)
                    m_src, s_src = (scan_rows[i, bass.ds(h, 1), :] for i in range(2))
                    n_src = norm_w[bass.ds(h, 1), :]
                sp.dma_start(Mb[:], m_src.to_broadcast([P, S])).then_inc(bc_in, 16)
                sp.dma_start(sI[:], s_src.to_broadcast([P, S])).then_inc(bc_in, 16)
                sp.dma_start(nwb[:], n_src.to_broadcast([P, DV])).then_inc(nw_in, 16)
                ada_bias(h, 0, first)
                ada_item(h, 0, first)
                ada_item(h, 1, first)
                for i in range(2, 16):
                    if i in (2, 4):
                        load_unit(h * 3 + 4, (i // 2 - 1,))
                    ada_item(h, i, first)
                    if i in (7, 11):
                        load_unit(h * 3 + 5, (i // 4 - 1,))
                    if i == 12:
                        ada_bias(h, 1, first)

            head(0, True)
            with sp.Fori(1, NH) as h:
                head(h, False)
            sp.wait_ge(o_mm, NT * NH)
            sp.wait_ge(dc_mm, (NT - 1) * NH)
            sp.wait_ge(c_ok, (NT - 1) * NH)
            sp.wait_ge(e_ok, NT * NH)
            sp.wait_ge(kwpt, NT * NH)
            sp.wait_ge(qs_ok, (NT - 1) * NH)
            sp.wait_ge(ad_mm, 2 * NH)
            for i in range(4):
                sp.dma_start(x2[:, 2 * i:2 * i + 2, :],
                             x[2 * i:2 * i + 2].rearrange("t p n -> p t n")).then_inc(x2_in[i], 16)
            mod_store(2 * NH - 1)
            with sp.Fori(U_OUT + 3, NU) as u:
                load_unit(u)
            for t in range(NT):
                sp.wait_ge(f_out, t + 1)
                sp.dma_start(out[t], x2[:, t, :]).then_inc(out_done, 16)
            sp.wait_ge(out_done, 16 * NT)

        @block.gpsimd
        def _(pool):
            nc.gpsimd.memset(ones[:], 1.0).then_inc(ones_ok, 1)
            nc.gpsimd.memset(ident[:], 0.0).then_inc(const_0, 1)
            nc.gpsimd.memset(maskb[:], 0.0).then_inc(const_0, 1)
            nc.gpsimd.memset(bcol[:], 0.0).then_inc(const_0, 1)
            pool.wait_ge(const_0, 3)
            nc.gpsimd.affine_select(out=ident[:], in_=ident[:], compare_op=ALU.not_equal, fill=1.0, base=0,
                                    pattern=[[-1, P]], channel_multiplier=1).then_inc(const_ok, 1)
            nc.gpsimd.affine_select(out=maskb[:], in_=maskb[:], compare_op=ALU.is_ge, fill=MASKED, base=0,
                                    pattern=[[1, P]], channel_multiplier=-1).then_inc(const_ok, 1)
            pool.dma_start(bcol[0:NH, :], b_if[0:NH, :]).then_inc(bif_in, 16)
            pool.dma_start(bcol[32:32 + NH, :], b_if[NH:2 * NH, :]).then_inc(bif_in, 16)

            for t in POOL_X:
                pool.wait_ge(n_rstd, t + 1)
                nc.gpsimd.tensor_scalar(xin[:, t, :], xin[:, t, :], rstd[:, t:t + 1], None,
                                        ALU.mult).then_inc(n_hnp, 1)
            pool.wait_ge(wg_in, 16)
            pool.wait_ge(wg_zero, 2)
            wgH, wgL = (w[:, 2, 0:KD * P].rearrange("p (k n) -> p k n", n=P)[:, :, 0:GATE_ROWS] for w in (wH, wL))
            nc.gpsimd.tensor_copy(wgH, wg_raw[:]).then_inc(wg_H, 1)
            pool.wait_ge(wg_H, 1)
            nc.gpsimd.tensor_tensor(wgL, wg_raw[:], wgH.bitcast(F32), ALU.subtract).then_inc(wg_L, 1)
            for k in range(1, KD):
                for half in range(2):
                    cols = slice(half * HALF, (half + 1) * HALF)
                    pool.wait_ge(m_H, 2 * k + half + 1)
                    if k == 1 and half == 0:
                        pool.wait_ge(m_L, 2)
                    nc.gpsimd.tensor_tensor(hL[:, k, cols], xnT[:, k, cols], hH[:, k, cols].bitcast(F32),
                                            ALU.subtract).then_inc(m_L, 1)
            pool.wait_ge(acc0_ok, KD * KD)
            nc.gpsimd.memset(rows[0:GATE_ROWS, A_, :], 0.0).then_inc(rows_set, 1)
            nc.gpsimd.memset(row(DD), 0.0).then_inc(rows_set, 1)
            nc.gpsimd.memset(row(MR), 1.0).then_inc(rows_set, 1)
            pool.wait_ge(rows_set, 3)
            nc.gpsimd.memset(rows[0:NH, MR, 0:S:P], 0.0).then_inc(rows_set, 1)

            def head_norm(t):
                pool.wait_ge(h_rs, 2 * (t // 4) + 2)
                pool.wait_ge(hg_ok, (NH - 1) * NT + t + 1)
                hv = hg[:, t, :].rearrange("p (h v) -> p h v", h=NH)
                rs = hrs[:].rearrange("p (h t) -> p t h", t=NT)[:, t, :]
                nc.gpsimd.tensor_tensor(hv, hv, rs.unsqueeze(2).to_broadcast([P, NH, DV]),
                                        ALU.mult).then_inc(og_n[1], 1)

            def head(h, first, last=False):
                if first:
                    pool.wait_ge(g_act, 5)
                    pool.dma_start(scan_rows[1], row(SI)).then_inc(rows_out, 16)
                    pool.dma_start(scan_rows[0], row(M_)).then_inc(rows_out, 16)
                pool.wait_ge(bc_in, h * 32 + 32)
                mv = Mb[:].rearrange("p (c l) -> p c l", l=P)
                nc.gpsimd.tensor_tensor(mv, mv, maskb[:].unsqueeze(1).to_broadcast([P, NT, P]),
                                        ALU.add).then_inc(masked, 1)
                pool.wait_ge(qk_ev, h * 4 + 4)
                for c in range(NT + 1):
                    if 1 <= c < NT:
                        if c >= 2:
                            pool.wait_ge(o_mm, h * NT + c - 1)
                        elif not first:
                            pool.wait_ge(o_mm, h * NT)
                        nc.gpsimd.tensor_tensor(qs[:, c % 2, :], qT[:, c * P:(c + 1) * P],
                                                sI[:, c * P:(c + 1) * P], ALU.mult).then_inc(qs_ok, 1)
                    if last and c == 7:
                        head_norm(0)
                    if 1 <= c:
                        pool.wait_ge(hc_ok, h * NT + c)
                        pool.wait_ge(gate_ok, h * NT + c)
                        dst = (hg[:, c - 1, 0:DV] if first else hg[:, c - 1, bass.ds(h * DV, DV)])
                        nc.gpsimd.tensor_tensor(dst, hc[:, (c - 1) % 2, :], gate[:, (c - 1) % 2, :],
                                                ALU.mult).then_inc(hg_ok, 1)
                    if last and c == 7:
                        head_norm(1)

            head(0, True)
            with pool.Fori(1, NH - 1) as h:
                head(h, False)
            head(NH - 1, False, True)

            pool.wait_ge(mod_out, 16 * 2)
            pool.dma_start(gb[:], mod_rows[0:2, :].rearrange("(o a) n -> o (a n)", o=1).to_broadcast([P, D])).then_inc(g1_in, 16)
            for t in range(3, NT, 2):
                head_norm(t)
            pool.wait_ge(mod_out, 16 * 2 * NH)
            pool.wait_ge(og_tr, 2 * NT)
            pool.dma_start(sh2[:], mod_rows[2:4, :].rearrange("(o a) n -> o (a n)", o=1).to_broadcast([P, D])).then_inc(sh2_in, 16)
            pool.dma_start(sc2[:], mod_rows[4:6, :].rearrange("(o a) n -> o (a n)", o=1).to_broadcast([P, D])).then_inc(sc2_in, 16)
            pool.wait_ge(sh2_in, 16)
            for t in range(NT):
                pool.wait_ge(n_hn, NT - len(POOL_X) + t + 1)
                nc.gpsimd.tensor_tensor(hn2[:, t % 2, :], hn2[:, t % 2, :], sh2[:], ALU.add).then_inc(n_sh, 1)
            pool.wait_ge(n_tr, 4 * NT)
            pool.dma_start(fw[:], final_w.to_broadcast([P, D])).then_inc(fw_in, 16)
            pool.wait_ge(y_g, 4 * NT)
            pool.dma_start(gb[:], mod_rows[6:8, :].rearrange("(o a) n -> o (a n)", o=1).to_broadcast([P, D])).then_inc(g2_in, 16)
            pool.wait_ge(g2_in, 16)

            def scale_down(u, g):
                for i in range(2):
                    pool.wait_ge(raw_in[i], u * 16 + 16)
                    nc.gpsimd.tensor_tensor(piece(raw, i), piece(raw, i), gb[:], ALU.mult).then_inc(w_scaled, 1)

            scale_down(U_FF + 3, 0)
            with pool.Fori(1, NG - 1) as g:
                scale_down(g * 3 + U_FF + 3, g)
            scale_down(NU - 1, NG - 1)

        @block.scalar
        def _(act):
            def split_H(u, k, free=None, pieces=(0, 1), down=None):
                for i in pieces:
                    act.wait_ge(raw_in[i], u * 16 + 16)
                    if down is not None:
                        act.wait_ge(w_scaled, down * 2 - 1 + i)
                    if i == 0 and free is not None:
                        act.wait_ge(*free)
                    nc.scalar.copy(piece(wH[:, slot(k), :], i), piece(raw, i)).then_inc(w_H, 1)

            act.wait_ge(c_in, 16)
            nc.scalar.activation(cact[:], craw[:], ACT.Silu).then_inc(c_act, 1)

            def square(i, src):
                nc.scalar.activation(junk[:], src, ACT.Square, accum_out=ms[:, i:i + 1]).then_inc(n_ms, 1)

            def root(i):
                act.wait_ge(n_var, i + 1)
                nc.scalar.activation(sd[:, i:i + 1], var[:, i:i + 1], ACT.Sqrt).then_inc(n_sd, 1)

            def evac_xT(t, j):
                act.wait_ge(n_tr, 2 * t + j + 1)
                nc.scalar.copy(xnT[:, 4 * j:4 * j + 4, t * P:(t + 1) * P],
                               XT_BANKS[2 * (t % 2) + j][:].rearrange("p (k n) -> p k n", n=P)).then_inc(xT_ok[j], 1)

            for t in range(NT):
                act.wait_ge(x_in[t], 16)
                if t:
                    act.wait_ge(n_ms, t)
                square(t, xin[:, t, :])
                if t:
                    root(t - 1)
                if t >= 2:
                    evac_xT(t - 2, 0)
            root(NT - 1)
            act.wait_ge(xT_ok[1], NT - 2)
            for t in range(NT - 2, NT):
                for j in range(2):
                    evac_xT(t, j)
            split_H(0, 0, pieces=(0,))
            for k in range(KD):
                act.wait_ge(mod1_ok, k + 1)
                if k == 0:
                    act.wait_ge(xT_ok[0], NT)
                elif k == 4:
                    act.wait_ge(xT_ok[1], NT)
                for half in range(2):
                    v = xnT[:, k, half * HALF:(half + 1) * HALF]
                    nc.scalar.activation(v, v, ACT.Identity, scale=mod1[:, 2 * k:2 * k + 1],
                                         bias=mod1[:, 2 * k + 1:2 * k + 2]).then_inc(m_x, 1)
                for half in range(2):
                    cols = slice(half * HALF, (half + 1) * HALF)
                    act.wait_ge(m_x, 2 * k + half + 1)
                    nc.scalar.copy(hH[:, k, cols], xnT[:, k, cols]).then_inc(m_H, 1)
                if k == 0:
                    split_H(0, 0, pieces=(1,))
            split_H(1, 1)

            def evac_qk(h, i):
                act.wait_ge(qk_mm, h * 4 + i + 1)
                dst = (qT if i % 2 == 0 else kT)[:, (i // 2) * HALF:(i // 2 + 1) * HALF]
                nc.scalar.activation(dst, QK_BANKS[i][:], ACT.Copy,
                                     scale=1.0 if i % 2 == 0 else float(DK) ** -0.5).then_inc(qk_ev, 1)

            def gates_scalar():
                act.wait_ge(b15_ok, 1)
                for j in range(2):
                    act.wait_ge(gates_mm, j + 1)
                    nc.scalar.activation(rows[0:GATE_ROWS, T_, j * HALF:(j + 1) * HALF], OP[j][0:GATE_ROWS, :],
                                         ACT.Tanh, bias=bcol15[0:GATE_ROWS, :], scale=1.0 / CAP).then_inc(g_act, 1)
                act.wait_ge(g_act, 2)
                nc.scalar.activation(row(NL), row(T_, 32, 32 + NH), ACT.Exp, scale=-CAP).then_inc(g_act, 1)
                act.wait_ge(g_act, 3)
                nc.scalar.activation(row(NL), row(NL), ACT.Ln, bias=1.0).then_inc(g_act, 1)

            def head_root(b):
                act.wait_ge(h_var, b + 1)
                nc.scalar.activation(four(hsd, 4 * b), four(hvar, 4 * b), ACT.Sqrt).then_inc(h_sd, 1)

            def og_high(t):
                for j in range(2):
                    act.wait_ge(og_tr, 2 * t + j + 1)
                    nc.scalar.copy(hH[:, 4 * j:4 * j + 4, t * P:(t + 1) * P],
                                   og_banks(t)[j][:].rearrange("p (k n) -> p k n", n=P)).then_inc(og_H, 1)

            def head(h, first, last=False):
                if first:
                    gates_scalar()
                else:
                    for i in range(4):
                        if i == 0:
                            act.wait_ge(o_mm, h * NT)
                            act.wait_ge(st_mm, h * NT)
                            act.wait_ge(qs_ok, h * (NT - 1))
                        evac_qk(h, i)
                        if i == 0:
                            split_H(h * 3 + 2, 2, (op_mm, h * NT))
                for t in range(NT):
                    act.wait_ge(v_mm, h * NT + t + 1)
                    nc.scalar.copy(va[:, t, 0:DV], OP[t % 2][:, 0:DV]).then_inc(v_ev, 1)
                    if first and t < 4:
                        evac_qk(h, t)
                    if first and t == 2:
                        act.wait_ge(g_dve, 6)
                        nc.scalar.activation(row(SI), row(SI), ACT.Exp).then_inc(g_act, 1)
                    if t == (NT - 1 if first else 1):
                        split_H(h * 3 + 3, 0, (qk_mm, h * 4 + 4))
                    if t == 3 and first:
                        split_H(2, 2, (gates_mm, 2))
                    if t == 5 and first:
                        act.wait_ge(rT_cp, 2)
                        nc.scalar.activation(thr[:], tT[:], ACT.Exp).then_inc(thr_ok, 1)
                act.wait_ge(masked, h + 1)

                def decay(c):
                    if c >= 2:
                        act.wait_ge(kwpt, h * NT + c - 1)
                    elif not first:
                        act.wait_ge(kwpt, h * NT)
                    col = aT[:, c:c + 1] if first else aT[:, bass.ds(h * NT + c, 1)]
                    nc.scalar.activation(E[:, c % 2, :], Mb[:, c * P:(c + 1) * P], ACT.Exp, scale=-1.0,
                                         bias=col).then_inc(e_ok, 1)

                def squares(c):
                    act.wait_ge(hc_ok, h * NT + c + 1)
                    if not (first and c == 0):
                        act.wait_ge(hms_ok, h * NT + c)
                    col = hms[:, c:c + 1] if first else hms[:, bass.ds(h * NT + c, 1)]
                    nc.scalar.activation(sqj[:], hc[:, c % 2, :], ACT.Square, accum_out=col).then_inc(hms_ok, 1)

                decay(0)
                for c in range(NT):
                    if c + 1 < NT:
                        decay(c + 1)
                    act.wait_ge(op_mm, h * NT + c + 1)
                    if c >= 2:
                        act.wait_ge(gate_ok, h * NT + c - 1)
                    elif not first:
                        act.wait_ge(gate_ok, h * NT)
                    nc.scalar.activation(th[:, c % 2, :], OP[c % 2][:, 0:DV], ACT.Tanh, scale=0.5).then_inc(th_ok, 1)
                    if c in (1, 3):
                        split_H(h * 3 + 4, 1, (v_mm, h * NT + NT), pieces=(c // 2,))
                    if c:
                        squares(c - 1)
                    if last and c == 5:
                        head_root(0)
                if last:
                    og_high(0)
                squares(NT - 1)

            head(0, True)
            with act.Fori(1, NH - 1) as h:
                head(h, False)
            head(NH - 1, False, True)

            head_root(1)
            for t in range(1, NT):
                og_high(t)
                if t == 4:
                    split_H(U_OUT + 2, 2, (op_mm, NH * NT))
            split_H(U_OUT + 3, 0, (y_mm, NT))
            split_H(U_FF, 1, (y_mm, 2 * NT))
            split_H(U_FF + 1, 2, (y_mm, 3 * NT))

            def square_x2(t):
                act.wait_ge(y_ev, 3 * NT + t + 1)
                act.wait_ge(n_ms, NT + t)
                square(NT + t, x2[:, t, :])
                root(NT + t)

            square_x2(0)
            for t in range(NT):
                if t + 1 < NT:
                    square_x2(t + 1)
                for j in range(2):
                    act.wait_ge(n_tr, 2 * (NT + t) + j + 1)
                    nc.scalar.copy(hH[:, 4 * j:4 * j + 4, t * P:(t + 1) * P],
                                   ST[j][:].rearrange("p (k n) -> p k n", n=P)).then_inc(n_H, 1)

            def silu(f_count, half):
                n = f_count * 2 + half
                act.wait_ge(gu_mm, n * 2 + 1)
                if not isinstance(n, int) or n >= 2:
                    act.wait_ge(st_ok, n - 1)
                nc.scalar.activation(sg[:, half, :], GU_BANKS[2 * half][:], ACT.Silu).then_inc(sg_ok, 1)

            def act_high(f_count, f, half):
                n = f_count * 2 + half
                act.wait_ge(st_ok, n + 1)
                nc.scalar.copy(actH[:, f, half * HALF:(half + 1) * HALF],
                               stage[:, f, half * HALF:(half + 1) * HALF]).then_inc(a_H, 1)

            act.wait_ge(n_sh, NT)
            split_H(U_FF + 2, 0, (y_mm, 4 * NT))
            for half in range(2):
                silu(0, half)
                act_high(0, 0, half)
            split_H(U_FF + 3, 1, (gu_mm, 4), down=1)
            for half in range(2):
                silu(1, half)
                act_high(1, 1, half)

            def group(g, last):
                u = g * 3 + (U_FF - 1)
                split_H(u + 2, 2, (gu_mm, g * 8))
                for half in range(2):
                    silu(g * 2, half)
                split_H(u + 3, 0, (gu_mm, g * 8 + 4), down=NG if last else None)
                act.wait_ge(d_mm, g * 16)
                for half in range(2):
                    act_high(g * 2, 0, half)
                if not last:
                    split_H(u + 4, 1, (d_mm, g * 16), down=g + 1)
                for half in range(2):
                    silu(g * 2 + 1, half)
                    act_high(g * 2 + 1, 1, half)

            with act.Fori(1, NG - 1) as g:
                group(g, False)
            group(NG - 1, True)
            for t in range(NT):
                i = 2 * NT + t
                act.wait_ge(d_ev, 16 * (NG - 1) + 2 * t + 2)
                act.wait_ge(n_ms, i)
                square(i, x2[:, t, :])
                root(i)

        @block.vector
        def _(dve):
            def split_L(u, k, pieces=(0, 1)):
                for i in pieces:
                    dve.wait_ge(w_H, u * 2 + i + 1)
                    nc.vector.tensor_tensor(piece(wL[:, slot(k), :], i), piece(raw, i),
                                            piece(wH[:, slot(k), :], i).bitcast(F32), ALU.subtract).then_inc(w_L, 1)

            for w in (wH, wL):
                nc.vector.memset(w[:, 2, 0:KD * P].bitcast(F32), 0.0).then_inc(wg_zero, 1)

            def sum1(k, r0, r1):
                for r in range(r0, r1):
                    if r == 0:
                        dve.wait_ge(ada0_in[k % 4], 16 * (k // 4 + 1))
                        if k >= 2:
                            dve.wait_ge(mod1_mm, k - 1)
                        nc.vector.tensor_scalar(acc0[:, k % 2, :], ada0[:, k % 4, 0, :], cact[:, 0:1], None,
                                                ALU.mult).then_inc(acc0_ok, 1)
                    else:
                        dve.wait_ge(acc0_ok, k * KD + r)
                        nc.vector.scalar_tensor_tensor(acc0[:, k % 2, :], ada0[:, k % 4, r, :], cact[:, r:r + 1],
                                                       acc0[:, k % 2, :], ALU.mult, ALU.add).then_inc(acc0_ok, 1)

            def mod_column(k):
                dve.wait_ge(mod1_mm, k + 1)
                if k == 0:
                    dve.wait_ge(b1_ok, 1)
                cols = slice(2 * k, 2 * k + 2)
                nc.vector.tensor_tensor(mod1[:, cols], MOD_BANKS[k % 2][:, cols], b1[:, cols],
                                        ALU.add).then_inc(mod1_ok, 1)

            def variance(i):
                dve.wait_ge(n_ms, i + 1)
                nc.vector.tensor_scalar(var[:, i:i + 1], ms[:, i:i + 1], 1.0 / D, EPS, ALU.mult,
                                        ALU.add).then_inc(n_var, 1)

            def inverse(i):
                dve.wait_ge(n_sd, i + 1)
                nc.vector.reciprocal(rstd[:, i:i + 1], sd[:, i:i + 1]).then_inc(n_rstd, 1)
                dve.wait_ge(n_rstd, i + 1)

            def low(t):
                for j in range(2):
                    dve.wait_ge(n_H, 2 * t + j + 1)
                    cols = slice(t * P, (t + 1) * P)
                    nc.vector.tensor_tensor(hL[:, 4 * j:4 * j + 4, cols], ST[j][:].rearrange("p (k n) -> p k n", n=P),
                                            hH[:, 4 * j:4 * j + 4, cols].bitcast(F32), ALU.subtract).then_inc(n_L, 1)

            def norm1(t):
                inverse(t)
                if t not in POOL_X:
                    nc.vector.tensor_scalar(xin[:, t, :], xin[:, t, :], rstd[:, t:t + 1], None,
                                            ALU.mult).then_inc(n_hn, 1)

            def evac_xT(t):
                dve.wait_ge(n_tr, 2 * t + 2)
                nc.vector.tensor_copy(xnT[:, 4:8, t * P:(t + 1) * P],
                                      XT_BANKS[2 * (t % 2) + 1][:].rearrange("p (k n) -> p k n",
                                                                             n=P)).then_inc(xT_ok[1], 1)

            def low1(k, half):
                cols = slice(half * HALF, (half + 1) * HALF)
                dve.wait_ge(m_H, 2 * k + half + 1)
                nc.vector.tensor_tensor(hL[:, k, cols], xnT[:, k, cols], hH[:, k, cols].bitcast(F32),
                                        ALU.subtract).then_inc(m_L, 1)

            for t in range(NT + 1):
                if t < NT:
                    variance(t)
                if t:
                    norm1(t - 1)
                if t >= 3:
                    evac_xT(t - 3)
                if t == NT - 1:
                    dve.wait_ge(b1_in, 16)
                    b1_scale = b1[:].rearrange("p (k m) -> p k m", m=2)[:, :, 0:1]
                    nc.vector.tensor_scalar(b1_scale, b1_scale, 1.0, None, ALU.add).then_inc(b1_ok, 1)
                    dve.wait_ge(c_act, 1)
                    sum1(0, 0, 2)
            sum1(0, 2, KD)
            mod_column(0)
            split_L(0, 0, pieces=(0,))
            sum1(1, 0, 2)
            low1(0, 0)
            low1(0, 1)
            sum1(1, 2, KD)
            mod_column(1)
            sum1(2, 0, KD)
            mod_column(2)
            sum1(3, 0, KD)
            split_L(0, 0, pieces=(1,))
            sum1(4, 0, 4)
            mod_column(3)
            sum1(4, 4, KD)
            sum1(5, 0, KD)
            for k in range(4, KD):
                mod_column(k)
                if k + 2 < KD:
                    sum1(k + 2, 0, KD)
            dve.wait_ge(bif_in, 32)
            nc.vector.tensor_scalar(bcol15[:], bcol[:], 1.0 / CAP, None, ALU.mult).then_inc(b15_ok, 1)
            split_L(1, 1)

            def gates_rows():
                dve.wait_ge(g_act, 4)
                dve.wait_ge(rows_set, 4)
                nc.vector.tensor_tensor_scan(row(NB), row(MR), row(NL), 0.0, ALU.mult, ALU.add).then_inc(g_dve, 1)
                dve.wait_ge(g_dve, 1)
                nc.vector.scalar_tensor_tensor(row(A_), row(T_), CAP, row(NB), ALU.mult, ALU.add).then_inc(g_dve, 1)
                nc.vector.tensor_scalar(rows[0:NH, DD, P:S:P], rows[0:NH, NB, P - 1:S - 1:P], -1.0, None,
                                        ALU.mult).then_inc(g_dve, 1)
                dve.wait_ge(g_dve, 3)
                nc.vector.tensor_tensor_scan(row(M_), row(DD), row(A_), 0.0, ALU.add, ALU.max).then_inc(g_dve, 1)
                nc.vector.memset(mp[0:NH, 0:1], 0.0).then_inc(g_dve, 1)
                dve.wait_ge(g_dve, 5)
                nc.vector.tensor_tensor(mp[0:NH, 1:NT], rows[0:NH, M_, P - 1:S - 1:P], rows[0:NH, DD, P:S:P],
                                        ALU.add).then_inc(rT_cp, 1)
                dve.wait_ge(rT_cp, 1)
                nc.vector.tensor_tensor(row(SI).rearrange("p (c l) -> p c l", l=P),
                                        mp[0:NH, :].unsqueeze(2).to_broadcast([NH, NT, P]),
                                        row(M_).rearrange("p (c l) -> p c l", l=P), ALU.subtract).then_inc(g_dve, 1)
                nc.vector.tensor_tensor(row(A_, 32, 32 + NH), row(NB), row(M_), ALU.subtract).then_inc(g_dve, 1)

            def gates_columns():
                dve.wait_ge(rT_mm, 1)
                for n, t in enumerate((aT, tT)):
                    ins = nc.vector.tensor_copy(t[:].rearrange("p (h c) -> p c h", h=NH),
                                                AD[:, 0:NT * GATE_ROWS].rearrange("p (c r) -> p c r", r=GATE_ROWS)
                                                [:, :, 32 * n:32 * n + NH])
                ins.then_inc(rT_cp, 1)

            def mod_row(n):
                dve.wait_ge(ad_mm, n + 1)
                if not (isinstance(n, int) and n == 0):
                    dve.wait_ge(mod_out, n * 16)
                nc.vector.tensor_copy(adarow[0:1, :], AD[0:1, :]).then_inc(ad_ev, 1)

            def head_var(b):
                dve.wait_ge(hms_ok, (NH - 1) * NT + 4 * b + 4)
                nc.vector.tensor_scalar(four(hvar, 4 * b), four(hms, 4 * b), 1.0 / DV, EPS, ALU.mult,
                                        ALU.add).then_inc(h_var, 1)

            def head_rstd(b):
                dve.wait_ge(h_sd, b + 1)
                nc.vector.reciprocal(four(hsd, 4 * b), four(hsd, 4 * b)).then_inc(h_rs, 1)
                dve.wait_ge(h_rs, 2 * b + 1)
                nc.vector.tensor_scalar(four(hrs, 4 * b), four(hsd, 4 * b), 0.5, None, ALU.mult).then_inc(h_rs, 1)

            def head_norm(t):
                dve.wait_ge(h_rs, 2 * (t // 4) + 2)
                dve.wait_ge(hg_ok, (NH - 1) * NT + t + 1)
                hv = hg[:, t, :].rearrange("p (h v) -> p h v", h=NH)
                rs = hrs[:].rearrange("p (h t) -> p t h", t=NT)[:, t, :]
                nc.vector.tensor_tensor(hv, hv, rs.unsqueeze(2).to_broadcast([P, NH, DV]), ALU.mult).then_inc(og_n[0], 1)

            def og_low(t):
                for j in range(2):
                    dve.wait_ge(og_H, 2 * t + j + 1)
                    cols = slice(t * P, (t + 1) * P)
                    nc.vector.tensor_tensor(hL[:, 4 * j:4 * j + 4, cols],
                                            og_banks(t)[j][:].rearrange("p (k n) -> p k n", n=P),
                                            hH[:, 4 * j:4 * j + 4, cols].bitcast(F32), ALU.subtract).then_inc(og_L, 1)

            def head(h, first, last=False):
                if first:
                    nc.vector.memset(va[:, :, DV:DV + 1], 1.0).then_inc(v_one, 1)
                    gates_rows()
                    split_L(2, 2)
                    gates_columns()
                    split_L(h * 3 + 3, 0)
                    dve.wait_ge(thr_ok, 1)
                else:
                    split_L(h * 3 + 2, 2)
                    split_L(h * 3 + 3, 0)
                    mod_row(h * 2 - 1)

                def weighted(c):
                    n = h * NT + c
                    dve.wait_ge(st_mm, n + 1)
                    dve.wait_ge(e_ok, n + 1)
                    if c >= 2:
                        dve.wait_ge(o_mm, n - 1)
                        dve.wait_ge(dc_mm, h * (NT - 1) + c - 1)
                    elif not first:
                        dve.wait_ge(o_mm, h * NT)
                        dve.wait_ge(dc_mm, h * (NT - 1))
                    nc.vector.tensor_scalar(kw[:, c % 2, :], ST[c % 2][:, P:2 * P], E[:, c % 2, P - 1:P], None, ALU.mult)
                    nc.vector.tensor_tensor(PT[:, c % 2, :], ST[c % 2][:, 0:P], E[:, c % 2, :],
                                            ALU.mult).then_inc(kwpt, 1)

                def state(c):
                    dve.wait_ge(dc_mm, h * (NT - 1) + c + 1)
                    if c == 0:
                        if not first:
                            dve.wait_ge(o_mm, h * NT)
                        nc.vector.tensor_copy(C[:], DC[:, 0:DV + 1]).then_inc(c_ok, 1)
                    else:
                        dve.wait_ge(c_ok, h * (NT - 1) + c)
                        e = (c + 1) * P - 1
                        nc.vector.scalar_tensor_tensor(C[:], C[:], sI[:, e:e + 1], DC[:, 0:DV + 1], ALU.mult,
                                                       ALU.add).then_inc(c_ok, 1)

                def divide(c):
                    n = h * NT + c
                    dve.wait_ge(o_mm, n + 1)
                    col = thr[:, c:c + 1] if first else thr[:, bass.ds(h * NT + c, 1)]
                    d = den[:, c % 2:c % 2 + 1]
                    nc.vector.tensor_scalar(d, O[c % 2][:, DV:DV + 1], -1.0, col, ALU.mult,
                                            ALU.max).then_inc(den_ok, 1)
                    dve.wait_ge(den_ok, n * 2 + 1)
                    nc.vector.tensor_scalar(d, O[c % 2][:, DV:DV + 1], d, None, ALU.max).then_inc(den_ok, 1)
                    dve.wait_ge(den_ok, n * 2 + 2)
                    nc.vector.reciprocal(rden[:, c % 2:c % 2 + 1], den[:, c % 2:c % 2 + 1]).then_inc(rden_ok, 1)
                    dve.wait_ge(rden_ok, n + 1)
                    if c >= 2:
                        dve.wait_ge(hg_ok, n - 1)
                        dve.wait_ge(hms_ok, n - 1)
                    elif not first:
                        dve.wait_ge(hg_ok, h * NT)
                        dve.wait_ge(hms_ok, h * NT)
                    nc.vector.tensor_scalar(hc[:, c % 2, :], O[c % 2][:, 0:DV], rden[:, c % 2:c % 2 + 1], None,
                                            ALU.mult).then_inc(hc_ok, 1)

                def gating(c):
                    n = h * NT + c
                    dve.wait_ge(th_ok, n + 1)
                    if c == 0:
                        dve.wait_ge(nw_in, h * 16 + 16)
                    if c >= 2:
                        dve.wait_ge(hg_ok, n - 1)
                    elif not first:
                        dve.wait_ge(hg_ok, h * NT)
                    nc.vector.scalar_tensor_tensor(gate[:, c % 2, :], th[:, c % 2, :], 1.0, nwb[:], ALU.add,
                                                   ALU.mult).then_inc(gate_ok, 1)

                def ada_item(i):
                    n = h * 16 + i
                    dve.wait_ge(ada_in[i % 2], h * 128 + (i // 2) * 16 + 16)
                    k = i % KD
                    if not (first and i == 0):
                        dve.wait_ge(acc_ok, n)
                    if k == 0:
                        if not (first and i == 0):
                            dve.wait_ge(ad_mm, h * 2 + i // KD)
                        nc.vector.tensor_scalar(acc[:], ada[:, i % 2, :], cact[:, 0:1], None,
                                                ALU.mult).then_inc(acc_ok, 1)
                    else:
                        nc.vector.scalar_tensor_tensor(acc[:], ada[:, i % 2, :], cact[:, k:k + 1], acc[:],
                                                       ALU.mult, ALU.add).then_inc(acc_ok, 1)

                for c in range(NT + 1):
                    if 1 <= c < NT:
                        state(c - 1)
                    if c < NT:
                        weighted(c)
                    if c:
                        divide(c - 1)
                        gating(c - 1)
                    if c == 5:
                        mod_row(h * 2)
                    if c < NT:
                        ada_item(2 * c)
                        ada_item(2 * c + 1)
                    if c in (2, 4):
                        split_L(h * 3 + 4, 1, pieces=(c // 2 - 1,))
                    if last:
                        if c == 5:
                            head_var(0)
                        if c == 6:
                            head_rstd(0)
                if last:
                    og_low(0)

            head(0, True)
            with dve.Fori(1, NH - 1) as h:
                head(h, False)
            head(NH - 1, False, True)

            def y_tile(n):
                j, t = divmod(n, NT)
                if n == 0:
                    dve.wait_ge(g1_in, 16)
                    dve.wait_ge(hg_ok, NH * NT)
                if j == 0 and t % 2 == 0:
                    dve.wait_ge(x2_in[t // 2], 16)
                dve.wait_ge(y_mm, n + 1)
                if n >= 2:
                    dve.wait_ge(y_ev, n - 1)
                nc.vector.tensor_tensor(tmp[:, n % 2, :], Y_BANKS[n % 4][:, 0:DV], gb[:, j * DV:(j + 1) * DV],
                                        ALU.mult).then_inc(y_g, 1)
                dve.wait_ge(y_g, n + 1)
                cols = slice(j * DV, (j + 1) * DV)
                nc.vector.tensor_tensor(x2[:, t, cols], x2[:, t, cols], tmp[:, n % 2, :], ALU.add).then_inc(y_ev, 1)

            head_norm(2)
            head_var(1)
            og_low(1)
            mod_row(2 * NH - 1)
            head_rstd(1)
            y_tile(0)
            for t in range(2, NT):
                og_low(t)
                y_tile(t - 1)
                if t % 2 == 0 and t + 2 < NT:
                    head_norm(t + 2)
                if t == 5:
                    split_L(U_OUT + 2, 2)
            y_tile(NT - 1)
            split_L(U_OUT + 3, 0)
            for n in range(NT, 2 * NT):
                y_tile(n)
            split_L(U_FF, 1)
            dve.wait_ge(sc2_in, 16)
            nc.vector.tensor_scalar(sc2[:], sc2[:], 1.0, None, ALU.add).then_inc(sc2_ok, 1)
            for n in range(2 * NT, 3 * NT):
                y_tile(n)
            split_L(U_FF + 1, 2)
            dve.wait_ge(sc2_ok, 1)
            for t in range(NT + 2):
                if t < NT:
                    y_tile(3 * NT + t)
                if 1 <= t <= NT:
                    variance(NT + t - 1)
                    i = NT + t - 1
                    inverse(i)
                    if t >= 3:
                        dve.wait_ge(n_tr, 2 * (i - 1))
                    nc.vector.scalar_tensor_tensor(hn2[:, (t - 1) % 2, :], x2[:, t - 1, :], rstd[:, i:i + 1], sc2[:],
                                                   ALU.mult, ALU.mult).then_inc(n_hn, 1)
                if t >= 2:
                    low(t - 2)

            def product(f_count, f, half):
                n = f_count * 2 + half
                dve.wait_ge(sg_ok, n + 1)
                dve.wait_ge(gu_mm, n * 2 + 2)
                if not isinstance(n, int) or n >= 4:
                    dve.wait_ge(a_L, n - 3)
                nc.vector.tensor_tensor(stage[:, f, half * HALF:(half + 1) * HALF], sg[:, half, :],
                                        GU_BANKS[2 * half + 1][:], ALU.mult).then_inc(st_ok, 1)

            def act_low(f_count, f, half):
                n = f_count * 2 + half
                dve.wait_ge(a_H, n + 1)
                cols = slice(half * HALF, (half + 1) * HALF)
                nc.vector.tensor_tensor(actL[:, f, cols], stage[:, f, cols], actH[:, f, cols].bitcast(F32),
                                        ALU.subtract).then_inc(a_L, 1)

            def add_down(g, first, lo, hi):
                for n in range(lo, hi):
                    dve.wait_ge(d_mm, g * 16 + n + 1)
                    t, j = divmod(n, 2)
                    cols = slice(j * HALF, (j + 1) * HALF)
                    nc.vector.tensor_tensor(x2[:, t, cols], x2[:, t, cols], Y_BANKS[n % 4][:],
                                            ALU.add).then_inc(d_ev, 1)

            split_L(U_FF + 2, 0)
            for half in range(2):
                product(0, 0, half)
                act_low(0, 0, half)
            split_L(U_FF + 3, 1)
            for half in range(2):
                product(1, 1, half)
                act_low(1, 1, half)

            def group(g, last):
                u = g * 3 + (U_FF - 1)
                split_L(u + 2, 2)
                for half in range(2):
                    product(g * 2, 0, half)
                if last:
                    add_down(g - 1, False, 0, 4)
                    split_L(u + 3, 0)
                    add_down(g - 1, False, 4, 16)
                else:
                    add_down(g - 1, False, 0, 4)
                    split_L(u + 3, 0)
                    add_down(g - 1, False, 4, 16)
                for half in range(2):
                    act_low(g * 2, 0, half)
                if not last:
                    split_L(u + 4, 1)
                for half in range(2):
                    product(g * 2 + 1, 1, half)
                    act_low(g * 2 + 1, 1, half)

            with dve.Fori(1, NG - 1) as g:
                group(g, False)
            group(NG - 1, True)
            dve.wait_ge(fw_in, 16)

            def finish(t):
                i = 2 * NT + t
                variance(i)
                dve.wait_ge(n_sd, i + 1)
                nc.vector.reciprocal(rstd[:, i:i + 1], sd[:, i:i + 1]).then_inc(n_rstd, 1)
                dve.wait_ge(n_rstd, i + 1)
                nc.vector.scalar_tensor_tensor(x2[:, t, :], x2[:, t, :], rstd[:, i:i + 1], fw[:], ALU.mult,
                                               ALU.mult).then_inc(f_out, 1)

            for t in range(NT):
                add_down(NG - 1, False, 2 * t, 2 * t + 2)
                dve.wait_ge(d_ev, 16 * (NG - 1) + 2 * t + 2)
                if t:
                    finish(t - 1)
            finish(NT - 1)

        @block.tensor
        def _(pe):
            def three(out_ap, lhs, rhs, k0, n, last):
                for i, (a, b) in enumerate(((0, 0), (0, 1), (1, 0))):
                    ins = nc.tensor.matmul(out_ap, lhs[a], rhs[b], start=(n == 0 and i == 0), stop=(last and i == 2))
                return ins

            def project(out_ap, lhs, rhs):
                for k in range(KD):
                    ins = three(out_ap, lhs(k), rhs(k), k, k, k == KD - 1)
                return ins

            def h_cols(half):
                return lambda k: tuple(h[:, k, half * HALF:(half + 1) * HALF] for h in (hH, hL))

            def h_tile(t):
                return lambda k: tuple(h[:, k, t * P:(t + 1) * P] for h in (hH, hL))

            def transposes2(t):
                pe.wait_ge(n_sh, t + 1)
                for j in range(2):
                    if t:
                        pe.wait_ge(n_L, 2 * (t - 1) + j + 1)
                    for k in range(4):
                        ins = nc.tensor.transpose(ST[j][:, k * P:(k + 1) * P],
                                                  hn2[:, t % 2, (4 * j + k) * P:(4 * j + k + 1) * P], ident[:])
                    ins.then_inc(n_tr, 1)

            def mod_columns(k):
                pe.wait_ge(acc0_ok, KD * (k + 1))
                for m in range(2):
                    ins = nc.tensor.matmul(MOD_BANKS[k % 2][:, 2 * k + m:2 * k + m + 1],
                                           acc0[:, k % 2, m * P:(m + 1) * P], ones[:, 0:1], start=True, stop=True)
                ins.then_inc(mod1_mm, 1)

            def start():
                pe.wait_ge(const_ok, 2)
                for t in range(NT):
                    if t in POOL_X:
                        pe.wait_ge(n_hnp, POOL_X.index(t) + 1)
                    else:
                        pe.wait_ge(n_hn, t + 1 - sum(i < t for i in POOL_X))
                    for j in range(2):
                        if t >= 2:
                            pe.wait_ge(xT_ok[j], t - 1)
                        for k in range(4):
                            ins = nc.tensor.transpose(XT_BANKS[2 * (t % 2) + j][:, k * P:(k + 1) * P],
                                                      xin[:, t, (4 * j + k) * P:(4 * j + k + 1) * P], ident[:])
                        ins.then_inc(n_tr, 1)
                pe.wait_ge(ones_ok, 1)
                mod_columns(0)
                pe.wait_ge(wg_L, 1)
                wg = [w[:, 2, 0:KD * P].rearrange("p (k n) -> p k n", n=P) for w in (wH, wL)]
                ws = unit_weights(0, 2 * DK)
                for k in range(KD):
                    if k % 4 == 0:
                        pe.wait_ge(w_L, k // 4 + 1)
                    if 1 < k < KD - 1:
                        mod_columns(k + 1)
                    for half in range(2):
                        pe.wait_ge(m_L, 2 * k + half + 1)
                        hs = h_cols(half)(k)
                        last = k == KD - 1
                        for m in range(2):
                            ins = three(QK_BANKS[2 * half + m][:], tuple(w[:, k, m * DK:(m + 1) * DK] for w in ws),
                                        hs, k, k, last)
                            if last:
                                ins.then_inc(qk_mm, 1)
                        ins = three(OP[half][:], tuple(w[:, k, :] for w in wg), hs, k, k, last)
                        if last:
                            ins.then_inc(gates_mm, 1)
                        if k < 2 and half == 0:
                            mod_columns(k + 1)

            def qk(h, i):
                ws = unit_weights(0, 2 * DK)
                m = i % 2
                project(QK_BANKS[i][:], lambda k: tuple(w[:, k, m * DK:(m + 1) * DK] for w in ws),
                        h_cols(i // 2)).then_inc(qk_mm, 1)

            def row_transposes():
                pe.wait_ge(g_dve, 7)
                for c in range(NT):
                    ins = nc.tensor.transpose(AD[:, c * GATE_ROWS:(c + 1) * GATE_ROWS],
                                              rows[0:GATE_ROWS, A_, c * P:(c + 1) * P],
                                              ident[0:GATE_ROWS, 0:GATE_ROWS])
                ins.then_inc(rT_mm, 1)

            def ada_row(n):
                pe.wait_ge(acc_ok, n * KD + KD)
                pe.wait_ge(brow_in, n * 16 + 16)
                if isinstance(n, int) and n == 0:
                    pe.wait_ge(rT_cp, 2)
                else:
                    pe.wait_ge(ad_ev, n)
                nc.tensor.matmul(AD[0:1, :], ones[:, 0:1], acc[:], start=True, stop=False)
                nc.tensor.matmul(AD[0:1, :], ones[0:1, 0:1], brow[0:1, :], start=False, stop=True).then_inc(ad_mm, 1)

            def out_transposes(t):
                if t and t % 2 == 0:
                    pe.wait_ge(og_n[0], t // 2)
                else:
                    pe.wait_ge(og_n[1], (t + 1) // 2 + 1)
                for j in range(2):
                    if t == 0:
                        pe.wait_ge(*((hc_ok, NH * NT - 1), (c_ok, NH * (NT - 1)))[j])
                    elif t == 1:
                        pe.wait_ge(kwpt, NH * NT)
                    elif t == 2 and j == 1:
                        pe.wait_ge(hc_ok, NH * NT)
                    else:
                        pe.wait_ge(og_L, 2 * (t - 2) + j + 1)
                    for k in range(4):
                        ins = nc.tensor.transpose(og_banks(t)[j][:, k * P:(k + 1) * P],
                                                  hg[:, t, (4 * j + k) * P:(4 * j + k + 1) * P], ident[:])
                    ins.then_inc(og_tr, 1)

            def head(h, first, last=False):
                if first:
                    start()
                else:
                    pe.wait_ge(w_L, h * 6 + 2)
                    for i in range(4):
                        pe.wait_ge((hc_ok, kwpt, kwpt, hc_ok)[i], h * NT - (1, 1, 0, 0)[i])
                        qk(h, i)
                    ada_row(h * 2 - 1)
                pe.wait_ge(w_L, h * 6 + 4)
                wv = unit_weights(1, DV)
                for t in range(NT):
                    if t >= 2:
                        pe.wait_ge(v_ev, h * NT + t - 1)
                    elif first:
                        pe.wait_ge(g_act, t + 1)
                    else:
                        pe.wait_ge(th_ok, h * NT - 1 + t)
                    project(OP[t % 2][:, 0:DV], h_tile(t),
                            lambda k: tuple(w[:, k, :] for w in wv)).then_inc(v_mm, 1)
                    if first and t == 3:
                        row_transposes()
                pe.wait_ge(qk_ev, h * 4 + 4)
                if first:
                    pe.wait_ge(v_one, 1)
                pe.wait_ge(w_L, h * 6 + 6)
                wo = unit_weights(2, DV)
                for c in range(NT):
                    n = h * NT + c
                    toks = slice(c * P, (c + 1) * P)
                    if c >= 2:
                        pe.wait_ge(kwpt, n - 1)
                    nc.tensor.matmul(ST[c % 2][:, 0:P], kT[:, toks], qT[:, toks], start=True, stop=True)
                    nc.tensor.transpose(ST[c % 2][:, P:2 * P], kT[:, toks], ident[:]).then_inc(st_mm, 1)
                    if c >= 2:
                        pe.wait_ge(th_ok, n - 1)
                    else:
                        pe.wait_ge(v_ev, h * NT + NT - 1 + c)
                    project(OP[c % 2][:, 0:DV], h_tile(c),
                            lambda k: tuple(w[:, k, :] for w in wo)).then_inc(op_mm, 1)
                    if c == 4:
                        ada_row(h * 2)
                    if c == NT - 1 and last:
                        out_transposes(0)
                    pe.wait_ge(kwpt, n + 1)
                    if c == 0:
                        pe.wait_ge(v_ev, h * NT + NT)
                    if c >= 2:
                        pe.wait_ge(hc_ok, n - 1)
                    if c:
                        pe.wait_ge(qs_ok, h * (NT - 1) + c)
                        pe.wait_ge(c_ok, h * (NT - 1) + c)
                        nc.tensor.matmul(O[c % 2][:, 0:DV + 1], qs[:, c % 2, :], C[:], start=True, stop=False)
                    nc.tensor.matmul(O[c % 2][:, 0:DV + 1], PT[:, c % 2, :], va[:, c, :], start=(c == 0),
                                     stop=True).then_inc(o_mm, 1)
                    if c < NT - 1:
                        nc.tensor.matmul(DC[:, 0:DV + 1], kw[:, c % 2, :], va[:, c, :], start=True,
                                         stop=True).then_inc(dc_mm, 1)

            head(0, True)
            with pe.Fori(1, NH - 1) as h:
                head(h, False)
            head(NH - 1, False, True)

            def y_tile(n):
                j, t = divmod(n, NT)
                if t == 0:
                    pe.wait_ge(w_L, 2 * (U_OUT + j) + 2)
                if j == 0:
                    pe.wait_ge(og_L, 2 * t + 2)
                if n >= 4:
                    pe.wait_ge(y_g, n - 3)
                else:
                    pe.wait_ge((th_ok, th_ok, c_ok, ad_ev)[n], (NH * NT, NH * NT, NH * (NT - 1), 2 * NH)[n])
                ws = unit_weights(j % 3, DV)
                project(Y_BANKS[n % 4][:, 0:DV], h_tile(t), lambda k: tuple(w[:, k, :] for w in ws)).then_inc(y_mm, 1)

            out_transposes(1)
            ada_row(2 * NH - 1)
            for t in range(NT):
                y_tile(t)
                if t + 2 < NT:
                    out_transposes(t + 2)
            for n in range(NT, 3 * NT):
                y_tile(n)
            for t in range(NT):
                y_tile(3 * NT + t)
                if t >= 3:
                    transposes2(t - 3)

            def gate_up(f_count, k, between=(None, None)):
                ws = unit_weights(k, 2 * P)
                for half in range(2):
                    n = f_count * 2 + half
                    for m in range(2):
                        if half == 0 and between[m]:
                            between[m]()
                        if not isinstance(n, int) or n >= 2:
                            pe.wait_ge((sg_ok, st_ok)[m], n - 1)
                        if isinstance(n, int) and n < 2:
                            pe.wait_ge(n_L, NT * (half + 1))
                        project(GU_BANKS[2 * half + m][:], lambda k: tuple(w[:, k, m * P:(m + 1) * P] for w in ws),
                                h_cols(half)).then_inc(gu_mm, 1)

            def down(g, k):
                pe.wait_ge(a_L, g * 4 + 4)
                ws = unit_weights(k, D)
                acts = (actH, actL)
                for n in range(16):
                    t, j = divmod(n, 2)
                    if isinstance(g, int) and g == 0 and n < 4:
                        pe.wait_ge(y_g, 4 * NT)
                    else:
                        pe.wait_ge(d_ev, g * 16 + n - 3)
                    for f in range(2):
                        ins = three(Y_BANKS[n % 4][:], tuple(a[:, f, t * P:(t + 1) * P] for a in acts),
                                    tuple(w[:, f, j * HALF:(j + 1) * HALF] for w in ws), f, f, f == 1)
                    ins.then_inc(d_mm, 1)

            transposes2(NT - 3)
            pe.wait_ge(w_L, 2 * U_FF + 2)
            gate_up(0, 1, (lambda: None, lambda: (transposes2(NT - 2), transposes2(NT - 1))))
            pe.wait_ge(w_L, 2 * U_FF + 4)
            gate_up(1, 2)

            def group(g):
                u = g * 3 + (U_FF - 1)
                pe.wait_ge(w_L, u * 2 + 2)
                gate_up(g * 2, 0)
                pe.wait_ge(w_L, u * 2 + 4)
                down(g - 1, 1)
                pe.wait_ge(w_L, u * 2 + 6)
                gate_up(g * 2 + 1, 2)

            group(1)
            with pe.Fori(2, NG) as g:
                group(g)
            pe.wait_ge(w_L, 2 * NU)
            down(NG - 1, 0)


def kernel(x, c, ada_w, ada_b, ml_w_in, ml_b_if, ml_norm_w, ml_w_out, gdn_w_in, gdn_conv_w, gdn_a_log, gdn_dt_bias,
           gdn_norm_w, gdn_w_out, ffn_w_gate_up, ffn_w_down, final_norm_w):
    import numpy as np
    import concourse.bacc as bacc
    from concourse.bass_utils import run_bass_kernel_spmd

    def tiled(w):
        return np.asarray(w).reshape(-1, P, w.shape[1]).transpose(1, 0, 2)

    w_in, w_out, gate_up, down = (np.asarray(a)[0] for a in (ml_w_in, ml_w_out, ffn_w_gate_up, ffn_w_down))
    units = []
    for h in range(NH):
        q, k = (w_in[:, n * NH * DK + h * DK:n * NH * DK + (h + 1) * DK] for n in range(2))
        v, o = (w_in[:, D * (n + 1) + h * DV:D * (n + 1) + (h + 1) * DV] for n in range(2))
        units += [np.concatenate([tiled(q), tiled(k)], 2), tiled(v), tiled(o)]
    units += [tiled(w_out[:, j * DV:(j + 1) * DV]) for j in range(4)]

    def gu(f):
        return np.concatenate([tiled(gate_up[:, n * DFF + f * P:n * DFF + (f + 1) * P]) for n in range(2)], 2)

    for g in range(NG):
        units.append(gu(2 * g))
        if g:
            units.append(tiled(down[(g - 1) * 2 * P:g * 2 * P]))
        units.append(gu(2 * g + 1))
    units.append(tiled(down[(NG - 1) * 2 * P:]))
    w_units = np.stack([u.reshape(P, 2, D).transpose(1, 0, 2) for u in units])

    gates = w_in[:, 3 * D:]
    pad = np.zeros((D, 32 - NH), gates.dtype)
    w_gates = np.ascontiguousarray(tiled(np.concatenate([gates[:, :NH], pad, gates[:, NH:]], 1)))
    mods = np.asarray(ada_w)[0].reshape(D, 6, D).transpose(1, 0, 2)
    first = mods[[1, 0]].reshape(2, KD, P, KD, P).transpose(3, 2, 1, 0, 4).reshape(KD, P, KD, 2 * P)
    rest = np.stack([mods[m].reshape(KD, P, 2, HALF).transpose(2, 0, 1, 3) for m in range(2, 6)])
    b = np.asarray(ada_b)[0].reshape(6, D)
    arrays = {
        "x": np.asarray(x)[0].reshape(NT, P, D),
        "c_col": np.asarray(c)[0].reshape(KD, P).T,
        "ada_first": first,
        "ada_first_b": b[[1, 0]].reshape(2, KD, P).transpose(2, 1, 0).reshape(P, 2 * KD),
        "ada_rest": rest.reshape(8 * KD, P, HALF),
        "ada_rest_b": b[2:].reshape(8, HALF),
        "w_units": w_units,
        "w_gates": w_gates,
        "b_if": np.asarray(ml_b_if)[0].reshape(2 * NH, 1),
        "norm_w": np.asarray(ml_norm_w)[0].reshape(NH, DV),
        "final_w": np.asarray(final_norm_w).reshape(1, D),
    }
    arrays = {n: np.ascontiguousarray(a) for n, a in arrays.items()}
    nc = bacc.Bacc("TRN2", target_bir_lowering=False, num_devices=1)
    args = [nc.dram_tensor(n, a.shape, mybir.dt.from_np(a.dtype), kind="ExternalInput").ap()
            for n, a in arrays.items()]
    args.append(nc.dram_tensor("out", (NT, P, D), F32, kind="ExternalOutput").ap())
    args.append(nc.dram_tensor("scan_rows", (2, NH, S), F32, kind="Internal").ap())
    args.append(nc.dram_tensor("mod_rows", (8, HALF), F32, kind="Internal").ap())
    build(nc, *args)
    got = run_bass_kernel_spmd(nc, [arrays], core_ids=[0])
    return got.results[0]["out"].reshape(1, S, D)
```

```python
from contextlib import ExitStack

import concourse.bass as bass
from concourse import mybir

F32 = mybir.dt.float32
F32R = mybir.dt.float32r
ALU = mybir.AluOpType
ACT = mybir.ActivationFunctionType

P = 128
D = 1024
S = 1024
NT = S // P
KD = D // P
NH = 4
DK = 128
DV = 256
DFF = 2816
NF = DFF // P
NG = NF // 2
HALF = 512
UW = 2 * D
EPS = 1e-6
CAP = 15.0
MASKED = 1e30
U_HEAD = 3
U_OUT = U_HEAD * NH
U_FF = U_OUT + 4
NU = U_FF + 3 * NG
POOL_HALF = (0, 2, 4)
N1 = KD + 1
GATE_ROWS = 36


def build(nc, x, c_col, ada_first, ada_first_b, ada_rest, ada_rest_b, w_units, w_gates, b_if, norm_w, final_w, out,
          scan_rows, mod_rows):
    with ExitStack() as ctx:
        base = (nc.sbuf_base + 63) // 64 * 64
        ctx.enter_context(nc.sbuf_tensor("arena", [P, (212800 - 64) // 4], F32))

        def at(name, shape, offset, dt=F32):
            return nc.alloc_sbuf_tensor_at(name, shape, dt, offset=base + offset)

        hH = at("hH", [P, KD, S], 0, F32R)
        hL = at("hL", [P, KD, S], 32768, F32R)
        xnT = at("xnT", [P, KD, S], 32768)
        wH = at("wH", [P, 3, UW], 65536, F32R)
        wL = at("wL", [P, 3, UW], 90112, F32R)
        raw = at("raw", [P, UW], 114688)
        G0 = 122880
        ada0 = at("ada0", [P, 4, KD, 2 * P], G0)
        rows = at("rows", [P, 8, S], G0)
        hg = at("hg", [P, NT, D], G0)
        sc2 = at("sc2", [P, D], G0)
        sh2 = at("sh2", [P, D], G0 + 4096)
        hn2 = at("hn2", [P, 4, D], G0 + 8192)
        stage = at("stage", [P, 2, S], G0)
        sg = at("sg", [P, 2, HALF], G0 + 8192)
        fw = at("fw", [P, D], G0 + 12288)
        actH = at("actH", [P, 2, S], G0 + 16384, F32R)
        actL = at("actL", [P, 2, S], G0 + 24576, F32R)
        X0 = G0 + 32768
        xin = at("xin", [P, NT, D], X0)
        qT = at("qT", [P, S], X0)
        kT = at("kT", [P, S], X0 + 4096)
        va = at("va", [P, NT, DV + 1], X0 + 8192)
        Mb = at("Mb", [P, S], X0 + 16416)
        sI = at("sI", [P, S], X0 + 20512)
        ada = at("ada", [P, 2, HALF], X0 + 24608)
        acc = at("acc", [P, HALF], X0 + 28704)
        x2 = at("x2", [P, NT, D], X0)
        gb = at("gb", [P, D], X0 + 32768)
        acc0 = at("acc0", [P, 2, 2, 2 * P], X0 + 32768)
        Z0 = X0 + 36864
        E = at("E", [P, 2, P], Z0)
        PT = at("PT", [P, 2, P], Z0 + 1024)
        kw = at("kw", [P, 2, P], Z0 + 2048)
        qs = at("qs", [P, 2, P], Z0 + 3072)
        junk = at("junk", [P, D], Z0)
        hc = at("hc", [P, 2, DV], Z0 + 4096)
        b1 = at("b1", [P, 2 * KD], Z0 + 4096)
        mod1 = at("mod1", [P, 2 * KD], Z0 + 4160)
        wg_raw = at("wg_raw", [P, KD, GATE_ROWS], Z0 + 4224)
        th = at("th", [P, 2, DV], Z0 + 6144)
        gate = at("gate", [P, 2, DV], Z0 + 8192)
        C = at("C", [P, DV + 1], Z0 + 10240)
        ident = at("ident", [P, P], Z0 + 11296)
        ones = at("ones", [P, P], Z0 + 11808)
        maskb = at("maskb", [P, P], Z0 + 12320)
        nwb = at("nwb", [P, DV], Z0 + 12832)
        brow = at("brow", [P, HALF], Z0 + 13856)
        adarow = at("adarow", [P, HALF], Z0 + 15904)
        Y0 = Z0 + 17952
        craw = at("craw", [P, KD], Y0)
        cact = at("cact", [P, KD], Y0 + 32)
        ms = at("ms", [P, 3 * NT], Y0 + 64)
        var = at("var", [P, 3 * NT], Y0 + 160)
        sd = at("sd", [P, 3 * NT], Y0 + 256)
        rstd = at("rstd", [P, 3 * NT], Y0 + 352)
        aT = at("aT", [P, NH * NT], Y0 + 448)
        tT = at("tT", [P, NH * NT], Y0 + 576)
        thr = at("thr", [P, NH * NT], Y0 + 704)
        hms = at("hms", [P, NH * NT], Y0 + 832)
        hvar = at("hvar", [P, NH * NT], Y0 + 960)
        hsd = at("hsd", [P, NH * NT], Y0 + 1088)
        hrs = at("hrs", [P, NH * NT], Y0 + 1216)
        den = at("den", [P, 2], Y0 + 1344)
        rden = at("rden", [P, 2], Y0 + 1376)
        bcol = at("bcol", [P, 1], Y0 + 1408)
        bcol15 = at("bcol15", [P, 1], Y0 + 1440)
        mp = at("mp", [P, NT], Y0 + 1472)
        sqj = at("sqj", [P, DV], Y0 + 1504, mybir.dt.bfloat16)

        T_, NL, NB, A_, DD, M_, SI, MR = range(8)

        def row(n, p0=0, p1=NH):
            return rows[p0:p1, n, :]

        ST = [ctx.enter_context(nc.psum_tensor(f"ST{i}", [P, HALF], F32)) for i in range(2)]
        O = [ctx.enter_context(nc.psum_tensor(f"O{i}", [P, HALF], F32)) for i in range(2)]
        OP = [ctx.enter_context(nc.psum_tensor(f"OP{i}", [P, HALF], F32)) for i in range(2)]
        DC = ctx.enter_context(nc.psum_tensor("DC", [P, HALF], F32))
        AD = ctx.enter_context(nc.psum_tensor("AD", [P, HALF], F32))
        QK_BANKS = [O[0], ST[0], ST[1], O[1]]
        Y_BANKS = [OP[0], OP[1], DC, AD]
        XT_BANKS = [ST[0], ST[1], O[0], O[1]]
        MOD_BANKS = [DC, AD]
        GU_BANKS = [O[0], O[1], ST[0], ST[1]]

        def sem(name):
            return ctx.enter_context(nc.semaphore(name))

        c_in, bif_in, wg_in, b1_in = sem("c_in"), sem("bif_in"), sem("wg_in"), sem("b1_in")
        ada0_in = [sem(f"ada0_in{i}") for i in range(4)]
        x_in = [sem(f"x_in{i}") for i in range(NT)]
        x2_in = [sem(f"x2_in{i}") for i in range(4)]
        raw_in = [sem(f"raw_in{i}") for i in range(2)]
        ada_in = [sem(f"ada_in{i}") for i in range(2)]
        rows_out = [sem(f"rows_out{i}") for i in range(2)]
        brow_in, mb_in, si_in, nw_in, mod_out = (sem("brow_in"), sem("mb_in"), sem("si_in"), sem("nw_in"),
                                                 sem("mod_out"))
        sc2_in, sh2_in, g1_in, g2_in, fw_in = sem("sc2_in"), sem("sh2_in"), sem("g1_in"), sem("g2_in"), sem("fw_in")
        out_done = sem("out_done")
        const_0, const_ok, ones_ok, rows_set = sem("const_0"), sem("const_ok"), sem("ones_ok"), sem("rows_set")
        c_act = sem("c_act")
        b1_ok, acc0_ok, mod1_mm, mod1_ok = sem("b1_ok"), sem("acc0_ok"), sem("mod1_mm"), sem("mod1_ok")
        xT_ok = [sem(f"xT_ok{j}") for j in range(2)]
        m_x, m_H, m_L, sc2_ok = sem("modulated"), sem("modulated_H"), sem("modulated_L"), sem("sc2_ok")
        n_ms, n_var, n_sd, n_rstd, n_hn, n_sh, n_tr, n_H, n_L = (
            sem(f"norm_{s}") for s in ("ms", "var", "sd", "rstd", "scaled", "shifted", "transposed", "H", "L"))
        w_H, w_L, w_scaled = sem("w_H"), sem("w_L"), sem("w_scaled")
        wg_zero, wg_H, wg_L, gates_mm = sem("wg_zero"), sem("wg_H"), sem("wg_L"), sem("gates_mm")
        g_part, g_sum = sem("g_part"), sem("g_sum")
        b15_ok, g_act, g_dve, rT_mm, rT_cp, thr_ok = (sem("b15_ok"), sem("g_act"), sem("g_dve"), sem("rT_mm"),
                                                      sem("rT_cp"), sem("thr_ok"))
        qk_mm, qk_ev, v_mm, v_ev, v_one = sem("qk_mm"), sem("qk_ev"), sem("v_mm"), sem("v_ev"), sem("v_one")
        masked, e_ok, st_mm, kwpt, qs_ok = sem("masked"), sem("e_ok"), sem("st_mm"), sem("kwpt"), sem("qs_ok")
        op_mm, th_ok, gate_ok = sem("op_mm"), sem("th_ok"), sem("gate_ok")
        o_mm, dc_mm, c_ok = sem("o_mm"), sem("dc_mm"), sem("c_ok")
        den_ok, rden_ok, hc_ok, hms_ok, hg_ok = sem("den_ok"), sem("rden_ok"), sem("hc_ok"), sem("hms_ok"), sem("hg_ok")
        acc_ok, ad_mm, ad_ev = sem("acc_ok"), sem("ad_mm"), sem("ad_ev")
        h_var, h_sd, h_rs = sem("h_var"), sem("h_sd"), sem("h_rs")
        og_n = [sem(f"og_n{i}") for i in range(2)]
        og_tr, og_H, og_L = sem("og_tr"), sem("og_H"), sem("og_L")
        y_mm, y_ev = sem("y_mm"), sem("y_ev")
        gu_mm, sg_ok, st_ok, a_H, a_L = sem("gu_mm"), sem("sg_ok"), sem("st_ok"), sem("a_H"), sem("a_L")
        d_mm, d_ev, f_half = sem("d_mm"), sem("d_ev"), sem("f_half")
        f_out = [sem(f"f_out{i}") for i in range(2)]

        def slot(k):
            return k % 3

        def unit_weights(k, width):
            return tuple(w[:, slot(k), :].rearrange("p (k n) -> p k n", n=width) for w in (wH, wL))

        def piece(t, i):
            return t[:, i * D:(i + 1) * D]

        def og_banks(t):
            return (O[0], DC) if t == 0 else (ST, O)[1 - t % 2]

        def n2_banks(t):
            return OP if t in (5, 7) else ST

        def four(v, t0):
            return v[:].rearrange("p (h t) -> p h t", t=NT)[:, :, t0:t0 + 4]

        gate_weights = wH[:, 2, 0:KD * P].rearrange("p (k n) -> p k n", n=P)

        block = ctx.enter_context(nc.Block())

        @block.sync
        def _(sp):
            def load_unit(u, pieces=(0, 1)):
                for i in pieces:
                    if not (isinstance(u, int) and u == 0):
                        sp.wait_ge(w_L, u * 2 - 1 + i)
                    src = w_units[u, i] if isinstance(u, int) else \
                        w_units[bass.ds(u, 1), i].rearrange("a p n -> (a p) n")
                    sp.dma_start(piece(raw, i), src).then_inc(raw_in[i], 16)

            sp.dma_start(craw[:], c_col).then_inc(c_in, 16)
            def ada_first_tile(k):
                if k >= 4:
                    sp.wait_ge(acc0_ok, N1 * (k - 3))
                sp.dma_start(ada0[:, k % 4], ada_first[k]).then_inc(ada0_in[k % 4], 16)

            sp.dma_start(b1[:], ada_first_b).then_inc(b1_in, 16)
            ada_first_tile(0)
            for t in range(NT):
                sp.dma_start(xin[:, t, :], x[t]).then_inc(x_in[t], 16)
                if t == 5:
                    load_unit(0, (0,))
            sp.dma_start(wg_raw[:], w_gates).then_inc(wg_in, 16)
            for k in range(1, KD):
                ada_first_tile(k)
                if k == 2:
                    load_unit(0, (1,))
                if k == 6:
                    load_unit(1, (0,))
            load_unit(1, (1,))
            load_unit(2)

            def ada_item(h, i, first):
                if not (first and i < 2):
                    sp.wait_ge(acc_ok, h * 16 + i - 1)
                sp.dma_start(ada[:, i % 2, :],
                               ada_rest[bass.ds(h * 16 + i, 1), :, :].rearrange("a p n -> (a p) n")
                               if not first else ada_rest[i]).then_inc(ada_in[i % 2], 16)

            def mod_store(n):
                sp.wait_ge(ad_ev, n + 1)
                sp.dma_start(mod_rows[bass.ds(n, 1), :] if not isinstance(n, int) else mod_rows[n:n + 1, :],
                             adarow[0:1, :]).then_inc(mod_out, 16)

            def ada_bias(h, half, first):
                if not (first and half == 0):
                    mod_store(h * 2 + half - 1)
                sp.dma_start(brow[0:1, :], ada_rest_b[bass.ds(h * 2 + half, 1), :] if not first
                               else ada_rest_b[half:half + 1, :]).then_inc(brow_in, 16)

            def head(h, first):
                if first:
                    sp.wait_ge(rows_out[0], 16)
                    m_src, s_src, n_src = scan_rows[0, 0:1, :], scan_rows[1, 0:1, :], norm_w[0:1, :]
                else:
                    sp.wait_ge(gate_ok, h * NT)
                    m_src, s_src = (scan_rows[i, bass.ds(h, 1), :] for i in range(2))
                    n_src = norm_w[bass.ds(h, 1), :]
                sp.dma_start(Mb[:], m_src.to_broadcast([P, S])).then_inc(mb_in, 16)
                if first:
                    sp.wait_ge(rows_out[1], 16)
                sp.dma_start(sI[:], s_src.to_broadcast([P, S])).then_inc(si_in, 16)
                sp.dma_start(nwb[:], n_src.to_broadcast([P, DV])).then_inc(nw_in, 16)
                load_unit(h * 3 + 3)
                ada_bias(h, 0, first)
                ada_item(h, 0, first)
                ada_item(h, 1, first)
                for i in range(2, 16):
                    if i in (2, 4):
                        load_unit(h * 3 + 4, (i // 2 - 1,))
                    ada_item(h, i, first)
                    if i in (7, 11):
                        load_unit(h * 3 + 5, (i // 4 - 1,))
                    if i == 12:
                        ada_bias(h, 1, first)

            head(0, True)
            with sp.Fori(1, NH) as h:
                head(h, False)
            sp.wait_ge(o_mm, NT * NH)
            sp.wait_ge(dc_mm, (NT - 1) * NH)
            sp.wait_ge(c_ok, (NT - 1) * NH)
            sp.wait_ge(e_ok, NT * NH)
            sp.wait_ge(kwpt, NT * NH)
            sp.wait_ge(qs_ok, (NT - 1) * NH)
            sp.wait_ge(ad_mm, 2 * NH)
            for i in range(4):
                sp.dma_start(x2[:, 2 * i:2 * i + 2, :],
                             x[2 * i:2 * i + 2].rearrange("t p n -> p t n")).then_inc(x2_in[i], 16)
            mod_store(2 * NH - 1)
            with sp.Fori(U_OUT + 3, NU) as u:
                load_unit(u)
            for t in range(NT):
                before = 2 * t - sum(i < t for i in POOL_HALF)
                if t < NT - 1:
                    if t in POOL_HALF:
                        sp.wait_ge(f_out[0], before + 1)
                        sp.wait_ge(f_out[1], POOL_HALF.index(t) + 1)
                    else:
                        sp.wait_ge(f_out[0], before + 2)
                    sp.dma_start(out[t], x2[:, t, :]).then_inc(out_done, 16)
                else:
                    for half in range(2):
                        sp.wait_ge(f_out[0], before + 1 + half)
                        cols = slice(half * HALF, (half + 1) * HALF)
                        sp.dma_start(out[t][:, cols], x2[:, t, cols]).then_inc(out_done, 16)
            sp.wait_ge(out_done, 16 * (NT + 1))

        @block.gpsimd
        def _(pool):
            nc.gpsimd.memset(ones[:], 1.0).then_inc(ones_ok, 1)
            nc.gpsimd.memset(ident[:], 0.0).then_inc(const_0, 1)
            nc.gpsimd.memset(maskb[:], 0.0).then_inc(const_0, 1)
            nc.gpsimd.memset(bcol[:], 0.0).then_inc(const_0, 1)
            pool.wait_ge(const_0, 3)
            nc.gpsimd.affine_select(out=ident[:], in_=ident[:], compare_op=ALU.not_equal, fill=1.0, base=0,
                                    pattern=[[-1, P]], channel_multiplier=1).then_inc(const_ok, 1)
            nc.gpsimd.affine_select(out=maskb[:], in_=maskb[:], compare_op=ALU.is_ge, fill=MASKED, base=0,
                                    pattern=[[1, P]], channel_multiplier=-1).then_inc(const_ok, 1)
            pool.dma_start(bcol[0:NH, :], b_if[0:NH, :]).then_inc(bif_in, 16)
            pool.dma_start(bcol[32:32 + NH, :], b_if[NH:2 * NH, :]).then_inc(bif_in, 16)

            pool.wait_ge(raw_in[0], 16)
            nc.gpsimd.tensor_copy(piece(wH[:, 0, :], 0), piece(raw, 0)).then_inc(w_H, 1)
            pool.wait_ge(w_H, 1)
            nc.gpsimd.tensor_tensor(piece(wL[:, 0, :], 0), piece(raw, 0), piece(wH[:, 0, :], 0).bitcast(F32),
                                    ALU.subtract).then_inc(w_L, 1)
            pool.wait_ge(wg_in, 16)
            pool.wait_ge(wg_zero, 1)
            wgH, wgL = (gate_weights[:, :, c:c + GATE_ROWS] for c in (0, 64))
            nc.gpsimd.tensor_copy(wgH, wg_raw[:]).then_inc(wg_H, 1)
            pool.wait_ge(wg_H, 1)
            nc.gpsimd.tensor_tensor(wgL, wg_raw[:], wgH.bitcast(F32), ALU.subtract).then_inc(wg_L, 1)
            pool.wait_ge(m_L, 1)
            for k in range(KD):
                for half in range(2):
                    if k or half:
                        cols = slice(half * HALF, (half + 1) * HALF)
                        pool.wait_ge(m_H, 2 * k + half + 1)
                        nc.gpsimd.tensor_tensor(hL[:, k, cols], xnT[:, k, cols], hH[:, k, cols].bitcast(F32),
                                                ALU.subtract).then_inc(m_L, 1)
            pool.wait_ge(acc0_ok, N1 * KD)
            nc.gpsimd.memset(rows[0:GATE_ROWS, A_, :], 0.0).then_inc(rows_set, 1)
            nc.gpsimd.memset(row(DD), 0.0).then_inc(rows_set, 1)
            nc.gpsimd.memset(row(MR), 1.0).then_inc(rows_set, 1)
            pool.wait_ge(rows_set, 3)
            nc.gpsimd.memset(rows[0:NH, MR, 0:S:P], 0.0).then_inc(rows_set, 1)

            def to_all(dst, n, done):
                src = mod_rows[n:n + 2, :].rearrange("(o a) n -> o (a n)", o=1).to_broadcast([P, D])
                pool.dma_start(dst[:], src).then_inc(done, 16)

            def scale_unit(u, pieces=(0, 1)):
                for i in pieces:
                    pool.wait_ge(raw_in[i], u * 16 + 16)
                    rv = piece(raw, i).rearrange("p (k n) -> p k n", n=DV)
                    j = u - U_OUT
                    nc.gpsimd.tensor_tensor(rv, rv, gb[:, j * DV:(j + 1) * DV].unsqueeze(1).to_broadcast([P, 4, DV]),
                                            ALU.mult).then_inc(w_scaled, 1)

            def head_norm(t):
                pool.wait_ge(h_rs, 2 * (t // 4) + 2)
                pool.wait_ge(hg_ok, (NH - 1) * NT + t + 1)
                hv = hg[:, t, :].rearrange("p (h v) -> p h v", h=NH)
                rs = hrs[:].rearrange("p (h t) -> p t h", t=NT)[:, t, :]
                nc.gpsimd.tensor_tensor(hv, hv, rs.unsqueeze(2).to_broadcast([P, NH, DV]),
                                        ALU.mult).then_inc(og_n[1], 1)

            def head(h, first, last=False):
                if first:
                    pool.wait_ge(g_dve, 4)
                    pool.dma_start(scan_rows[0], row(M_)).then_inc(rows_out[0], 16)
                    pool.wait_ge(g_act, 5)
                    pool.dma_start(scan_rows[1], row(SI)).then_inc(rows_out[1], 16)
                if last:
                    pool.wait_ge(mod_out, 16 * 2)
                    to_all(gb, 0, g1_in)
                pool.wait_ge(mb_in, h * 16 + 16)
                mv = Mb[:].rearrange("p (c l) -> p c l", l=P)
                nc.gpsimd.tensor_tensor(mv, mv, maskb[:].unsqueeze(1).to_broadcast([P, NT, P]),
                                        ALU.add).then_inc(masked, 1)
                if last:
                    pool.wait_ge(g1_in, 16)
                    scale_unit(U_OUT)
                    scale_unit(U_OUT + 1, (0,))
                pool.wait_ge(qk_ev, h * 4 + 4)
                pool.wait_ge(si_in, h * 16 + 16)
                for c in range(NT + 1):
                    if 1 <= c < NT:
                        if c >= 2:
                            pool.wait_ge(o_mm, h * NT + c - 1)
                        elif not first:
                            pool.wait_ge(o_mm, h * NT)
                        nc.gpsimd.tensor_tensor(qs[:, c % 2, :], qT[:, c * P:(c + 1) * P],
                                                sI[:, c * P:(c + 1) * P], ALU.mult).then_inc(qs_ok, 1)
                    if last and c == 7:
                        head_norm(0)
                    if 1 <= c:
                        pool.wait_ge(hc_ok, h * NT + c)
                        pool.wait_ge(gate_ok, h * NT + c)
                        dst = (hg[:, c - 1, 0:DV] if first else hg[:, c - 1, bass.ds(h * DV, DV)])
                        nc.gpsimd.tensor_tensor(dst, hc[:, (c - 1) % 2, :], gate[:, (c - 1) % 2, :],
                                                ALU.mult).then_inc(hg_ok, 1)
                    if last and c == 7:
                        head_norm(1)
                    if last and c == 2:
                        scale_unit(U_OUT + 1, (1,))
                    if last and c == 5:
                        scale_unit(U_OUT + 2, (0,))

            head(0, True)
            with pool.Fori(1, NH - 1) as h:
                head(h, False)
            head(NH - 1, False, True)

            head_norm(3)
            scale_unit(U_OUT + 2, (1,))
            for t in range(5, NT, 2):
                head_norm(t)
            pool.wait_ge(mod_out, 16 * 2 * NH)
            pool.wait_ge(og_tr, 2 * NT)
            to_all(sh2, 2, sh2_in)
            to_all(sc2, 4, sc2_in)
            scale_unit(U_OUT + 3)
            pool.wait_ge(sh2_in, 16)
            for t in range(NT - 2):
                pool.wait_ge(n_hn, NT + t + 1)
                nc.gpsimd.tensor_tensor(hn2[:, t % 4, :], hn2[:, t % 4, :], sh2[:], ALU.add).then_inc(n_sh, 1)
            pool.wait_ge(n_tr, 4 * NT)
            pool.dma_start(fw[:], final_w.to_broadcast([P, D])).then_inc(fw_in, 16)
            to_all(gb, 6, g2_in)
            pool.wait_ge(g2_in, 16)

            def scale_down(u):
                for i in range(2):
                    pool.wait_ge(raw_in[i], u * 16 + 16)
                    nc.gpsimd.tensor_tensor(piece(raw, i), piece(raw, i), gb[:], ALU.mult).then_inc(w_scaled, 1)

            scale_down(U_FF + 3)
            with pool.Fori(1, NG - 1) as g:
                scale_down(g * 3 + U_FF + 3)
            scale_down(NU - 1)
            pool.wait_ge(fw_in, 16)
            for n, t in enumerate(POOL_HALF):
                i = 2 * NT + t
                v = x2[:, t, HALF:]
                pool.wait_ge(n_rstd, i + 1)
                nc.gpsimd.tensor_scalar(v, v, rstd[:, i:i + 1], None, ALU.mult).then_inc(f_half, 1)
                pool.wait_ge(f_half, n + 1)
                nc.gpsimd.tensor_tensor(v, v, fw[:, HALF:], ALU.mult).then_inc(f_out[1], 1)

        @block.scalar
        def _(act):
            def split_H(u, k, free=None, pieces=(0, 1), scaled=None):
                for i in pieces:
                    act.wait_ge(raw_in[i], u * 16 + 16)
                    if scaled is not None:
                        act.wait_ge(w_scaled, scaled * 2 - 1 + i)
                    if i == 0 and free is not None:
                        act.wait_ge(*free)
                    nc.scalar.copy(piece(wH[:, slot(k), :], i), piece(raw, i)).then_inc(w_H, 1)

            act.wait_ge(c_in, 16)
            nc.scalar.activation(cact[:], craw[:], ACT.Silu).then_inc(c_act, 1)

            def square(i, src):
                nc.scalar.activation(junk[:], src, ACT.Square, accum_out=ms[:, i:i + 1]).then_inc(n_ms, 1)

            def root(i):
                act.wait_ge(n_var, i + 1)
                nc.scalar.activation(sd[:, i:i + 1], var[:, i:i + 1], ACT.Sqrt).then_inc(n_sd, 1)

            def evac_xT(t, j=0):
                act.wait_ge(n_tr, 2 * t + j + 1)
                nc.scalar.copy(xnT[:, 4 * j:4 * j + 4, t * P:(t + 1) * P],
                               XT_BANKS[2 * (t % 2) + j][:].rearrange("p (k n) -> p k n", n=P)).then_inc(xT_ok[j], 1)

            def mod_columns(k):
                act.wait_ge(mod1_mm, k + 1)
                for m in range(2):
                    col = slice(2 * k + m, 2 * k + m + 1)
                    nc.scalar.activation(mod1[:, col], MOD_BANKS[k % 2][:, col], ACT.Identity,
                                         bias=b1[:, col]).then_inc(mod1_ok, 1)

            def modulate(k, half):
                cols = slice(half * HALF, (half + 1) * HALF)
                if k == 0:
                    act.wait_ge(xT_ok[0], 4 * (half + 1))
                elif k == 4 and half == 0:
                    act.wait_ge(xT_ok[1], NT)
                act.wait_ge(mod1_ok, 2 * k + 2)
                nc.scalar.activation(xnT[:, k, cols], xnT[:, k, cols], ACT.Identity, scale=mod1[:, 2 * k:2 * k + 1],
                                     bias=mod1[:, 2 * k + 1:2 * k + 2]).then_inc(m_x, 1)
                act.wait_ge(m_x, 2 * k + half + 1)
                nc.scalar.copy(hH[:, k, cols], xnT[:, k, cols]).then_inc(m_H, 1)

            for t in range(NT):
                act.wait_ge(x_in[t], 16)
                if t:
                    act.wait_ge(n_ms, t)
                square(t, xin[:, t, :])
                if t >= 2:
                    evac_xT(t - 2)
                root(t)
                if t == 2:
                    act.wait_ge(b1_ok, 1)
                    mod_columns(0)
            modulate(0, 0)
            evac_xT(NT - 2)
            evac_xT(NT - 1)
            modulate(0, 1)
            act.wait_ge(xT_ok[1], NT - 2)
            evac_xT(NT - 2, 1)
            evac_xT(NT - 1, 1)
            for k in range(1, KD):
                mod_columns(k)
                modulate(k, 0)
                modulate(k, 1)
                if k in (1, 6, 7):
                    split_H(k // 6, k // 6, pieces=(0 if k == 6 else 1,))

            def evac_qk(h, i):
                act.wait_ge(qk_mm, h * 4 + i + 1)
                dst = (qT if i % 2 == 0 else kT)[:, (i // 2) * HALF:(i // 2 + 1) * HALF]
                nc.scalar.activation(dst, QK_BANKS[i][:], ACT.Copy,
                                     scale=1.0 if i % 2 == 0 else float(DK) ** -0.5).then_inc(qk_ev, 1)

            def gates_scalar():
                act.wait_ge(b15_ok, 1)
                for j in range(2):
                    act.wait_ge(gates_mm, j + 1)
                    nc.scalar.copy(rows[0:GATE_ROWS, SI, j * HALF:(j + 1) * HALF],
                                   OP[j][64:64 + GATE_ROWS, :]).then_inc(g_part, 1)
                for j in range(2):
                    act.wait_ge(g_sum, j + 1)
                    t = rows[0:GATE_ROWS, T_, j * HALF:(j + 1) * HALF]
                    nc.scalar.activation(t, t, ACT.Tanh, bias=bcol15[0:GATE_ROWS, :],
                                         scale=1.0 / CAP).then_inc(g_act, 1)
                act.wait_ge(g_act, 2)
                nc.scalar.activation(row(NL), row(T_, 32, 32 + NH), ACT.Exp, scale=-CAP).then_inc(g_act, 1)
                act.wait_ge(g_act, 3)
                nc.scalar.activation(row(NL), row(NL), ACT.Ln, bias=1.0).then_inc(g_act, 1)

            def head_root(b):
                act.wait_ge(h_var, b + 1)
                nc.scalar.activation(four(hsd, 4 * b), four(hvar, 4 * b), ACT.Sqrt).then_inc(h_sd, 1)

            def og_high(t):
                for j in range(2):
                    act.wait_ge(og_tr, 2 * t + j + 1)
                    nc.scalar.copy(hH[:, 4 * j:4 * j + 4, t * P:(t + 1) * P],
                                   og_banks(t)[j][:].rearrange("p (k n) -> p k n", n=P)).then_inc(og_H, 1)

            def head(h, first, last=False):
                if first:
                    gates_scalar()
                else:
                    for i in range(4):
                        if i == 0:
                            act.wait_ge(o_mm, h * NT)
                            act.wait_ge(st_mm, h * NT)
                            act.wait_ge(qs_ok, h * (NT - 1))
                        evac_qk(h, i)
                        if i == 0:
                            split_H(h * 3 + 2, 2, (op_mm, h * NT))
                for t in range(NT):
                    if not first or t >= 2:
                        act.wait_ge(v_mm, h * NT + t + 1)
                        if first and t == 2:
                            act.wait_ge(v_ev, 2)
                        nc.scalar.copy(va[:, t, 0:DV], OP[t % 2][:, 0:DV]).then_inc(v_ev, 1)
                    if first and t < 4:
                        evac_qk(h, t)
                    if first and t == 2:
                        act.wait_ge(g_dve, 6)
                        nc.scalar.activation(row(SI), row(SI), ACT.Exp).then_inc(g_act, 1)
                    if t == 1 and not first:
                        split_H(h * 3 + 3, 0, (qk_mm, h * 4 + 4), scaled=1 if last else None)
                    if t == 3 and first:
                        split_H(2, 2, (gates_mm, 2))
                    if t == 6 and first:
                        act.wait_ge(rT_cp, 2)
                        nc.scalar.activation(thr[:], tT[:], ACT.Exp).then_inc(thr_ok, 1)
                act.wait_ge(masked, h + 1)

                def decay(c):
                    if c >= 2:
                        act.wait_ge(kwpt, h * NT + c - 1)
                    elif not first:
                        act.wait_ge(kwpt, h * NT)
                    col = aT[:, c:c + 1] if first else aT[:, bass.ds(h * NT + c, 1)]
                    nc.scalar.activation(E[:, c % 2, :], Mb[:, c * P:(c + 1) * P], ACT.Exp, scale=-1.0,
                                         bias=col).then_inc(e_ok, 1)

                def squares(c):
                    act.wait_ge(hc_ok, h * NT + c + 1)
                    if not (first and c == 0):
                        act.wait_ge(hms_ok, h * NT + c)
                    col = hms[:, c:c + 1] if first else hms[:, bass.ds(h * NT + c, 1)]
                    nc.scalar.activation(sqj[:], hc[:, c % 2, :], ACT.Square, accum_out=col).then_inc(hms_ok, 1)

                decay(0)
                for c in range(NT):
                    if c + 1 < NT:
                        decay(c + 1)
                    act.wait_ge(op_mm, h * NT + c + 1)
                    if c >= 2:
                        act.wait_ge(gate_ok, h * NT + c - 1)
                    elif not first:
                        act.wait_ge(gate_ok, h * NT)
                    nc.scalar.activation(th[:, c % 2, :], OP[c % 2][:, 0:DV], ACT.Tanh, scale=0.5).then_inc(th_ok, 1)
                    if c == 0 and first:
                        split_H(3, 0, (qk_mm, 4))
                    if c in (1, 3):
                        split_H(h * 3 + 4, 1, (v_mm, h * NT + NT), (c // 2,), 2 if last else None)
                    if c:
                        squares(c - 1)
                    if last and c == 5:
                        head_root(0)
                if last:
                    og_high(0)
                squares(NT - 1)

            head(0, True)
            with act.Fori(1, NH - 1) as h:
                head(h, False)
            head(NH - 1, False, True)

            head_root(1)
            for t in range(1, NT):
                og_high(t)
                if t == 4:
                    split_H(U_OUT + 2, 2, (op_mm, NH * NT), scaled=3)
            split_H(U_OUT + 3, 0, (y_mm, NT), scaled=4)
            split_H(U_FF, 1, (y_mm, 2 * NT))
            split_H(U_FF + 1, 2, (y_mm, 3 * NT))

            for t in range(NT + 3):
                if t < NT:
                    act.wait_ge(y_ev, 3 * NT + t + 1)
                    act.wait_ge(n_ms, NT + t)
                    square(NT + t, x2[:, t, :])
                    root(NT + t)
                for j in range(2):
                    if t >= 3:
                        act.wait_ge(n_tr, 2 * (NT + t - 3) + j + 1)
                        nc.scalar.copy(hH[:, 4 * j:4 * j + 4, (t - 3) * P:(t - 2) * P],
                                       n2_banks(t - 3)[j][:].rearrange("p (k n) -> p k n", n=P)).then_inc(n_H, 1)

            def silu(f_count, half):
                n = f_count * 2 + half
                act.wait_ge(gu_mm, n * 2 + 1)
                if not isinstance(n, int) or n >= 2:
                    act.wait_ge(st_ok, n - 1)
                nc.scalar.activation(sg[:, half, :], GU_BANKS[2 * half][:], ACT.Silu).then_inc(sg_ok, 1)

            def act_high(f_count, f, half):
                n = f_count * 2 + half
                act.wait_ge(st_ok, n + 1)
                nc.scalar.copy(actH[:, f, half * HALF:(half + 1) * HALF],
                               stage[:, f, half * HALF:(half + 1) * HALF]).then_inc(a_H, 1)

            act.wait_ge(n_sh, NT)
            split_H(U_FF + 2, 0, (y_mm, 4 * NT))
            for half in range(2):
                silu(0, half)
                act_high(0, 0, half)
            split_H(U_FF + 3, 1, (gu_mm, 4), scaled=5)
            for half in range(2):
                silu(1, half)
                act_high(1, 1, half)

            def group(g, last):
                u = g * 3 + (U_FF - 1)
                split_H(u + 2, 2, (gu_mm, g * 8))
                for half in range(2):
                    silu(g * 2, half)
                split_H(u + 3, 0, (gu_mm, g * 8 + 4), scaled=NG + 4 if last else None)
                act.wait_ge(d_mm, g * 16)
                for half in range(2):
                    act_high(g * 2, 0, half)
                if not last:
                    split_H(u + 4, 1, (d_mm, g * 16), scaled=g + 5)
                for half in range(2):
                    silu(g * 2 + 1, half)
                    act_high(g * 2 + 1, 1, half)

            with act.Fori(1, NG - 1) as g:
                group(g, False)
            group(NG - 1, True)
            for t in range(NT):
                i = 2 * NT + t
                act.wait_ge(d_ev, 16 * (NG - 1) + 2 * t + 2)
                act.wait_ge(n_ms, i)
                square(i, x2[:, t, :])
                root(i)

        @block.vector
        def _(dve):
            def split_L(u, k, pieces=(0, 1)):
                for i in pieces:
                    dve.wait_ge(w_H, u * 2 + i + 1)
                    nc.vector.tensor_tensor(piece(wL[:, slot(k), :], i), piece(raw, i),
                                            piece(wH[:, slot(k), :], i).bitcast(F32), ALU.subtract).then_inc(w_L, 1)

            nc.vector.memset(wH[:, 2, 0:KD * P].bitcast(F32), 0.0).then_inc(wg_zero, 1)

            def sum1(k, r0=0, r1=N1):
                even, odd = (acc0[:, k % 2, i, :] for i in range(2))
                for r in range(r0, r1):
                    acc1 = (even, odd)[r % 2]
                    if r == 0:
                        dve.wait_ge(ada0_in[k % 4], 16 * (k // 4 + 1))
                        if k >= 2:
                            dve.wait_ge(mod1_mm, k - 1)
                    if r == KD:
                        dve.wait_ge(acc0_ok, k * N1 + r)
                        nc.vector.tensor_tensor(even, even, odd, ALU.add).then_inc(acc0_ok, 1)
                    elif r < 2:
                        nc.vector.tensor_scalar(acc1, ada0[:, k % 4, r, :], cact[:, r:r + 1], None,
                                                ALU.mult).then_inc(acc0_ok, 1)
                    else:
                        dve.wait_ge(acc0_ok, k * N1 + r - 1)
                        nc.vector.scalar_tensor_tensor(acc1, ada0[:, k % 4, r, :], cact[:, r:r + 1], acc1,
                                                       ALU.mult, ALU.add).then_inc(acc0_ok, 1)

            def variance(i):
                dve.wait_ge(n_ms, i + 1)
                nc.vector.tensor_scalar(var[:, i:i + 1], ms[:, i:i + 1], 1.0 / D, EPS, ALU.mult,
                                        ALU.add).then_inc(n_var, 1)

            def inverse(i):
                dve.wait_ge(n_sd, i + 1)
                nc.vector.reciprocal(rstd[:, i:i + 1], sd[:, i:i + 1]).then_inc(n_rstd, 1)
                dve.wait_ge(n_rstd, i + 1)

            def low(t):
                for j in range(2):
                    dve.wait_ge(n_H, 2 * t + j + 1)
                    cols = slice(t * P, (t + 1) * P)
                    nc.vector.tensor_tensor(hL[:, 4 * j:4 * j + 4, cols],
                                            n2_banks(t)[j][:].rearrange("p (k n) -> p k n", n=P),
                                            hH[:, 4 * j:4 * j + 4, cols].bitcast(F32), ALU.subtract).then_inc(n_L, 1)

            def norm1(t):
                inverse(t)
                nc.vector.tensor_scalar(xin[:, t, :], xin[:, t, :], rstd[:, t:t + 1], None, ALU.mult).then_inc(n_hn, 1)

            def evac_xT(t):
                dve.wait_ge(n_tr, 2 * t + 2)
                nc.vector.tensor_copy(xnT[:, 4:8, t * P:(t + 1) * P],
                                      XT_BANKS[2 * (t % 2) + 1][:].rearrange("p (k n) -> p k n",
                                                                             n=P)).then_inc(xT_ok[1], 1)

            def low1(k, half):
                cols = slice(half * HALF, (half + 1) * HALF)
                dve.wait_ge(m_H, 2 * k + half + 1)
                nc.vector.tensor_tensor(hL[:, k, cols], xnT[:, k, cols], hH[:, k, cols].bitcast(F32),
                                        ALU.subtract).then_inc(m_L, 1)

            dve.wait_ge(b1_in, 16)
            b1_scale = b1[:].rearrange("p (k m) -> p k m", m=2)[:, :, 0:1]
            nc.vector.tensor_scalar(b1_scale, b1_scale, 1.0, None, ALU.add).then_inc(b1_ok, 1)
            dve.wait_ge(c_act, 1)
            sum1(0)
            for t in range(NT):
                variance(t)
                if t >= 2:
                    evac_xT(t - 2)
                norm1(t)
                if t == NT - 1:
                    low1(0, 0)
            for k in range(1, KD):
                sum1(k)
                if k == 3:
                    split_L(0, 0, pieces=(1,))
            dve.wait_ge(bif_in, 32)
            nc.vector.tensor_scalar(bcol15[:], bcol[:], 1.0 / CAP, None, ALU.mult).then_inc(b15_ok, 1)
            split_L(1, 1)

            def gates_rows():
                for j in range(2):
                    dve.wait_ge(g_part, j + 1)
                    cols = slice(j * HALF, (j + 1) * HALF)
                    nc.vector.tensor_tensor(rows[0:GATE_ROWS, T_, cols], OP[j][0:GATE_ROWS, :],
                                            rows[0:GATE_ROWS, SI, cols], ALU.add).then_inc(g_sum, 1)
                for t in range(2):
                    dve.wait_ge(v_mm, t + 1)
                    nc.vector.tensor_copy(va[:, t, 0:DV], OP[t][:, 0:DV]).then_inc(v_ev, 1)
                dve.wait_ge(g_act, 4)
                dve.wait_ge(rows_set, 4)
                nc.vector.tensor_tensor_scan(row(NB), row(MR), row(NL), 0.0, ALU.mult, ALU.add).then_inc(g_dve, 1)
                dve.wait_ge(g_dve, 1)
                nc.vector.scalar_tensor_tensor(row(A_), row(T_), CAP, row(NB), ALU.mult, ALU.add).then_inc(g_dve, 1)
                nc.vector.tensor_scalar(rows[0:NH, DD, P:S:P], rows[0:NH, NB, P - 1:S - 1:P], -1.0, None,
                                        ALU.mult).then_inc(g_dve, 1)
                dve.wait_ge(g_dve, 3)
                nc.vector.tensor_tensor_scan(row(M_), row(DD), row(A_), 0.0, ALU.add, ALU.max).then_inc(g_dve, 1)
                nc.vector.memset(mp[0:NH, 0:1], 0.0).then_inc(g_dve, 1)
                dve.wait_ge(g_dve, 5)
                nc.vector.tensor_tensor(mp[0:NH, 1:NT], rows[0:NH, M_, P - 1:S - 1:P], rows[0:NH, DD, P:S:P],
                                        ALU.add).then_inc(rT_cp, 1)
                dve.wait_ge(rT_cp, 1)
                nc.vector.tensor_tensor(row(SI).rearrange("p (c l) -> p c l", l=P),
                                        mp[0:NH, :].unsqueeze(2).to_broadcast([NH, NT, P]),
                                        row(M_).rearrange("p (c l) -> p c l", l=P), ALU.subtract).then_inc(g_dve, 1)
                nc.vector.tensor_tensor(row(A_, 32, 32 + NH), row(NB), row(M_), ALU.subtract).then_inc(g_dve, 1)

            def gates_columns():
                dve.wait_ge(rT_mm, 1)
                for n, t in enumerate((aT, tT)):
                    ins = nc.vector.tensor_copy(t[:].rearrange("p (h c) -> p c h", h=NH),
                                                AD[:, 0:NT * GATE_ROWS].rearrange("p (c r) -> p c r", r=GATE_ROWS)
                                                [:, :, 32 * n:32 * n + NH])
                ins.then_inc(rT_cp, 1)

            def mod_row(n):
                dve.wait_ge(ad_mm, n + 1)
                dve.wait_ge(brow_in, n * 16 + 16)
                if not (isinstance(n, int) and n == 0):
                    dve.wait_ge(mod_out, n * 16)
                nc.vector.tensor_tensor(adarow[0:1, :], AD[0:1, :], brow[0:1, :], ALU.add).then_inc(ad_ev, 1)

            def head_var(b):
                dve.wait_ge(hms_ok, (NH - 1) * NT + 4 * b + 4)
                nc.vector.tensor_scalar(four(hvar, 4 * b), four(hms, 4 * b), 1.0 / DV, EPS, ALU.mult,
                                        ALU.add).then_inc(h_var, 1)

            def head_rstd(b):
                dve.wait_ge(h_sd, b + 1)
                nc.vector.reciprocal(four(hsd, 4 * b), four(hsd, 4 * b)).then_inc(h_rs, 1)
                dve.wait_ge(h_rs, 2 * b + 1)
                nc.vector.tensor_scalar(four(hrs, 4 * b), four(hsd, 4 * b), 0.5, None, ALU.mult).then_inc(h_rs, 1)

            def head_norm(t):
                dve.wait_ge(h_rs, 2 * (t // 4) + 2)
                dve.wait_ge(hg_ok, (NH - 1) * NT + t + 1)
                hv = hg[:, t, :].rearrange("p (h v) -> p h v", h=NH)
                rs = hrs[:].rearrange("p (h t) -> p t h", t=NT)[:, t, :]
                nc.vector.tensor_tensor(hv, hv, rs.unsqueeze(2).to_broadcast([P, NH, DV]), ALU.mult).then_inc(og_n[0], 1)

            def og_low(t):
                for j in range(2):
                    dve.wait_ge(og_H, 2 * t + j + 1)
                    cols = slice(t * P, (t + 1) * P)
                    nc.vector.tensor_tensor(hL[:, 4 * j:4 * j + 4, cols],
                                            og_banks(t)[j][:].rearrange("p (k n) -> p k n", n=P),
                                            hH[:, 4 * j:4 * j + 4, cols].bitcast(F32), ALU.subtract).then_inc(og_L, 1)

            def head(h, first, last=False):
                if first:
                    nc.vector.memset(va[:, :, DV:DV + 1], 1.0).then_inc(v_one, 1)
                    gates_rows()
                    split_L(2, 2)
                    gates_columns()
                    dve.wait_ge(thr_ok, 1)
                else:
                    split_L(h * 3 + 2, 2)
                    split_L(h * 3 + 3, 0)
                    mod_row(h * 2 - 1)

                def weighted(c):
                    n = h * NT + c
                    dve.wait_ge(st_mm, n + 1)
                    dve.wait_ge(e_ok, n + 1)
                    if c >= 2:
                        dve.wait_ge(o_mm, n - 1)
                        dve.wait_ge(dc_mm, h * (NT - 1) + c - 1)
                    elif not first:
                        dve.wait_ge(o_mm, h * NT)
                        dve.wait_ge(dc_mm, h * (NT - 1))
                    nc.vector.tensor_scalar(kw[:, c % 2, :], ST[c % 2][:, P:2 * P], E[:, c % 2, P - 1:P], None, ALU.mult)
                    nc.vector.tensor_tensor(PT[:, c % 2, :], ST[c % 2][:, 0:P], E[:, c % 2, :],
                                            ALU.mult).then_inc(kwpt, 1)

                def state(c):
                    dve.wait_ge(dc_mm, h * (NT - 1) + c + 1)
                    if c == 0:
                        if not first:
                            dve.wait_ge(o_mm, h * NT)
                        nc.vector.tensor_copy(C[:], DC[:, 0:DV + 1]).then_inc(c_ok, 1)
                    else:
                        if c == 1:
                            dve.wait_ge(si_in, h * 16 + 16)
                        dve.wait_ge(c_ok, h * (NT - 1) + c)
                        e = (c + 1) * P - 1
                        nc.vector.scalar_tensor_tensor(C[:], C[:], sI[:, e:e + 1], DC[:, 0:DV + 1], ALU.mult,
                                                       ALU.add).then_inc(c_ok, 1)

                def divide(c):
                    n = h * NT + c
                    dve.wait_ge(o_mm, n + 1)
                    col = thr[:, c:c + 1] if first else thr[:, bass.ds(h * NT + c, 1)]
                    d = den[:, c % 2:c % 2 + 1]
                    nc.vector.tensor_scalar(d, O[c % 2][:, DV:DV + 1], -1.0, col, ALU.mult,
                                            ALU.max).then_inc(den_ok, 1)
                    dve.wait_ge(den_ok, n * 2 + 1)
                    nc.vector.tensor_scalar(d, O[c % 2][:, DV:DV + 1], d, None, ALU.max).then_inc(den_ok, 1)
                    dve.wait_ge(den_ok, n * 2 + 2)
                    nc.vector.reciprocal(rden[:, c % 2:c % 2 + 1], den[:, c % 2:c % 2 + 1]).then_inc(rden_ok, 1)
                    dve.wait_ge(rden_ok, n + 1)
                    if c >= 2:
                        dve.wait_ge(hg_ok, n - 1)
                        dve.wait_ge(hms_ok, n - 1)
                    elif not first:
                        dve.wait_ge(hg_ok, h * NT)
                        dve.wait_ge(hms_ok, h * NT)
                    nc.vector.tensor_scalar(hc[:, c % 2, :], O[c % 2][:, 0:DV], rden[:, c % 2:c % 2 + 1], None,
                                            ALU.mult).then_inc(hc_ok, 1)

                def gating(c):
                    n = h * NT + c
                    dve.wait_ge(th_ok, n + 1)
                    if c == 0:
                        dve.wait_ge(nw_in, h * 16 + 16)
                    if c >= 2:
                        dve.wait_ge(hg_ok, n - 1)
                    elif not first:
                        dve.wait_ge(hg_ok, h * NT)
                    nc.vector.scalar_tensor_tensor(gate[:, c % 2, :], th[:, c % 2, :], 1.0, nwb[:], ALU.add,
                                                   ALU.mult).then_inc(gate_ok, 1)

                def ada_item(i):
                    n = h * 16 + i
                    dve.wait_ge(ada_in[i % 2], h * 128 + (i // 2) * 16 + 16)
                    k = i % KD
                    if not (first and i == 0):
                        dve.wait_ge(acc_ok, n)
                    if k == 0:
                        if not (first and i == 0):
                            dve.wait_ge(ad_mm, h * 2 + i // KD)
                        nc.vector.tensor_scalar(acc[:], ada[:, i % 2, :], cact[:, 0:1], None,
                                                ALU.mult).then_inc(acc_ok, 1)
                    else:
                        nc.vector.scalar_tensor_tensor(acc[:], ada[:, i % 2, :], cact[:, k:k + 1], acc[:],
                                                       ALU.mult, ALU.add).then_inc(acc_ok, 1)

                for c in range(NT + 1):
                    if 1 <= c < NT:
                        state(c - 1)
                    if c < NT:
                        weighted(c)
                    if last and c == 6:
                        head_rstd(0)
                    if c:
                        divide(c - 1)
                        gating(c - 1)
                    if first and c < 2:
                        split_L(h * 3 + 3, 0, (c,))
                    if c == 5:
                        mod_row(h * 2)
                    if c < NT:
                        ada_item(2 * c)
                        ada_item(2 * c + 1)
                    if c in (2, 4):
                        split_L(h * 3 + 4, 1, pieces=(c // 2 - 1,))
                    if last:
                        if c == 5:
                            head_var(0)
                if last:
                    og_low(0)

            head(0, True)
            with dve.Fori(1, NH - 1) as h:
                head(h, False)
            head(NH - 1, False, True)

            def y_tile(n):
                j, t = divmod(n, NT)
                if j == 0 and t % 2 == 0:
                    dve.wait_ge(x2_in[t // 2], 16)
                dve.wait_ge(y_mm, n + 1)
                cols = slice(j * DV, (j + 1) * DV)
                nc.vector.tensor_tensor(x2[:, t, cols], x2[:, t, cols], Y_BANKS[n % 4][:, 0:DV],
                                        ALU.add).then_inc(y_ev, 1)

            head_norm(2)
            head_var(1)
            og_low(1)
            mod_row(2 * NH - 1)
            head_rstd(1)
            y_tile(0)
            for t in range(2, NT):
                og_low(t)
                y_tile(t - 1)
                if t % 2 == 0 and t + 2 < NT:
                    head_norm(t + 2)
                if t == 5:
                    split_L(U_OUT + 2, 2)
            y_tile(NT - 1)
            split_L(U_OUT + 3, 0)
            for n in range(NT, 2 * NT):
                y_tile(n)
            split_L(U_FF, 1)
            dve.wait_ge(sc2_in, 16)
            nc.vector.tensor_scalar(sc2[:], sc2[:], 1.0, None, ALU.add).then_inc(sc2_ok, 1)
            for n in range(2 * NT, 3 * NT):
                y_tile(n)
            split_L(U_FF + 1, 2)
            dve.wait_ge(sc2_ok, 1)
            dve.wait_ge(sh2_in, 16)
            for t in range(NT + 3):
                i = NT + t - 1
                if 1 <= t <= NT:
                    dve.wait_ge(n_sd, i + 1)
                    nc.vector.reciprocal(rstd[:, i:i + 1], sd[:, i:i + 1]).then_inc(n_rstd, 1)
                if t < NT:
                    y_tile(3 * NT + t)
                if 1 <= t <= NT:
                    dve.wait_ge(n_rstd, i + 1)
                    if t >= 5:
                        dve.wait_ge(n_tr, 2 * (i - 3))
                    nc.vector.scalar_tensor_tensor(hn2[:, (t - 1) % 4, :], x2[:, t - 1, :], rstd[:, i:i + 1], sc2[:],
                                                   ALU.mult, ALU.mult).then_inc(n_hn, 1)
                    if t >= NT - 1:
                        dve.wait_ge(n_hn, i + 1)
                        dve.wait_ge(n_sh, t - 1)
                        nc.vector.tensor_tensor(hn2[:, (t - 1) % 4, :], hn2[:, (t - 1) % 4, :], sh2[:],
                                                ALU.add).then_inc(n_sh, 1)
                if t < NT:
                    variance(NT + t)
                if t >= 3:
                    low(t - 3)

            def product(f_count, f, half):
                n = f_count * 2 + half
                dve.wait_ge(sg_ok, n + 1)
                dve.wait_ge(gu_mm, n * 2 + 2)
                if not isinstance(n, int) or n >= 4:
                    dve.wait_ge(a_L, n - 3)
                nc.vector.tensor_tensor(stage[:, f, half * HALF:(half + 1) * HALF], sg[:, half, :],
                                        GU_BANKS[2 * half + 1][:], ALU.mult).then_inc(st_ok, 1)

            def act_low(f_count, f, half):
                n = f_count * 2 + half
                dve.wait_ge(a_H, n + 1)
                cols = slice(half * HALF, (half + 1) * HALF)
                nc.vector.tensor_tensor(actL[:, f, cols], stage[:, f, cols], actH[:, f, cols].bitcast(F32),
                                        ALU.subtract).then_inc(a_L, 1)

            def add_down(g, lo, hi):
                for n in range(lo, hi):
                    dve.wait_ge(d_mm, g * 16 + n + 1)
                    t, j = divmod(n, 2)
                    cols = slice(j * HALF, (j + 1) * HALF)
                    nc.vector.tensor_tensor(x2[:, t, cols], x2[:, t, cols], Y_BANKS[n % 4][:],
                                            ALU.add).then_inc(d_ev, 1)

            split_L(U_FF + 2, 0)
            for half in range(2):
                product(0, 0, half)
                act_low(0, 0, half)
            split_L(U_FF + 3, 1)
            for half in range(2):
                product(1, 1, half)
                act_low(1, 1, half)

            def group(g, last):
                u = g * 3 + (U_FF - 1)
                split_L(u + 2, 2)
                for half in range(2):
                    product(g * 2, 0, half)
                add_down(g - 1, 0, 4)
                split_L(u + 3, 0)
                add_down(g - 1, 4, 16)
                for half in range(2):
                    act_low(g * 2, 0, half)
                if not last:
                    split_L(u + 4, 1)
                for half in range(2):
                    product(g * 2 + 1, 1, half)
                    act_low(g * 2 + 1, 1, half)

            with dve.Fori(1, NG - 1) as g:
                group(g, False)
            group(NG - 1, True)
            dve.wait_ge(fw_in, 16)

            def finish(t):
                i = 2 * NT + t
                dve.wait_ge(n_sd, i + 1)
                nc.vector.reciprocal(rstd[:, i:i + 1], sd[:, i:i + 1]).then_inc(n_rstd, 1)
                dve.wait_ge(n_rstd, i + 1)
                for half in range(1 if t in POOL_HALF else 2):
                    cols = slice(half * HALF, (half + 1) * HALF)
                    nc.vector.scalar_tensor_tensor(x2[:, t, cols], x2[:, t, cols], rstd[:, i:i + 1], fw[:, cols],
                                                   ALU.mult, ALU.mult).then_inc(f_out[0], 1)

            for t in range(NT):
                add_down(NG - 1, 2 * t, 2 * t + 1)
                if t:
                    variance(2 * NT + t - 1)
                add_down(NG - 1, 2 * t + 1, 2 * t + 2)
                if t:
                    finish(t - 1)
            variance(3 * NT - 1)
            finish(NT - 1)

        @block.tensor
        def _(pe):
            def three(out_ap, lhs, rhs, k0, n, last):
                for i, (a, b) in enumerate(((0, 0), (0, 1), (1, 0))):
                    ins = nc.tensor.matmul(out_ap, lhs[a], rhs[b], start=(n == 0 and i == 0), stop=(last and i == 2))
                return ins

            def project(out_ap, lhs, rhs):
                for k in range(KD):
                    ins = three(out_ap, lhs(k), rhs(k), k, k, k == KD - 1)
                return ins

            def h_cols(half):
                return lambda k: tuple(h[:, k, half * HALF:(half + 1) * HALF] for h in (hH, hL))

            def h_tile(t):
                return lambda k: tuple(h[:, k, t * P:(t + 1) * P] for h in (hH, hL))

            def transposes2(t):
                pe.wait_ge(n_sh, t + 1)
                if t == 5:
                    pe.wait_ge(y_ev, 3 * NT + 6)
                for j in range(2):
                    if t and t != 5:
                        pe.wait_ge(n_L, 2 * (t - 1 if t < 5 else t - 2) + j + 1)
                    for k in range(4):
                        ins = nc.tensor.transpose(n2_banks(t)[j][:, k * P:(k + 1) * P],
                                                  hn2[:, t % 4, (4 * j + k) * P:(4 * j + k + 1) * P], ident[:])
                    ins.then_inc(n_tr, 1)

            def mod_columns(k):
                pe.wait_ge(acc0_ok, N1 * (k + 1))
                for m in range(2):
                    ins = nc.tensor.matmul(MOD_BANKS[k % 2][:, 2 * k + m:2 * k + m + 1],
                                           acc0[:, k % 2, 0, m * P:(m + 1) * P], ones[:, 0:1], start=True, stop=True)
                ins.then_inc(mod1_mm, 1)

            def start():
                pe.wait_ge(ones_ok, 1)
                mod_columns(0)
                pe.wait_ge(const_ok, 2)
                for t in range(NT):
                    pe.wait_ge(n_hn, t + 1)
                    for j in range(2):
                        if t >= 2:
                            pe.wait_ge(xT_ok[j], t - 1)
                        for k in range(4):
                            ins = nc.tensor.transpose(XT_BANKS[2 * (t % 2) + j][:, k * P:(k + 1) * P],
                                                      xin[:, t, (4 * j + k) * P:(4 * j + k + 1) * P], ident[:])
                        ins.then_inc(n_tr, 1)
                pe.wait_ge(wg_L, 1)
                ws = unit_weights(0, 2 * DK)
                for k in range(KD):
                    if k % 4 == 0:
                        pe.wait_ge(w_L, k // 4 + 1)
                    if 0 < k < KD - 1:
                        mod_columns(k + 1)
                    for half in range(2):
                        pe.wait_ge(m_L, 2 * k + half + 1)
                        if k == 0:
                            pe.wait_ge(xT_ok[half], NT)
                        hs = h_cols(half)(k)
                        last = k == KD - 1
                        for m in range(2):
                            ins = three(QK_BANKS[2 * half + m][:], tuple(w[:, k, m * DK:(m + 1) * DK] for w in ws),
                                        hs, k, k, last)
                            if last:
                                ins.then_inc(qk_mm, 1)
                        for i in range(2):
                            ins = nc.tensor.matmul(OP[half][:], gate_weights[:, k, :], hs[i], start=(k == 0 and i == 0),
                                                   stop=(last and i == 1))
                        if last:
                            ins.then_inc(gates_mm, 1)
                        if k == 0 and half == 0:
                            mod_columns(1)

            def qk(h, i):
                ws = unit_weights(0, 2 * DK)
                m = i % 2
                project(QK_BANKS[i][:], lambda k: tuple(w[:, k, m * DK:(m + 1) * DK] for w in ws),
                        h_cols(i // 2)).then_inc(qk_mm, 1)

            def row_transposes():
                pe.wait_ge(g_dve, 7)
                for c in range(NT):
                    ins = nc.tensor.transpose(AD[:, c * GATE_ROWS:(c + 1) * GATE_ROWS],
                                              rows[0:GATE_ROWS, A_, c * P:(c + 1) * P],
                                              ident[0:GATE_ROWS, 0:GATE_ROWS])
                ins.then_inc(rT_mm, 1)

            def ada_row(n):
                pe.wait_ge(acc_ok, n * KD + KD)
                if isinstance(n, int) and n == 0:
                    pe.wait_ge(rT_cp, 2)
                else:
                    pe.wait_ge(ad_ev, n)
                nc.tensor.matmul(AD[0:1, :], ones[:, 0:1], acc[:], start=True, stop=True).then_inc(ad_mm, 1)

            def out_transposes(t):
                if t and t % 2 == 0:
                    pe.wait_ge(og_n[0], t // 2)
                else:
                    pe.wait_ge(og_n[1], (t + 1) // 2 + 1)
                for j in range(2):
                    if t == 0:
                        pe.wait_ge(*((hc_ok, NH * NT - 1), (c_ok, NH * (NT - 1)))[j])
                    elif t == 1:
                        pe.wait_ge(kwpt, NH * NT)
                    elif t == 2 and j == 1:
                        pe.wait_ge(hc_ok, NH * NT)
                    else:
                        pe.wait_ge(og_L, 2 * (t - 2) + j + 1)
                    for k in range(4):
                        ins = nc.tensor.transpose(og_banks(t)[j][:, k * P:(k + 1) * P],
                                                  hg[:, t, (4 * j + k) * P:(4 * j + k + 1) * P], ident[:])
                    ins.then_inc(og_tr, 1)

            def head(h, first, last=False):
                if first:
                    start()
                else:
                    pe.wait_ge(w_L, h * 6 + 2)
                    for i in range(4):
                        pe.wait_ge((hc_ok, kwpt, kwpt, hc_ok)[i], h * NT - (1, 1, 0, 0)[i])
                        qk(h, i)
                    ada_row(h * 2 - 1)
                pe.wait_ge(w_L, h * 6 + 4)
                wv = unit_weights(1, DV)
                for t in range(NT):
                    if t >= 2:
                        pe.wait_ge(v_ev, h * NT + t - 1)
                    elif first:
                        pe.wait_ge(g_sum, t + 1)
                    else:
                        pe.wait_ge(th_ok, h * NT - 1 + t)
                    project(OP[t % 2][:, 0:DV], h_tile(t),
                            lambda k: tuple(w[:, k, :] for w in wv)).then_inc(v_mm, 1)
                    if first and t == 4:
                        row_transposes()
                pe.wait_ge(qk_ev, h * 4 + 4)
                if first:
                    pe.wait_ge(v_one, 1)
                pe.wait_ge(w_L, h * 6 + 6)
                wo = unit_weights(2, DV)
                for c in range(NT):
                    n = h * NT + c
                    toks = slice(c * P, (c + 1) * P)
                    if c >= 2:
                        pe.wait_ge(kwpt, n - 1)
                    nc.tensor.matmul(ST[c % 2][:, 0:P], kT[:, toks], qT[:, toks], start=True, stop=True)
                    nc.tensor.transpose(ST[c % 2][:, P:2 * P], kT[:, toks], ident[:]).then_inc(st_mm, 1)
                    if c >= 2:
                        pe.wait_ge(th_ok, n - 1)
                    else:
                        pe.wait_ge(v_ev, h * NT + NT - 1 + c)
                    project(OP[c % 2][:, 0:DV], h_tile(c),
                            lambda k: tuple(w[:, k, :] for w in wo)).then_inc(op_mm, 1)
                    if c == 4:
                        ada_row(h * 2)
                    if c == NT - 1 and last:
                        out_transposes(0)
                    pe.wait_ge(kwpt, n + 1)
                    if c == 0:
                        pe.wait_ge(v_ev, h * NT + NT)
                    if c >= 2:
                        pe.wait_ge(hc_ok, n - 1)
                    if c:
                        pe.wait_ge(qs_ok, h * (NT - 1) + c)
                        pe.wait_ge(c_ok, h * (NT - 1) + c)
                        nc.tensor.matmul(O[c % 2][:, 0:DV + 1], qs[:, c % 2, :], C[:], start=True, stop=False)
                    nc.tensor.matmul(O[c % 2][:, 0:DV + 1], PT[:, c % 2, :], va[:, c, :], start=(c == 0),
                                     stop=True).then_inc(o_mm, 1)
                    if c < NT - 1:
                        nc.tensor.matmul(DC[:, 0:DV + 1], kw[:, c % 2, :], va[:, c, :], start=True,
                                         stop=True).then_inc(dc_mm, 1)

            head(0, True)
            with pe.Fori(1, NH - 1) as h:
                head(h, False)
            head(NH - 1, False, True)

            def y_tile(n):
                j, t = divmod(n, NT)
                if t == 0:
                    pe.wait_ge(w_L, 2 * (U_OUT + j) + 2)
                if j == 0:
                    pe.wait_ge(og_L, 2 * t + 2)
                if n >= 4:
                    pe.wait_ge(y_ev, n - 3)
                else:
                    pe.wait_ge((th_ok, th_ok, c_ok, ad_ev)[n], (NH * NT, NH * NT, NH * (NT - 1), 2 * NH)[n])
                ws = unit_weights(j % 3, DV)
                project(Y_BANKS[n % 4][:, 0:DV], h_tile(t), lambda k: tuple(w[:, k, :] for w in ws)).then_inc(y_mm, 1)

            ada_row(2 * NH - 1)
            out_transposes(1)
            for t in range(NT):
                y_tile(t)
                if t + 2 < NT:
                    out_transposes(t + 2)
            for n in range(NT, 3 * NT):
                y_tile(n)
            for t in range(NT):
                y_tile(3 * NT + t)
                if t >= 3:
                    transposes2(t - 3)

            def gate_up(f_count, k, between=(None, None)):
                ws = unit_weights(k, 2 * P)
                for half in range(2):
                    n = f_count * 2 + half
                    for m in range(2):
                        if half == 0 and between[m]:
                            between[m]()
                        if not isinstance(n, int) or n >= 2:
                            pe.wait_ge((sg_ok, st_ok)[m], n - 1)
                        if isinstance(n, int) and n < 2:
                            pe.wait_ge(n_L, NT * (half + 1))
                        project(GU_BANKS[2 * half + m][:], lambda k: tuple(w[:, k, m * P:(m + 1) * P] for w in ws),
                                h_cols(half)).then_inc(gu_mm, 1)

            def down(g, k):
                pe.wait_ge(a_L, g * 4 + 3)
                ws = unit_weights(k, D)
                acts = (actH, actL)
                for n in range(16):
                    t, j = divmod(n, 2)
                    if n == 8:
                        pe.wait_ge(a_L, g * 4 + 4)
                    if isinstance(g, int) and g == 0 and n < 4:
                        pe.wait_ge(y_ev, 4 * NT)
                    else:
                        pe.wait_ge(d_ev, g * 16 + n - 3)
                    for f in range(2):
                        ins = three(Y_BANKS[n % 4][:], tuple(a[:, f, t * P:(t + 1) * P] for a in acts),
                                    tuple(w[:, f, j * HALF:(j + 1) * HALF] for w in ws), f, f, f == 1)
                    ins.then_inc(d_mm, 1)

            transposes2(NT - 3)
            pe.wait_ge(w_L, 2 * U_FF + 2)
            gate_up(0, 1, (lambda: None, lambda: (transposes2(NT - 2), transposes2(NT - 1))))
            pe.wait_ge(w_L, 2 * U_FF + 4)
            gate_up(1, 2)

            def group(g):
                u = g * 3 + (U_FF - 1)
                pe.wait_ge(w_L, u * 2 + 2)
                gate_up(g * 2, 0)
                pe.wait_ge(w_L, u * 2 + 4)
                down(g - 1, 1)
                pe.wait_ge(w_L, u * 2 + 6)
                gate_up(g * 2 + 1, 2)

            group(1)
            with pe.Fori(2, NG) as g:
                group(g)
            pe.wait_ge(w_L, 2 * NU)
            down(NG - 1, 0)


def kernel(x, c, ada_w, ada_b, ml_w_in, ml_b_if, ml_norm_w, ml_w_out, gdn_w_in, gdn_conv_w, gdn_a_log, gdn_dt_bias,
           gdn_norm_w, gdn_w_out, ffn_w_gate_up, ffn_w_down, final_norm_w):
    import numpy as np
    import concourse.bacc as bacc
    from concourse.bass_utils import run_bass_kernel_spmd

    def tiled(w):
        return np.asarray(w).reshape(-1, P, w.shape[1]).transpose(1, 0, 2)

    w_in, w_out, gate_up, down = (np.asarray(a)[0] for a in (ml_w_in, ml_w_out, ffn_w_gate_up, ffn_w_down))
    units = []
    for h in range(NH):
        q, k = (w_in[:, n * NH * DK + h * DK:n * NH * DK + (h + 1) * DK] for n in range(2))
        v, o = (w_in[:, D * (n + 1) + h * DV:D * (n + 1) + (h + 1) * DV] for n in range(2))
        units += [np.concatenate([tiled(q), tiled(k)], 2), tiled(v), tiled(o)]
    units += [tiled(w_out[:, j * DV:(j + 1) * DV]) for j in range(4)]

    def gu(f):
        return np.concatenate([tiled(gate_up[:, n * DFF + f * P:n * DFF + (f + 1) * P]) for n in range(2)], 2)

    for g in range(NG):
        units.append(gu(2 * g))
        if g:
            units.append(tiled(down[(g - 1) * 2 * P:g * 2 * P]))
        units.append(gu(2 * g + 1))
    units.append(tiled(down[(NG - 1) * 2 * P:]))
    w_units = np.stack([u.reshape(P, 2, D).transpose(1, 0, 2) for u in units])

    gates = w_in[:, 3 * D:]
    pad = np.zeros((D, 32 - NH), gates.dtype)
    w_gates = np.ascontiguousarray(tiled(np.concatenate([gates[:, :NH], pad, gates[:, NH:]], 1)))
    mods = np.asarray(ada_w)[0].reshape(D, 6, D).transpose(1, 0, 2)
    first = mods[[1, 0]].reshape(2, KD, P, KD, P).transpose(3, 2, 1, 0, 4).reshape(KD, P, KD, 2 * P)
    rest = np.stack([mods[m].reshape(KD, P, 2, HALF).transpose(2, 0, 1, 3) for m in range(2, 6)])
    b = np.asarray(ada_b)[0].reshape(6, D)
    arrays = {
        "x": np.asarray(x)[0].reshape(NT, P, D),
        "c_col": np.asarray(c)[0].reshape(KD, P).T,
        "ada_first": first,
        "ada_first_b": b[[1, 0]].reshape(2, KD, P).transpose(2, 1, 0).reshape(P, 2 * KD),
        "ada_rest": rest.reshape(8 * KD, P, HALF),
        "ada_rest_b": b[2:].reshape(8, HALF),
        "w_units": w_units,
        "w_gates": w_gates,
        "b_if": np.asarray(ml_b_if)[0].reshape(2 * NH, 1),
        "norm_w": np.asarray(ml_norm_w)[0].reshape(NH, DV),
        "final_w": np.asarray(final_norm_w).reshape(1, D),
    }
    arrays = {n: np.ascontiguousarray(a) for n, a in arrays.items()}
    nc = bacc.Bacc("TRN2", target_bir_lowering=False, num_devices=1)
    args = [nc.dram_tensor(n, a.shape, mybir.dt.from_np(a.dtype), kind="ExternalInput").ap()
            for n, a in arrays.items()]
    args.append(nc.dram_tensor("out", (NT, P, D), F32, kind="ExternalOutput").ap())
    args.append(nc.dram_tensor("scan_rows", (2, NH, S), F32, kind="Internal").ap())
    args.append(nc.dram_tensor("mod_rows", (8, HALF), F32, kind="Internal").ap())
    build(nc, *args)
    got = run_bass_kernel_spmd(nc, [arrays], core_ids=[0])
    return got.results[0]["out"].reshape(1, S, D)
```
